# Optimizing a Trainium2 kernel written in Bass

```python
import math
import jax, jax.numpy as jnp
from jax import lax
import numpy as np

D_MODEL = 1024
BATCH = 1
SEQ = 512
DEPTH = 1
DEC_BATCH = 8
DEC_SEQ = 4
PAST_LEN = 4096
PAGE_SIZE = 128

N_HEADS = 4
DK = D_MODEL // N_HEADS
DV = D_MODEL // N_HEADS
CONV_CH = D_MODEL
CONV_K = 31
D_FF = ((8 * D_MODEL // 3 + 127) // 128) * 128
FFN_K = 3
CHUNK = 128
EPS = 1e-6
IN_SIZES = (N_HEADS * DK, N_HEADS * DK, N_HEADS * DV, N_HEADS * DV,
            N_HEADS, N_HEADS,
            CONV_CH, CONV_CH,
            D_MODEL, D_MODEL)
IN_SPLITS = tuple(int(s) for s in np.cumsum(IN_SIZES)[:-1])
N_IN = int(sum(IN_SIZES))

kernel_name = "mlstm_conformer_gated_hybrid_step"

def rmsnorm(x, g):
    xf = x.astype(jnp.float32)
    y = xf * lax.rsqrt(jnp.mean(xf * xf, axis=-1, keepdims=True) + EPS)
    return (y * g.astype(jnp.float32)).astype(x.dtype)

def layernorm(x, g, b):
    xf = x.astype(jnp.float32)
    mu = jnp.mean(xf, axis=-1, keepdims=True)
    xc = xf - mu
    y = xc * lax.rsqrt(jnp.mean(xc * xc, axis=-1, keepdims=True) + EPS)
    return (y * g.astype(jnp.float32) + b.astype(jnp.float32)).astype(x.dtype)

def causal_dwconv(u, buf, w, b):
    full = jnp.concatenate([buf.astype(u.dtype), u], axis=1)
    y = lax.conv_general_dilated(full, w[:, None, :].astype(u.dtype), (1,), 'VALID',
                                 dimension_numbers=('NWC', 'WIO', 'NWC'),
                                 feature_group_count=u.shape[-1])
    return y + b.astype(u.dtype), full[:, full.shape[1] - (w.shape[0] - 1):]

def mlstm_chunk(carry, inp):
    C, n, m = carry
    q, k, v, ig, lf = inp
    L = q.shape[2]
    b = jnp.cumsum(lf, axis=-1)
    inter = b + m[..., None]
    D = b[..., :, None] - b[..., None, :] + ig[..., None, :]
    causal = jnp.tril(jnp.ones((L, L), dtype=bool))
    D = jnp.where(causal, D, -jnp.inf)
    m_t = jnp.maximum(inter, jnp.max(D, axis=-1))
    w_inter = jnp.exp(inter - m_t)
    s = jnp.einsum('bhtk,bhsk->bhts', q, k) * jnp.exp(D - m_t[..., None])
    num = w_inter[..., None] * jnp.einsum('bhvk,bhtk->bhtv', C, q) + jnp.einsum('bhts,bhsv->bhtv', s, v)
    den = w_inter * jnp.einsum('bhk,bhtk->bht', n, q) + jnp.sum(s, axis=-1)
    h = num / jnp.maximum(jnp.abs(den), jnp.exp(-m_t))[..., None]
    m_new = m_t[..., -1]
    g_inter = jnp.exp(b[..., -1] + m - m_new)
    g_s = jnp.exp(b[..., -1:] - b + ig - m_new[..., None])
    C_new = g_inter[..., None, None] * C + jnp.einsum('bhs,bhsv,bhsk->bhvk', g_s, v, k)
    n_new = g_inter[..., None] * n + jnp.einsum('bhs,bhsk->bhk', g_s, k)
    return (C_new, n_new, m_new), h

def mlstm(q, k, v, ig, lf, C, n, m):
    B, H, T, _ = q.shape
    L = math.gcd(T, CHUNK)
    nc = T // L

    def split(a):
        return jnp.moveaxis(a.reshape(a.shape[:2] + (nc, L) + a.shape[3:]), 2, 0)

    (C, n, m), h = lax.scan(mlstm_chunk, (C, n, m), tuple(split(a) for a in (q, k, v, ig, lf)))
    h = jnp.moveaxis(h, 0, 2).reshape(B, H, T, -1)
    return h, C, n, m

def layer(x, C, n, m, conv_buf, ffn_buf, mix_g, w_in, b_if, head_g, w_mo, conv_w, conv_b,
          cln_g, cln_b, w_co, w_out, ffn_g, w_up, fconv_w, fconv_b, w_down):
    B, T, _ = x.shape
    f32 = jnp.float32
    hn = rmsnorm(x, mix_g)
    z = hn @ w_in
    q, k, v, o, ig, fg, glu_v, glu_g, g_a, g_b = jnp.split(z, IN_SPLITS, axis=-1)

    def heads(a, d):
        return a.reshape(B, T, N_HEADS, d).transpose(0, 2, 1, 3).astype(f32)

    ig_t = (ig.astype(f32) + b_if[:N_HEADS].astype(f32)).transpose(0, 2, 1)
    lf_t = jax.nn.log_sigmoid(fg.astype(f32) + b_if[N_HEADS:].astype(f32)).transpose(0, 2, 1)
    hA, C_new, n_new, m_new = mlstm(heads(q, DK), heads(k, DK) * (DK ** -0.5), heads(v, DV),
                                     ig_t, lf_t, C.astype(f32), n.astype(f32), m.astype(f32))
    hA = hA.transpose(0, 2, 1, 3)
    mu = jnp.mean(hA, axis=-1, keepdims=True)
    hc = hA - mu
    hA = (hc * lax.rsqrt(jnp.mean(hc * hc, axis=-1, keepdims=True) + EPS)).reshape(B, T, N_HEADS * DV)
    hA = (hA * head_g.astype(f32) * jax.nn.sigmoid(o.astype(f32))).astype(x.dtype)
    yA = hA @ w_mo

    u = glu_v * jax.nn.sigmoid(glu_g)
    uc, conv_buf_new = causal_dwconv(u, conv_buf, conv_w, conv_b)
    uc = jax.nn.silu(layernorm(uc, cln_g, cln_b))
    yB = uc @ w_co

    mix = jax.nn.sigmoid(g_a) * yA + jax.nn.sigmoid(g_b) * yB
    x = x + mix @ w_out

    hf = rmsnorm(x, ffn_g)
    up = hf @ w_up
    upc, ffn_buf_new = causal_dwconv(up, ffn_buf, fconv_w, fconv_b)
    a, gt = jnp.split(upc, 2, axis=-1)
    x = x + (jax.nn.silu(a) * gt) @ w_down
    dt = x.dtype
    return x, C_new.astype(dt), n_new.astype(dt), m_new.astype(dt), conv_buf_new, ffn_buf_new

def setup_inputs(seed: int = 0) -> dict:
    key = jax.random.key(seed)
    ks = iter(jax.random.split(key, 40))
    f32 = jnp.float32

    def nrm(shape, scale):
        return jax.random.normal(next(ks), shape, f32) * scale

    def uni(shape, lo, hi):
        return jax.random.uniform(next(ks), shape, f32, lo, hi)

    H = N_HEADS
    b_if = jnp.concatenate([nrm((DEPTH, H), 0.1), uni((DEPTH, H), 3.0, 6.0)], axis=-1)
    return {
        "x_prompt": nrm((BATCH, SEQ, D_MODEL), 1.0),
        "x_sample": nrm((DEC_BATCH, DEC_SEQ, D_MODEL), 1.0),
        "state_C": nrm((DEPTH, DEC_BATCH, H, DV, DK), 0.1),
        "state_n": nrm((DEPTH, DEC_BATCH, H, DK), 0.1),
        "state_m": uni((DEPTH, DEC_BATCH, H), 0.0, 4.0),
        "state_conv": nrm((DEPTH, DEC_BATCH, CONV_K - 1, CONV_CH), 0.5),
        "state_ffn": nrm((DEPTH, DEC_BATCH, FFN_K - 1, 2 * D_FF), 0.5),
        "mix_norm_g": 1.0 + nrm((DEPTH, D_MODEL), 0.05),
        "w_in": nrm((DEPTH, D_MODEL, N_IN), D_MODEL ** -0.5),
        "b_if": b_if,
        "head_norm_g": 1.0 + nrm((DEPTH, H * DV), 0.05),
        "w_mlstm_out": nrm((DEPTH, H * DV, D_MODEL), (H * DV) ** -0.5),
        "conv_w": nrm((DEPTH, CONV_K, CONV_CH), CONV_K ** -0.5),
        "conv_b": nrm((DEPTH, CONV_CH), 0.02),
        "conv_ln_g": 1.0 + nrm((DEPTH, CONV_CH), 0.05),
        "conv_ln_b": nrm((DEPTH, CONV_CH), 0.02),
        "w_conv_out": nrm((DEPTH, CONV_CH, D_MODEL), CONV_CH ** -0.5),
        "w_out": nrm((DEPTH, D_MODEL, D_MODEL), D_MODEL ** -0.5),
        "ffn_norm_g": 1.0 + nrm((DEPTH, D_MODEL), 0.05),
        "w_up": nrm((DEPTH, D_MODEL, 2 * D_FF), D_MODEL ** -0.5),
        "ffn_conv_w": nrm((DEPTH, FFN_K, 2 * D_FF), FFN_K ** -0.5),
        "ffn_conv_b": nrm((DEPTH, 2 * D_FF), 0.02),
        "w_down": nrm((DEPTH, D_FF, D_MODEL), D_FF ** -0.5),
        "final_norm_g": 1.0 + nrm((D_MODEL,), 0.05),
    }

def reference(x_prompt, x_sample, state_C, state_n, state_m, state_conv, state_ffn,
              mix_norm_g, w_in, b_if, head_norm_g, w_mlstm_out, conv_w, conv_b, conv_ln_g,
              conv_ln_b, w_conv_out, w_out, ffn_norm_g, w_up, ffn_conv_w, ffn_conv_b, w_down,
              final_norm_g):
    f32 = jnp.float32
    B = x_prompt.shape[0]
    xp, xs = x_prompt, x_sample
    Cp_l, np_l, mp_l, cp_l, fp_l = [], [], [], [], []
    Cs_l, ns_l, ms_l, cs_l, fs_l = [], [], [], [], []
    for l in range(DEPTH):
        w = (mix_norm_g[l], w_in[l], b_if[l], head_norm_g[l], w_mlstm_out[l], conv_w[l], conv_b[l],
             conv_ln_g[l], conv_ln_b[l], w_conv_out[l], w_out[l], ffn_norm_g[l], w_up[l],
             ffn_conv_w[l], ffn_conv_b[l], w_down[l])
        xp, Cp, n_p, mp, cp, fp = layer(
            xp,
            jnp.zeros((B, N_HEADS, DV, DK), f32), jnp.zeros((B, N_HEADS, DK), f32),
            jnp.zeros((B, N_HEADS), f32),
            jnp.zeros((B, CONV_K - 1, CONV_CH), xp.dtype),
            jnp.zeros((B, FFN_K - 1, 2 * D_FF), xp.dtype), *w)
        xs, Cs, n_s, ms, cs, fs = layer(xs, state_C[l], state_n[l], state_m[l], state_conv[l],
                                        state_ffn[l], *w)
        Cp_l.append(Cp); np_l.append(n_p); mp_l.append(mp); cp_l.append(cp); fp_l.append(fp)
        Cs_l.append(Cs); ns_l.append(n_s); ms_l.append(ms); cs_l.append(cs); fs_l.append(fs)
    y_prompt = rmsnorm(xp, final_norm_g)
    y_sample = rmsnorm(xs, final_norm_g)
    return (y_prompt, y_sample,
            jnp.stack(Cp_l), jnp.stack(np_l), jnp.stack(mp_l), jnp.stack(cp_l), jnp.stack(fp_l),
            jnp.stack(Cs_l), jnp.stack(ns_l), jnp.stack(ms_l), jnp.stack(cs_l), jnp.stack(fs_l))


_drawn_inputs = setup_inputs


def setup_inputs(seed=0):
    import zlib

    import numpy as np

    out = dict(_drawn_inputs(seed))
    spreads = {}
    factors = {'head_norm_g': 3.737,
     'conv_b': 4.143,
     'conv_ln_g': 2.846,
     'conv_ln_b': 8.0,
     'ffn_conv_b': 4.203}
    for name, (base, spread) in spreads.items():
        noise = np.random.default_rng([zlib.crc32(name.encode()), seed]).standard_normal(out[name].shape)
        drawn = base * np.exp(spread * noise) if base else spread * noise
        out[name] = __import__('jax').numpy.asarray(drawn.astype(out[name].dtype))
    for name, factor in factors.items():
        out[name] = (out[name] * factor).astype(out[name].dtype)
    return out
```

```python
from contextlib import ExitStack

import concourse.bass as bass
from concourse import mybir

F32 = mybir.dt.float32
F32R = mybir.dt.float32r
ALU = mybir.AluOpType
ACT = mybir.ActivationFunctionType

P = 128
D = 1024
KT = D // P
TP = 512
NB, NS = 8, 4
TS = NB * NS
T = TP + TS
HALVES = ((0, 256), (256, T))
NH, DH = 4, 256
NI = TP // P
CK = 31
CH = CK - 1
SEG = CH + NS
DFF = 2816
KF = DFF // P
FK = 3
FSEG = FK - 1 + NS
UPW = CH + TP + NB * SEG
FPW = FK - 1 + TP + NB * FSEG + 4
FOUT = TP + NB * FSEG
EPS = 1e-6
NRAW = 3
RING = 3
COLS = 256


class Count:

    def __init__(self, sem):
        self.sem, self.n = sem, 0

    def raised_by(self, ins):
        ins.then_inc(self.sem, 1)
        self.n += 1


def plan():
    steps = [("setup", 0), ("panel", "if", 0), ("gates", 0)]
    for j in range(KT):
        steps.append(("panel", "glu", j))
        if j:
            steps.append(("tail", j - 1))
    steps.append(("panel", "k", 0))
    steps.append(("tail", KT - 1))
    for h in range(NH):
        if h:
            steps += [("panel", "k", h), ("av", h - 1)]
        steps.append(("panel", "v", h))
        if h:
            steps.append(("headout", h - 1))
        steps += [("kv", h), ("panel", "q", h), ("panel", "o", h), ("scores", h)]
    steps += [("panel", "gate", 0), ("av", NH - 1), ("panel", "gate", 1), ("headout", NH - 1), ("convnorm", 0)]
    for i in range(KT):
        steps.append(("panel", "branch", i))
        if i + 2 < KT:
            steps.append(("panel", "gate", i + 2))
    steps.append(("residual", 0))
    for i in range(4):
        steps.append(("panel", "out", i))
    steps.append(("norm2", 0))
    for i in range(KF):
        steps += [("fstate", i), ("panel", "up", i), ("ftail", i)]
    for g in range(4):
        steps += [("panel", "down", (g, s)) for s in range(3)]
    steps.append(("final", 0))
    return steps


def build(nc, x_prompt, x_sample, state_C, state_n, state_m, state_conv, state_ffn, mix_norm_g,
          w_in, b_if, head_norm_g, w_mlstm_out, conv_w, conv_b, conv_ln_g, conv_ln_b, w_conv_out,
          w_out, ffn_norm_g, w_up, ffn_conv_w, ffn_conv_b, w_down, final_norm_g,
          y_prompt, y_sample, C_prompt, n_prompt, m_prompt, conv_prompt, ffn_prompt,
          C_sample, n_sample, m_sample, conv_sample, ffn_sample):
    ctx = ExitStack()
    steps = plan()

    at = [16512]

    def sb(name, shape, dt=F32, offset=None):
        size = 4
        for n in shape[1:]:
            size *= n
        if offset is None:
            offset = at[0]
            at[0] += (size + 31) // 32 * 32
        assert offset + size <= nc.sbuf_usable_end, (name, offset + size)
        return nc.alloc_sbuf_tensor_at(name, shape, dt, offset=offset)

    def after(offset, *shape):
        size = 4
        for n in shape:
            size *= n
        return offset + (size + 31) // 32 * 32

    raw = sb("raw", [P, NRAW, KT * COLS])
    whi = sb("whi", [P, 2, KT * COLS], F32R)
    wlo = sb("wlo", [P, 2, KT * COLS], F32R)
    ahi = sb("ahi", [P, KT, T], F32R)
    alo = sb("alo", [P, KT, T], F32R)
    ident = sb("ident", [P, P])
    ones = sb("ones", [P, P])
    vec = sb("vec", [P, 92])
    fcw = sb("fcw", [P, FK, KF * 2])
    cw = sb("cw", [P, KT, CK])
    stat = sb("stat", [P, 40])
    epsc = sb("epsc", [P, 2])
    sel_at = at[0]
    sel = sb("sel", [NH, NH, P])
    bmask = sb("bmask", [TS, NB])
    rows = sb("rows", [P, T])
    mrow = sb("mrow", [NH, T + TS + NB])
    rt = sb("rt", [P, NI + 1, P])
    em = sb("em", [P, NI + 1, NH])
    gib = sb("gib", [NB, NH])
    mb = sb("mb", [P, T + TS + NB])
    fsm_end = at[0]

    MIXG, HEADG, CB, CLG, CLB, FG, FB = 0, 8, 16, 24, 32, 40, 48

    arena = at[0]
    upad = sb("upad", [P, KT, UPW])
    ulo = sb("ulo", [P, KT, UPW], F32R, offset=arena)
    hab_at = at[0]
    hab = sb("hab", [P, KT, T])
    hlo = sb("hlo", [P, KT, T], F32R, offset=hab_at)
    x1 = sb("x1", [P, KT, T], offset=hab_at)
    work = at[0]
    kT = sb("kT", [P, 2, T])
    vqT = sb("vqT", [P, 2, T])
    gk = sb("gk", [P, NI + 1, DH])
    vk = sb("vk", [P, NI + 1, DH + 1])
    sT = sb("sT", [P, NI, TP])
    sTs = sb("sTs", [TS, TS])
    ht = sb("ht", [P, NI + 1, DH + 1])
    cin = sb("cin", [P, 2, 2, DH])
    cT_at = at[0]
    cT = sb("cT", [P, 2, 2, DH + 1])
    cnew_at = at[0]
    cnew = sb("cnew", [P, 2, 2, DH])
    qm = sb("qm", [P, 2, 36 * NB])
    km = sb("km", [TS, 2, DH])
    nT = sb("nT", [P, 2, TS])
    nh = sb("nh", [NB, NH, DH])
    nout = sb("nout", [NB, 2, DH])
    cout = sb("cout", [P, 2, DH])
    cacc = sb("cacc", [P, T])
    prod_at = at[0]
    prod = sb("prod", [P, NB, 2, CK])
    sg = sb("sg", [P, T], offset=cnew_at)
    cstage = sb("cstage", [TS, 2, 2 * P], offset=cT_at)
    unew = sb("unew", [P, 2, TS], offset=cnew_at + 4 * T)
    xin = sb("xin", [P, NI + 1, D], offset=work)
    s1 = after(work, NI + 1, D)
    cst = sb("cst", [NB // 2 * CH, 2, D], offset=s1)
    s2 = after(s1, 2, D)
    vrow = sb("vrow", [P, 3, P], offset=s2)
    cwrow = sb("cwrow", [CK, D], offset=after(s2, 3, P))
    gates = sb("gates", [P, 6, T], offset=after(after(s2, 3, P), D))
    nin = sb("nin", [TS, DH], offset=after(after(after(s2, 3, P), D), 6, T))
    assert after(after(after(after(s2, 3, P), D), 6, T), DH) <= prod_at
    sga = sb("sga", [P, 2, 2, T], offset=work)
    b1 = after(work, 4, T)
    uhi = sb("uhi", [P, KT, T], F32R, offset=b1)
    b2 = after(b1, KT, T)
    hhi = sb("hhi", [P, KT, T], F32R, offset=b2)
    b3 = after(b2, KT, T)
    mix = sb("mix", [P, KT, T], offset=b3)
    lnt = sb("lnt", [P, 6, T], offset=b3)
    xin2 = sb("xin2", [P, NI + 1, D], offset=arena)
    sq2 = sb("sq2", [P, 4, T], offset=work)
    f0 = arena
    hact = sb("hact", [P, 17, T], offset=work)
    hact2 = sb("hact2", [P, KF - 17, T], offset=f0)
    f1 = after(f0, KF - 17, T)
    dhi = sb("dhi", [P, 3, T], F32R, offset=f1)
    dlo_at = after(f1, 3, T)
    f3 = sel_at
    fst = sb("fst", [NB * 2, 2, 2 * P], offset=after(work, 17, T))
    f4 = after(after(work, 17, T), 2, 2 * P)
    fout = sb("fout", [NB * 2 + 2, 2, 2 * P], offset=f4)
    f5 = after(f4, 2, 2 * P)
    up = sb("up", [P, 2, FPW], offset=f5)
    f6 = after(f5, 2, FPW)
    upc = sb("upc", [P, 2, FOUT], offset=f6)
    f7 = after(f6, 2, FOUT)
    usig = sb("usig", [P, FOUT], offset=f7)
    flast = sb("flast", [P, 2, 18], offset=after(f7, FOUT))
    dlo = sb("dlo", [P, 3, T], F32R, offset=dlo_at)
    assert after(dlo_at, 3, T) <= hab_at
    x2 = sb("x2", [P, KT, T], offset=hab_at)
    yt = sb("yt", [P, NI + 1, D], offset=work)
    fgb = sb("fgb", [P, D], offset=after(work, NI + 1, D))
    junk = sb("junk", [P, TP], offset=after(after(work, NI + 1, D), D))

    with ctx:
        acc = ctx.enter_context(nc.psum_tensor("acc", [P, 2, 2, 512], F32))
        small = ctx.enter_context(nc.psum_tensor("small", [P, RING, 512], F32))
        held = ctx.enter_context(nc.psum_tensor("held", [P, 512], F32))

        def sem(name):
            return ctx.enter_context(nc.semaphore(name))

        raw_in = [sem(f"raw_in{i}") for i in range(NRAW)]
        raw_zeroed = sem("raw_zeroed")
        w_hi, w_lo = sem("w_hi"), sem("w_lo")
        down_part = sem("down_part")
        acc_done = sem("acc_done")
        acc_out = [sem("acc_out0"), sem("acc_out1")]
        small_done = sem("small_done")
        small_out = [sem(f"small_out{i}") for i in range(RING)]
        held_done, held_out = sem("held_done"), sem("held_out")
        x_in = [sem(f"x_in{i}") for i in range(NI + 1)]
        consts_in = [sem(f"consts_in{i}") for i in range(22)]
        consts_set = sem("consts_set")
        rs_ready, xs_ready, xn_hi = sem("rs_ready"), sem("xs_ready"), sem("xn_hi")
        ssq_ready = sem("ssq_ready")
        gates_act, gates_dve, rows_ready, rt_ready, m_ready = (sem(x) for x in ("gates_act", "gates_dve", "rows_ready", "rt_ready", "m_ready"))
        em_ready = sem("em_ready")
        cstage_out = [sem("cstage_out0"), sem("cstage_out1")]
        uc_ready = sem("uc_ready")
        unew_ready, flast_ready = sem("unew_ready"), sem("flast_ready")
        exp_ready, st_ready, st_masked, qm_ready = sem("exp_ready"), sem("st_ready"), sem("st_masked"), sem("qm_ready")
        cin_in = [sem("cin_in0"), sem("cin_in1")]
        cnew_out = [sem("cnew_out0"), sem("cnew_out1")]
        nT_ready = sem("nT_ready")
        ncol_ready = sem("ncol_ready")
        km_ready = sem("km_ready")
        ht_in, hv_ready, hr_ready, hn_ready = sem("ht_in"), sem("hv_ready"), sem("hr_ready"), sem("hn_ready")
        cout_ready, cout_out = sem("cout_ready"), sem("cout_out")
        nout_out = sem("nout_out")
        hhi_ready, hlo_ready = sem("hhi_ready"), sem("hlo_ready")
        xc_ready, sqc_ready, lnstd, yln, ysig, zs, uhi_ready, ulo_ready = (
            sem(x) for x in ("xc_ready", "sqc_ready", "lnstd", "yln", "ysig", "zs", "uhi_ready", "ulo_ready"))
        mix_ready, mhi_ready, mlo_ready = sem("mix_ready"), sem("mhi_ready"), sem("mlo_ready")
        x1_in = sem("x1_in")
        x1_ready, sq_ready, std2, hf_ready, hfhi, hflo = (sem(x) for x in ("x1_ready", "sq_ready", "std2", "hf_ready", "hfhi", "hflo"))
        xin2_in = [sem(f"xin2_in{i}") for i in range(NI + 1)]
        fst_in = [sem("fst_in0"), sem("fst_in1")]
        fout_out = [sem("fout_out0"), sem("fout_out1")]
        sig_ready, act_ready, dhi_ready, dlo_ready = sem("sig_ready"), sem("act_ready"), sem("dhi_ready"), sem("dlo_ready")
        ffn_used = sem("ffn_used")
        down_kt = sem("down_kt")
        fg_in = sem("fg_in")
        yssq, yrs, y_ready, y_out = sem("yssq"), sem("yrs"), sem("y_ready"), sem("y_out")
        rowcopy_out, m_out = sem("rowcopy_out"), sem("m_out")
        act_chain, dve_chain, pool_chain = sem("act_chain"), sem("dve_chain"), sem("pool_chain")

        panels = [s[1:] for s in steps if s[0] == "panel"]
        index_of = {p: n for n, p in enumerate(panels)}

        def block_count(p):
            if p[0] == "if":
                return 1
            return 2 if p[0] != "down" or p[1][1] == 2 else 0

        first_block, raw_value, n_blocks = [], [], 0
        raw_total = [0] * NRAW
        sources = []
        OQ = 0
        OK_, OV, OO = D, 2 * D, 3 * D
        OI = 4 * D
        OGV = OI + 2 * NH
        OGG, OGA, OGB = OGV + D, OGV + 2 * D, OGV + 3 * D
        for n, (kind, i) in enumerate(panels):
            first_block.append(n_blocks)
            n_blocks += block_count((kind, i))
            if kind == "if":
                src = [(w_in, 0, KT, OI, NH, 0), (w_in, 0, KT, OI + NH, NH, 32)]
            elif kind == "glu":
                src = [(w_in, 0, KT, OGV + P * i, P, 0), (w_in, 0, KT, OGG + P * i, P, P)]
            elif kind in "kvqo":
                base = {"q": OQ, "k": OK_, "v": OV, "o": OO}[kind]
                src = [(w_in, 0, KT, base + COLS * i, COLS, 0)]
            elif kind == "gate":
                src = [(w_in, 0, KT, OGA + P * i, P, 0), (w_in, 0, KT, OGB + P * i, P, P)]
            elif kind == "branch":
                src = [(w_mlstm_out, 0, KT, P * i, P, 0), (w_conv_out, 0, KT, P * i, P, P)]
            elif kind == "out":
                src = [(w_out, 0, KT, COLS * i, COLS, 0)]
            elif kind == "up":
                src = [(w_up, 0, KT, P * i, P, 0), (w_up, 0, KT, DFF + P * i, P, P)]
            else:
                g, s = i
                src = [(w_down, s * 8, min(8, KF - 8 * s), COLS * g, COLS, 0)]
            sources.append(src)
            raw_total[n % NRAW] += 16 * len(src)
            raw_value.append(raw_total[n % NRAW])

        def width(n):
            return P if panels[n][0] == "if" else COLS

        def ktiles(n):
            return sources[n][0][2]

        def panel_view(tile, slot, n):
            return tile[:, slot, 0:ktiles(n) * width(n)].rearrange("p (k c) -> p k c", c=width(n))

        def wait_panel_used(eng, n):
            kind, i = panels[n]
            if kind == "down" and i[1] < 2:
                eng.wait_ge(down_part, 2 * i[0] + i[1] + 1)
            else:
                eng.wait_ge(acc_done, first_block[n] + block_count(panels[n]))

        def acc_ready(eng, n, c):
            b = first_block[n] + c
            eng.wait_ge(acc_done, b + 1)
            return acc[:, b % 2, :, 0:256], acc[:, b % 2, 1, 256:256 + TS], acc_out[b % 2]

        def wait_acc_out(eng, n, c):
            b = first_block[n] + c
            eng.wait_ge(acc_out[b % 2], b // 2 + 1)

        ring_of = {}

        def small_at(name):
            return small[:, ring_of[name] % RING, :]

        def take(eng, name):
            eng.wait_ge(small_done, ring_of[name] + 1)
            return small_at(name)

        def out_sem(name):
            return small_out[ring_of[name] % RING]

        def wait_taken(eng, name):
            k = ring_of[name]
            eng.wait_ge(small_out[k % RING], k // RING + 1)

        def act_tile(k):
            return hact[:, k, :] if k < 17 else hact2[:, k - 17, :]

        def wait_down(eng, u):
            g, k = u // KF, u % KF
            if k in (7, 15):
                eng.wait_ge(down_part, 2 * g + (k + 1) // 8)
            elif k == KF - 1:
                eng.wait_ge(acc_done, first_block[index_of[("down", (g, 2))]] + 2)
            else:
                eng.wait_ge(ffn_used, (KF - 3) * g + k + 1 - (k > 7) - (k > 15))

        block = ctx.enter_context(nc.Block())

        @block.tensor
        def _(pe):
            held_n = [0]

            def begin(name):
                k = len(ring_of)
                ring_of[name] = k
                if k >= RING:
                    pe.wait_ge(small_out[k % RING], k // RING)
                return small[:, k % RING, :]

            def end(ins):
                ins.then_inc(small_done, 1)

            def turn(out, src, n):
                return pe.transpose(out, src, ident[0:n, 0:n])

            def setup():
                pe.wait_ge(consts_set, 1)
                for i, w in enumerate((92, 88, 44)):
                    pe.wait_ge(consts_in[i], 16)
                    if i == 0:
                        for q in range(8, 14):
                            pe.wait_ge(consts_in[q], 16)
                    if i == 1:
                        pe.wait_ge(consts_in[15], 16)
                    o = begin(("vec", i))
                    end(turn(o[:, 0:w], vrow[0:w, i, :], w))
                pe.wait_ge(consts_in[3], 16)
                o = begin("cw")
                for j in range(KT):
                    t = turn(o[:, CK * j:CK * j + CK], cwrow[:, P * j:P * j + P], CK)
                end(t)
                for s in range(2):
                    pe.wait_ge(consts_in[4 + s], 16)
                    for q in range(2):
                        o = begin(("cst", s, q))
                        for j in range(4):
                            t = turn(o[:, 120 * j:120 * j + 120], cst[:, s, P * (4 * q + j):P * (4 * q + j) + P], 120)
                        end(t)
                pe.wait_ge(consts_in[6], 16)
                o = begin("nT")
                for c in range(2):
                    t = turn(o[:, TS * c:TS * c + TS], nin[:, P * c:P * c + P], TS)
                end(t)
                for k in range(KT):
                    o = begin(("xT", k))
                    if k == 0:
                        pe.wait_ge(xs_ready, NI + 1)
                    for i in range(NI):
                        t = turn(o[:, P * i:P * i + P], xin[:, i, P * k:P * k + P], P)
                    end(t)
                o = begin("xTs")
                for k in range(KT):
                    t = turn(o[:, TS * k:TS * k + TS], xin[0:TS, NI, P * k:P * k + P], TS)
                end(t)

            def gates_step():
                pe.wait_ge(rows_ready, 1)
                o = begin("rt")
                for i in range(NI):
                    t = turn(o[:, P * i:P * i + P], rows[:, P * i:P * i + P], P)
                end(t)
                o = begin("rts")
                turn(o[0:TS, 0:P], rows[:, TP:T], P)
                end(turn(o[0:NB, P:P + NH], mrow[:, T + TS:T + TS + NB], NH))

            def tail(j):
                wait_acc_out(pe, index_of[("glu", j)], 0)
                o = begin(("ut", j))
                turn(o[0:CH, 0:P], upad[:, j, CH + TP - CH:CH + TP], P)
                pe.wait_ge(unew_ready, j + 1)
                end(turn(o[0:TS, P:2 * P], unew[:, j % 2, :], P))

            def kv(h):
                wait_acc_out(pe, index_of[("k", h)], 1)
                for what, src in (("kt", kT), ("vt", vqT)):
                    if what == "vt":
                        wait_acc_out(pe, index_of[("v", h)], 1)
                        wait_acc_out(pe, index_of[("v", h)], 0)
                    else:
                        wait_acc_out(pe, index_of[("k", h)], 0)
                    for q in range(3):
                        o = begin((what, h, q))
                        for i in ((0, 1), (2, 3), (4,))[q]:
                            n = P if i < NI else TS
                            for c in range(2):
                                at_ = 256 * (i % 2) + P * c
                                t = turn(o[0:n, at_:at_ + P], src[:, c, P * i:P * i + n], P)
                        end(t)

            def scores(h):
                o = begin(("mb", h))
                end(pe.matmul(o, sel[:, h, :], mrow[:, 0:TP], start=True, stop=True))
                o = begin(("mbs", h))
                end(pe.matmul(o[:, 0:2 * TS + NB], sel[:, h, :], mrow[:, TP:], start=True, stop=True))
                wait_acc_out(pe, index_of[("q", h)], 0)
                wait_acc_out(pe, index_of[("q", h)], 1)
                for j in range(NI):
                    o = begin(("s", h, j))
                    for c in range(2):
                        t = pe.matmul(o[:, P * j:TP], kT[:, c, P * j:P * j + P], vqT[:, c, P * j:TP],
                                      start=(c == 0), stop=(c == 1))
                    end(t)
                o = begin(("ss", h))
                for c in range(2):
                    t = pe.matmul(o[0:TS, 0:TS], kT[:, c, TP:T], vqT[:, c, TP:T], start=(c == 0), stop=(c == 1))
                end(t)

            def av(h):
                pe.wait_ge(consts_set, 3)
                wait_taken(pe, ("vt", h, 0))
                wait_taken(pe, ("vt", h, 1))
                wait_taken(pe, ("vt", h, 2))
                pe.wait_ge(st_masked, (NI + 2) * h + NI)
                for i in range(NI):
                    o = begin(("h", h, i))
                    for j in range(i + 1):
                        t = pe.matmul(o[:, 0:DH + 1], sT[:, j, P * i:P * i + P], vk[:, j, :],
                                      start=(j == 0), stop=(j == i))
                    end(t)
                o = begin(("C", h))
                for c in range(2):
                    for j in range(NI):
                        t = pe.matmul(o[:, DH * c:DH * c + DH], vk[:, j, P * c:P * c + P], gk[:, j, :],
                                      start=(j == 0), stop=(j == NI - 1))
                end(t)
                o = begin(("n", h))
                for j in range(NI):
                    pe.matmul(o[0:1, 0:DH], vk[:, j, DH:DH + 1], gk[:, j, :], start=(j == 0), stop=(j == NI - 1))
                end(pe.matmul(o[0:NB, DH:2 * DH], bmask[:, :], gk[0:TS, NI, :], start=True, stop=True))
                if h:
                    pe.wait_ge(held_out, h)
                pe.wait_ge(st_masked, (NI + 2) * (h + 1))
                pe.matmul(held[0:TS, 0:DH + 1], sTs[:, :], vk[0:TS, NI, :], start=True, stop=False)
                pe.wait_ge(qm_ready, h + 1)

                def state_turn(b):
                    u = NB * h + b
                    pe.wait_ge(cin_in[u % 2], 16 * (u // 2 + 1))
                    o = begin(("ct", h, b))
                    for c in range(2):
                        for v in range(2):
                            t = turn(o[:, DH * c + P * v:DH * c + P * v + P], cin[:, u % 2, v, P * c:P * c + P], P)
                    end(t)

                state_turn(0)
                for b in range(NB):
                    u = NB * h + b
                    if b + 1 < NB:
                        state_turn(b + 1)
                    pe.wait_ge(km_ready, u + 1)
                    o = begin(("u", h, b))
                    for c in range(2):
                        t = pe.matmul(o[:, DH * c:DH * c + DH], vk[0:TS, NI, P * c:P * c + P], km[:, u % 2, :],
                                      start=True, stop=True)
                    end(t)
                    wait_taken(pe, ("ct", h, b))
                    pe.wait_ge(ncol_ready, u + 1)
                    for c in range(2):
                        t = pe.matmul(held[0:TS, 0:DH + 1], qm[:, c, TS * b:TS * b + TS], cT[:, u % 2, c, :],
                                      start=False, stop=(b == NB - 1 and c == 1))
                    if b < NB - 1:
                        t.then_inc(down_kt, 1)
                    else:
                        t.then_inc(held_done, 1)

            def headout(h):
                pe.wait_ge(hn_ready, h + 1)
                for c in range(2):
                    o = begin(("hT", h, c))
                    for i in range(NI):
                        t = turn(o[:, P * i:P * i + P], ht[:, i, P * c:P * c + P], P)
                    end(t)
                o = begin(("hTs", h))
                for c in range(2):
                    t = turn(o[:, TS * c:TS * c + TS], ht[0:TS, NI, P * c:P * c + P], TS)
                end(t)

            def convnorm():
                oa, ob = begin("mua"), None
                ob = begin("mub")
                pe.wait_ge(uc_ready, KT)
                for o, (a, b) in ((oa, HALVES[0]), (ob, HALVES[1])):
                    for j in range(KT):
                        t = pe.matmul(o[:, 0:b - a], ones[:, :], upad[:, j, CH + a:CH + b],
                                      start=(j == 0), stop=(j == KT - 1))
                    end(t)
                oa, ob = begin("vara"), begin("varb")
                for j in range(KT):
                    pe.wait_ge(sqc_ready, j + 1)
                    for o, (a, b) in ((oa, HALVES[0]), (ob, HALVES[1])):
                        t = pe.matmul(o[:, 0:b - a], ones[:, :], lnt[:, 2 + j % 4, a:b],
                                      start=(j == 0), stop=(j == KT - 1))
                        if j == KT - 1:
                            end(t)
                    if j < KT - 1:
                        t.then_inc(m_ready, 1)

            def residual():
                for k in range(KT):
                    o = begin(("xr", k))
                    if k == 0:
                        for i in range(NI + 1):
                            pe.wait_ge(xin2_in[i], 16)
                    for i in range(NI):
                        t = turn(o[:, P * i:P * i + P], xin2[:, i, P * k:P * k + P], P)
                    end(t)
                o = begin("xrs")
                for k in range(KT):
                    t = turn(o[:, TS * k:TS * k + TS], xin2[0:TS, NI, P * k:P * k + P], TS)
                end(t)

            def norm2():
                oa, ob = begin("qa"), begin("qb")
                for j in range(KT):
                    pe.wait_ge(sq_ready, j + 1)
                    for o, (a, b) in ((oa, HALVES[0]), (ob, HALVES[1])):
                        t = pe.matmul(o[:, 0:b - a], ones[:, :], sq2[:, j % 4, a:b],
                                      start=(j == 0), stop=(j == KT - 1))
                        if j == KT - 1:
                            end(t)
                    if j < KT - 1:
                        t.then_inc(x1_in, 1)

            def fstate(i):
                pe.wait_ge(fst_in[i % 2], 32 * (i // 2 + 1))
                o = begin(("fs", i))
                for c in range(2):
                    t = turn(o[:, 16 * c:16 * c + 16], fst[:, i % 2, P * c:P * c + P], 16)
                end(t)

            def ftail(i):
                pe.wait_ge(flast_ready, i + 1)
                o = begin(("ft", i))
                for c in range(2):
                    t = turn(o[0:18, P * c:P * c + P], flast[:, c, :], P)
                end(t)

            def final():
                for i in range(NI + 1):
                    n = P if i < NI else TS
                    for q in range(2):
                        o = begin(("y", i, q))
                        for j in range(4):
                            k = 4 * q + j
                            if i == 0:
                                wait_acc_out(pe, index_of[("down", (k // 2, 2))], k % 2)
                            t = turn(o[0:n, P * j:P * j + P], x2[:, k, P * i:P * i + n], P)
                        end(t)

            def panel(kind, i):
                n = index_of[(kind, i)]
                pe.wait_ge(w_hi, n + 1)
                pe.wait_ge(w_lo, n + 1)
                hi, lo = panel_view(whi, n % 2, n), panel_view(wlo, n % 2, n)
                if kind == "down":
                    g, s = i
                    kt0 = 8 * s
                    for k in range(ktiles(n)):
                        u = KF * g + kt0 + k
                        pe.wait_ge(dhi_ready, u + 1)
                        pe.wait_ge(dlo_ready, u + 1)
                        for c in range(2):
                            b = first_block[n] + c
                            if s == 0 and k == 0:
                                pe.wait_ge(acc_out[b % 2], b // 2)
                            for q, (w, x) in enumerate(((hi, dhi), (hi, dlo), (lo, dhi))):
                                for a, (t0, t1) in enumerate(HALVES):
                                    t = pe.matmul(acc[:, b % 2, a, 0:t1 - t0], w[:, k, P * c:P * c + P],
                                                  x[:, u % 3, t0:t1],
                                                  start=(s == 0 and k == 0 and q == 0),
                                                  stop=(s == 2 and k == ktiles(n) - 1 and q == 2))
                            if k == ktiles(n) - 1 and s == 2:
                                t.then_inc(acc_done, 1)
                        if not (k == ktiles(n) - 1):
                            t.then_inc(ffn_used, 1)
                    if s < 2:
                        t.then_inc(down_part, 1)
                    return
                for c in range(block_count((kind, i))):
                    xh, xl = ahi, alo
                    cut = 0
                    if kind == "if":
                        for k in range(KT):
                            wait_taken(pe, ("xT", k))
                        wait_taken(pe, "xTs")
                    if kind == "branch":
                        xh, xl = (hhi, hlo) if c == 0 else (uhi, ulo)
                        cut = 0 if c == 0 else CH
                        if i == 0:
                            if c == 0:
                                pe.wait_ge(hhi_ready, KT)
                                pe.wait_ge(hlo_ready, KT)
                            else:
                                pe.wait_ge(ulo_ready, KT)
                    b = first_block[n] + c
                    if b >= 2:
                        pe.wait_ge(acc_out[b % 2], b // 2)
                    for k in range(KT):
                        if kind == "out" and i == 0 and c == 0:
                            pe.wait_ge(mlo_ready, k + 1)
                        if kind == "up" and i == 0 and c == 0:
                            pe.wait_ge(hflo, k + 1)
                        for q, (w, x, off) in enumerate(((hi, xh, 0), (hi, xl, cut), (lo, xh, 0))):
                            for a, (t0, t1) in enumerate(HALVES):
                                t = pe.matmul(acc[:, b % 2, a, 0:t1 - t0], w[:, k, P * c:P * c + P],
                                              x[:, k, off + t0:off + t1],
                                              start=(k == 0 and q == 0), stop=(k == KT - 1 and q == 2))
                    t.then_inc(acc_done, 1)

            for s in steps:
                {"setup": lambda: setup(), "gates": lambda: gates_step(), "tail": lambda: tail(s[1]),
                 "kv": lambda: kv(s[1]), "scores": lambda: scores(s[1]), "av": lambda: av(s[1]),
                 "headout": lambda: headout(s[1]), "convnorm": lambda: convnorm(),
                 "residual": lambda: residual(), "norm2": lambda: norm2(), "fstate": lambda: fstate(s[1]),
                 "ftail": lambda: ftail(s[1]), "final": lambda: final(),
                 "panel": lambda: panel(*s[1:])}[s[0]]()

        @block.sync
        def _(sp):
            xp, xs = x_prompt[0], x_sample.rearrange("b t d -> (b t) d")
            for i in range(NI):
                sp.dma_start(xin[:, i, :], xp[P * i:P * i + P, :]).then_inc(x_in[i], 16)
            sp.dma_start(xin[0:TS, NI, :], xs).then_inc(x_in[NI], 16)

            def load(n):
                slot = n % NRAW
                if n == 0:
                    sp.wait_ge(raw_zeroed, 1)
                if n >= NRAW:
                    sp.wait_ge(w_hi, n - NRAW + 1)
                    sp.wait_ge(w_lo, n - NRAW + 1)
                view = panel_view(raw, slot, n)
                for mat, k0, kn, c0, cn, to in sources[n]:
                    src = mat[0, P * k0:P * (k0 + kn), c0:c0 + cn].rearrange("(k p) c -> p k c", p=P)
                    sp.dma_start(view[:, :, to:to + cn], src).then_inc(raw_in[slot], 16)

            for n in range(len(panels)):
                load(n)

        @block.scalar
        def _(act):
            chain = Count(act_chain)

            def link(ins):
                chain.raised_by(ins)
                act.wait_ge(act_chain, chain.n)

            def split_hi(n):
                act.wait_ge(raw_in[n % NRAW], raw_value[n])
                if n >= 2:
                    wait_panel_used(act, n - 2)
                act.activation(panel_view(whi, n % 2, n), panel_view(raw, n % NRAW, n), ACT.Copy).then_inc(w_hi, 1)

            def out_of(n, c, dst, func, scale=1.0, last=True):
                p, s, done = acc_ready(act, n, c)
                chain.raised_by(act.activation(dst[:, TP:T], s, func, scale=scale))
                act.activation(dst[:, 0:TP].rearrange("p (a t) -> p a t", a=2), p, func, scale=scale).then_inc(done, 1)

            def setup():
                for i in range(NI + 1):
                    n = P if i < NI else TS
                    act.wait_ge(x_in[i], 16)
                    if i == 0:
                        act.wait_ge(consts_set, 1)
                    link(act.activation(gates[0:n, 0:2, 0:512], xin[0:n, i, :].rearrange("p (a b) -> p a b", a=2), ACT.Square,
                                        accum_out=stat[0:n, i:i + 1]))
                act.activation(stat[:, 30:31], epsc[:, 0:1], ACT.Copy).then_inc(ssq_ready, 1)
                for n in range(2):
                    split_hi(n)
                act.wait_ge(rs_ready, 1)
                for i in range(NI + 1):
                    n = P if i < NI else TS
                    act.activation(xin[0:n, i, :], xin[0:n, i, :], ACT.Copy, scale=stat[0:n, 8 + i:9 + i]).then_inc(xs_ready, 1)
                for i, w in enumerate((92, 88, 44)):
                    o = take(act, ("vec", i))
                    dst = vec[:, 0:92] if i == 0 else (fcw[:, 0:2, :] if i == 1 else fcw[:, 2, :])
                    src = o[:, 0:w] if i != 1 else o[:, 0:w].rearrange("p (a b) -> p a b", a=2)
                    act.activation(dst, src, ACT.Copy).then_inc(out_sem(("vec", i)), 1)
                o = take(act, "cw")
                act.activation(cw[:, :, :], o[:, 0:KT * CK].rearrange("p (j k) -> p j k", j=KT), ACT.Copy).then_inc(out_sem("cw"), 1)
                for s in range(2):
                    for q in range(2):
                        o = take(act, ("cst", s, q))
                        for j in range(4):
                            dst = upad[:, 4 * q + j, CH + TP:UPW].rearrange("p (b s) -> p b s", s=SEG)[:, 4 * s:4 * s + 4, 0:CH]
                            t = act.activation(dst, o[:, 120 * j:120 * j + 120].rearrange("p (b s) -> p b s", s=CH), ACT.Copy)
                            if j < 3:
                                chain.raised_by(t)
                        t.then_inc(out_sem(("cst", s, q)), 1)
                o = take(act, "nT")
                act.activation(nT[:, :, :], o[:, 0:2 * TS].rearrange("p (c t) -> p c t", c=2), ACT.Copy).then_inc(out_sem("nT"), 1)
                wait_taken(act, ("vec", 0))
                for k in range(KT):
                    o = take(act, ("xT", k))
                    act.activation(ahi[:, k, 0:TP], o, ACT.Copy, scale=vec[:, MIXG + k:MIXG + k + 1]).then_inc(xn_hi, 1)
                o = take(act, "xTs")
                for k in range(KT):
                    act.activation(ahi[:, k, TP:T], o[:, TS * k:TS * k + TS], ACT.Copy,
                                   scale=vec[:, MIXG + k:MIXG + k + 1]).then_inc(xn_hi, 1)

            def gates_step():
                act.wait_ge(gates_dve, 1)
                link(act.activation(gates[32:36, 2, :], gates[32:36, 1, :], ACT.Exp))
                act.activation(gates[32:36, 3, :], gates[32:36, 2, :], ACT.Ln, bias=1.0).then_inc(gates_act, 1)
                act.wait_ge(gates_dve, 2)
                chain.raised_by(act.activation(rows[64:68, :], gates[0:4, 4, :], ACT.Exp))
                chain.raised_by(act.activation(mrow[:, T:T + TS + NB], gates[0:4, 5, 0:TS + NB], ACT.Exp))
                act.activation(rows[96:100, TP:T], gates[0:4, 5, 0:TS], ACT.Exp).then_inc(rows_ready, 1)
                o = take(act, "rt")
                act.activation(rt[:, 0:NI, :], o.rearrange("p (i c) -> p i c", i=NI), ACT.Copy).then_inc(out_sem("rt"), 1)
                o = take(act, "rts")
                act.activation(rt[0:TS, NI, :], o[0:TS, 0:P], ACT.Copy).then_inc(rt_ready, 1)
                act.activation(gib[:, :], o[0:NB, P:P + NH], ACT.Copy).then_inc(out_sem("rts"), 1)
                wait_taken(act, "rt")
                wait_taken(act, "rts")
                act.wait_ge(rt_ready, 1)
                act.activation(em[:, :, :], rt[:, :, 32:32 + NH], ACT.Exp, scale=-1.0).then_inc(em_ready, 1)

            def tail(j):
                o = take(act, ("ut", j))
                if j >= 2:
                    act.wait_ge(cstage_out[j % 2], 32 * (j // 2))
                chain.raised_by(act.activation(cstage[0:CH, j % 2, 0:P], o[0:CH, 0:P], ACT.Copy))
                act.activation(cstage[:, j % 2, P:2 * P], o[0:TS, P:2 * P], ACT.Copy).then_inc(out_sem(("ut", j)), 1)

            def kv(h):
                for q in range(3):
                    o = take(act, ("vt", h, q))
                    if q < 2:
                        act.activation(vk[:, 2 * q:2 * q + 2, 0:DH], o.rearrange("p (i c) -> p i c", i=2), ACT.Copy).then_inc(out_sem(("vt", h, q)), 1)
                    else:
                        act.activation(vk[0:TS, NI, 0:DH], o[0:TS, 0:DH], ACT.Copy).then_inc(out_sem(("vt", h, q)), 1)

            def scores(h):
                o = take(act, ("mb", h))
                act.activation(mb[:, 0:TP], o, ACT.Copy).then_inc(out_sem(("mb", h)), 1)
                o = take(act, ("mbs", h))
                act.activation(mb[:, TP:], o[:, 0:2 * TS + NB], ACT.Copy).then_inc(out_sem(("mbs", h)), 1)
                wait_taken(act, ("mb", h))
                wait_taken(act, ("mbs", h))
                if h:
                    act.wait_ge(held_done, h)
                for j in range(NI):
                    act.activation(sT[:, j, P * j:TP], mb[:, P * j:TP], ACT.Exp, bias=rt[:, j, h:h + 1], scale=-1.0).then_inc(exp_ready, 1)
                act.activation(sTs[:, :], mb[0:TS, TP:T], ACT.Exp, bias=rt[0:TS, NI, h:h + 1], scale=-1.0).then_inc(exp_ready, 1)

            def av(h):
                for i in range(NI):
                    o = take(act, ("h", h, i))
                    act.activation(ht[:, i, :], o[:, 0:DH + 1], ACT.Copy).then_inc(out_sem(("h", h, i)), 1)
                o = take(act, ("C", h))
                if h:
                    act.wait_ge(cout_out, 16 * h)
                act.activation(cout[:, :, :], o.rearrange("p (c k) -> p c k", c=2), ACT.Copy).then_inc(out_sem(("C", h)), 1)
                if h == 0:
                    for q in range(2):
                        act.wait_ge(cstage_out[q], 32 * KT // 2)
                for b in range(NB):
                    u = NB * h + b
                    o = take(act, ("ct", h, b))
                    if u >= 2:
                        if b >= 2:
                            act.wait_ge(down_kt, (NB - 1) * h + b - 1)
                        else:
                            act.wait_ge(held_done, h)
                    act.activation(cT[:, u % 2, :, 0:DH], o.rearrange("p (c k) -> p c k", c=2), ACT.Copy).then_inc(out_sem(("ct", h, b)), 1)
                act.wait_ge(held_done, h + 1)
                act.activation(ht[0:TS, NI, :], held[0:TS, 0:DH + 1], ACT.Copy).then_inc(held_out, 1)

            def convnorm():
                for k in range(KT):
                    h, c = k // 2, k % 2
                    if k == 0:
                        wait_taken(act, ("hTs", NH - 1))
                        wait_taken(act, ("hT", NH - 1, 0))
                        wait_taken(act, ("hT", NH - 1, 1))
                        act.wait_ge(ncol_ready, NB * NH)
                        wait_taken(act, ("u", NH - 1, NB - 1))
                        wait_taken(act, ("n", NH - 1))
                        for s in range(2):
                            act.wait_ge(cnew_out[s], 16 * NB * NH // 2)
                        act.wait_ge(cout_out, 16 * NH)
                        act.wait_ge(nout_out, 32 * NH)
                    act.activation(hhi[:, k, :], hab[:, k, :], ACT.Copy).then_inc(hhi_ready, 1)
                for j in range(KT):
                    act.wait_ge(xc_ready, j + 1)
                    if j >= 4:
                        act.wait_ge(m_ready, j - 3)
                    act.activation(lnt[:, 2 + j % 4, :], upad[:, j, CH:CH + T], ACT.Square).then_inc(sqc_ready, 1)
                for name, (a, b) in (("vara", HALVES[0]), ("varb", HALVES[1])):
                    o = take(act, name)
                    act.activation(lnt[:, 1, a:b], o[:, 0:b - a], ACT.Sqrt, scale=1.0 / D, bias=epsc[:, 0:1]).then_inc(out_sem(name), 1)
                for j in range(KT):
                    act.wait_ge(yln, j + 1)
                    if j >= 2:
                        act.wait_ge(zs, j - 1)
                    act.activation(lnt[:, 4 + j % 2, :], lnt[:, 2 + j % 2, :], ACT.Sigmoid,
                                   bias=vec[:, CLB + j:CLB + j + 1], scale=vec[:, CLG + j:CLG + j + 1]).then_inc(ysig, 1)
                    act.wait_ge(zs, j + 1)
                    act.activation(uhi[:, j, :], upad[:, j, CH:CH + T], ACT.Copy).then_inc(uhi_ready, 1)

            def residual():
                for k in range(KT):
                    o = take(act, ("xr", k))
                    act.activation(x1[:, k, 0:TP], o, ACT.Copy).then_inc(out_sem(("xr", k)), 1)
                o = take(act, "xrs")
                act.activation(x1[:, :, TP:T], o[:, 0:KT * TS].rearrange("p (k t) -> p k t", k=KT), ACT.Copy).then_inc(out_sem("xrs"), 1)

            def norm2():
                for j in range(KT):
                    wait_acc_out(act, index_of[("out", j // 2)], j % 2)
                    if j >= 4:
                        act.wait_ge(x1_in, j - 3)
                    act.activation(sq2[:, j % 4, :], x1[:, j, :], ACT.Square).then_inc(sq_ready, 1)
                for name, (a, b) in (("qa", HALVES[0]), ("qb", HALVES[1])):
                    o = take(act, name)
                    act.activation(mb[:, a:b], o[:, 0:b - a], ACT.Sqrt, scale=1.0 / D, bias=epsc[:, 0:1]).then_inc(out_sem(name), 1)
                for j in range(KT):
                    act.wait_ge(hf_ready, j + 1)
                    act.activation(ahi[:, j, :], sq2[:, j % 4, :], ACT.Copy).then_inc(hfhi, 1)

            def fstate(i):
                o = take(act, ("fs", i))
                if i:
                    act.wait_ge(act_ready, 2 * i)
                    act.wait_ge(small_done, ring_of[("ft", i - 1)] + 1)
                    act.wait_ge(flast_ready, i)
                dst = up[:, :, FK - 1 + TP:FK - 1 + TP + NB * FSEG].rearrange("p c (b s) -> p c b s", s=FSEG)
                for c in range(2):
                    t = act.activation(dst[:, c, :, 0:2], o[:, 16 * c:16 * c + 16].rearrange("p (b s) -> p b s", s=2), ACT.Copy)
                    if c == 0:
                        chain.raised_by(t)
                t.then_inc(out_sem(("fs", i)), 1)

            def ftail(i):
                o = take(act, ("ft", i))
                if i >= 2:
                    act.wait_ge(fout_out[i % 2], 64 * (i // 2))
                act.activation(fout[:, i % 2, :], o[0:18, 0:2 * P], ACT.Copy).then_inc(out_sem(("ft", i)), 1)

            def final():
                for i in range(NI + 1):
                    n = P if i < NI else TS
                    for q in range(2):
                        o = take(act, ("y", i, q))
                        chain.raised_by(act.activation(yt[0:n, i, 512 * q:512 * q + 512], o[0:n, :], ACT.Copy))
                        if i or q:
                            act.wait_ge(yssq, 2 * i + q)
                        link(act.activation(junk[0:n, :], o[0:n, :], ACT.Square, accum_out=stat[0:n, 16 + 2 * i + q:17 + 2 * i + q]))
                        act.activation(stat[0:n, 31:32], epsc[0:n, 0:1], ACT.Copy).then_inc(yssq, 1)
                        act.wait_ge(yssq, 2 * i + q + 1)
                        act.activation(stat[0:n, 32:33], epsc[0:n, 0:1], ACT.Copy).then_inc(out_sem(("y", i, q)), 1)

            def panel(kind, i):
                n = index_of[(kind, i)]
                if kind == "glu":
                    if i:
                        wait_acc_out(act, index_of[("glu", i - 1)], 0)
                    out_of(n, 1, sg[:, :], ACT.Sigmoid)
                elif kind == "k":
                    if i == 0:
                        for m in range(NI + 1):
                            pass
                        wait_taken(act, "xTs")
                        wait_taken(act, "rts")
                        act.wait_ge(gates_dve, 2)
                        wait_taken(act, ("cst", 1, 1))
                    for c in range(2):
                        out_of(n, c, kT[:, c, :], ACT.Copy, scale=DH ** -0.5)
                elif kind in "vq":
                    for c in range(2):
                        out_of(n, c, vqT[:, c, :], ACT.Copy)
                elif kind == "o":
                    for c in range(2):
                        out_of(n, c, hab[:, 2 * i + c, :], ACT.Sigmoid)
                elif kind == "gate":
                    if i == 0:
                        act.wait_ge(small_done, ring_of[("ss", NH - 1)] + 1)
                        act.wait_ge(qm_ready, NH)
                    if i >= 2:
                        act.wait_ge(mix_ready, i - 1)
                    for c in range(2):
                        out_of(n, c, sga[:, i % 2, c, :], ACT.Sigmoid)
                elif kind == "branch":
                    if i == KT - 1:
                        for k in range(KT):
                            if k == KT - 1:
                                act.wait_ge(mix_ready, KT)
                            act.wait_ge(mix_ready, k + 1)
                            act.activation(ahi[:, k, :], mix[:, k, :], ACT.Copy).then_inc(mhi_ready, 1)
                elif kind == "up":
                    for c in range(2):
                        p, s, done = acc_ready(act, n, c)
                        dst = up[:, c, FK - 1 + TP:FK - 1 + TP + NB * FSEG].rearrange("p (b s) -> p b s", s=FSEG)[:, :, 2:FSEG]
                        chain.raised_by(act.activation(dst, s.rearrange("p (b s) -> p b s", s=NS), ACT.Copy))
                        act.activation(up[:, c, FK - 1:FK - 1 + TP].rearrange("p (a t) -> p a t", a=2), p, ACT.Copy).then_inc(done, 1)
                    wait_acc_out(act, n, 0)
                    wait_acc_out(act, n, 1)
                    act.wait_ge(act_chain, chain.n)
                    ends = up[:, :, TP:TP + 9 * FSEG].rearrange("p c (b s) -> p c b s", s=FSEG)[:, :, :, 0:2]
                    act.activation(flast[:, :, :].rearrange("p c (b s) -> p c b s", s=2), ends, ACT.Copy).then_inc(flast_ready, 1)
                    act.wait_ge(sig_ready, 2 * i + 1)
                    act.activation(usig[:, :], upc[:, 0, :], ACT.Sigmoid).then_inc(sig_ready, 1)
                elif kind == "down":
                    g, s = i
                    for k in range(ktiles(n)):
                        kt = 8 * s + k
                        u = KF * g + kt
                        if u >= 3:
                            wait_down(act, u - 3)
                        if u == 0:
                            act.wait_ge(act_ready, 2 * KF)
                        act.activation(dhi[:, u % 3, :], act_tile(kt), ACT.Copy).then_inc(dhi_ready, 1)
                if n + 2 < len(panels):
                    split_hi(n + 2)

            for s in steps:
                {"setup": lambda: setup(), "gates": lambda: gates_step(), "tail": lambda: tail(s[1]),
                 "kv": lambda: kv(s[1]), "scores": lambda: scores(s[1]), "av": lambda: av(s[1]),
                 "headout": lambda: None, "convnorm": lambda: convnorm(),
                 "residual": lambda: residual(), "norm2": lambda: norm2(), "fstate": lambda: fstate(s[1]),
                 "ftail": lambda: ftail(s[1]), "final": lambda: final(),
                 "panel": lambda: panel(*s[1:])}[s[0]]()

        @block.vector
        def _(dve):
            chain = Count(dve_chain)
            tt, stt, ts = dve.tensor_tensor, dve.scalar_tensor_tensor, dve.tensor_scalar

            def link(ins):
                chain.raised_by(ins)
                dve.wait_ge(dve_chain, chain.n)

            def split_lo(n):
                dve.wait_ge(w_hi, n + 1)
                tt(panel_view(wlo, n % 2, n), panel_view(raw, n % NRAW, n), panel_view(whi, n % 2, n).bitcast(F32),
                   ALU.subtract).then_inc(w_lo, 1)

            def setup():
                for n in range(2):
                    split_lo(n)
                wait_taken(dve, ("vec", 0))
                for k in range(KT):
                    o = take(dve, ("xT", k))
                    dve.wait_ge(xn_hi, k + 1)
                    stt(alo[:, k, 0:TP], o, vec[:, MIXG + k:MIXG + k + 1], ahi[:, k, 0:TP].bitcast(F32),
                        ALU.mult, ALU.subtract).then_inc(out_sem(("xT", k)), 1)
                o = take(dve, "xTs")
                dve.wait_ge(xn_hi, 2 * KT)
                for k in range(KT):
                    t = stt(alo[:, k, TP:T], o[:, TS * k:TS * k + TS], vec[:, MIXG + k:MIXG + k + 1],
                            ahi[:, k, TP:T].bitcast(F32), ALU.mult, ALU.subtract)
                    if k < KT - 1:
                        chain.raised_by(t)
                t.then_inc(out_sem("xTs"), 1)

            def gates_step():
                n = index_of[("if", 0)]
                p, s, done = acc_ready(dve, n, 0)
                dve.wait_ge(consts_in[7], 16)
                dve.wait_ge(consts_in[16], 16)
                dve.wait_ge(consts_in[17], 16)
                dve.wait_ge(consts_set, 2)
                dve.wait_ge(ssq_ready, 1)
                G = gates
                zi, zf = G[0:4, 0, :], G[32:36, 0, :]
                for r, b in ((0, 0), (32, 1)):
                    link(ts(G[r:r + 4, 0, 0:TP].rearrange("p (a t) -> p a t", a=2), p[r:r + 4], stat[r:r + 4, 38:39], None, ALU.add))
                    if b == 0:
                        link(ts(G[r:r + 4, 0, TP:T], s[r:r + 4], stat[r:r + 4, 38:39], None, ALU.add))
                    else:
                        ts(G[r:r + 4, 0, TP:T], s[r:r + 4], stat[r:r + 4, 38:39], None, ALU.add).then_inc(done, 1)
                        wait_acc_out(dve, n, 0)
                link(ts(G[32:36, 2, :], zf, -1.0, None, ALU.mult))
                tt(G[32:36, 1, :], zf, G[32:36, 2, :], ALU.min).then_inc(gates_dve, 1)
                dve.wait_ge(gates_act, 1)
                link(stt(G[0:4, 1, :], zf, 0.0, G[32:36, 3, :], ALU.min, ALU.subtract))
                link(dve.tensor_tensor_scan(G[0:4, 2, 0:TP], ones4(), G[0:4, 1, 0:TP], 0.0, ALU.mult, ALU.add))
                sb_ = G[0:4, 2, TP:T].rearrange("p (b t) -> p b t", t=NS)
                lf_ = G[0:4, 1, TP:T].rearrange("p (b t) -> p b t", t=NS)
                link(dve.tensor_copy(sb_[:, :, 0], lf_[:, :, 0]))
                for t in range(1, NS):
                    link(tt(sb_[:, :, t], sb_[:, :, t - 1], lf_[:, :, t], ALU.add))
                link(tt(rows[0:4, :], zi, G[0:4, 2, :], ALU.subtract))
                link(dve.tensor_tensor_scan(mrow[:, 0:TP], ones4(), rows[0:4, 0:TP], 0.0, ALU.mult, ALU.max))
                sm_ = mrow[:, TP:T].rearrange("p (b t) -> p b t", t=NS)
                a_ = rows[0:4, TP:T].rearrange("p (b t) -> p b t", t=NS)
                m0 = stat[0:4, 22:30]
                link(tt(sm_[:, :, 0], m0, a_[:, :, 0], ALU.max))
                for t in range(1, NS):
                    link(tt(sm_[:, :, t], sm_[:, :, t - 1], a_[:, :, t], ALU.max))
                tt(rows[32:36, :], G[0:4, 2, :], mrow[:, 0:T], ALU.add).then_inc(m_out, 1)
                link(ts(G[0:4, 4, 0:TP], rows[0:4, 0:TP], mrow[:, TP - 1:TP], None, ALU.subtract))
                last = sm_[:, :, NS - 1:NS]
                link(tt(G[0:4, 4, TP:T].rearrange("p (b t) -> p b t", t=NS), a_, last.broadcast_to([NH, NB, NS]), ALU.subtract))
                m0b = m0.rearrange("p (b t) -> p b t", t=1)
                link(tt(G[0:4, 5, 0:TS].rearrange("p (b t) -> p b t", t=NS), m0b.broadcast_to([NH, NB, NS]), sm_, ALU.subtract))
                dve.wait_ge(m_out, 1)
                tt(G[0:4, 5, TS:TS + NB], m0, sm_[:, :, NS - 1], ALU.subtract).then_inc(gates_dve, 1)

            def ones4():
                return gates[0:4, 3, 0:TP]

            conv_queue = []

            def conv_block(j):
                u = upad[:, j, :]
                steps_ = []
                seg = u[:, CH + TP:UPW].rearrange("p (b s) -> p b s", s=SEG)

                def window(q):
                    w = seg[:, :, 2 * q:2 * q + 2]
                    ap = [list(x) for x in w.ap]
                    return bass.AP(w.tensor, w.offset, [ap[0], ap[1], [1, 2], [1, CK]])

                steps_.append(lambda: link(ts(cacc[:, 0:TP], u[:, 0:TP], cw[:, j, 0:1], vec[:, CB + j:CB + j + 1], ALU.mult, ALU.add)))
                for q in range(2):
                    steps_.append(lambda q=q: link(tt(prod[:, :, :, :], window(q),
                                                      cw[:, j, :].rearrange("p (b t k) -> p b t k", b=1, t=1).broadcast_to([P, NB, 2, CK]), ALU.mult)))
                    steps_.append(lambda q=q: link(dve.tensor_reduce(cacc[:, TP:T].rearrange("p (b t) -> p b t", t=NS)[:, :, 2 * q:2 * q + 2],
                                                                     prod[:, :, :, :], mybir.AxisListType.X, ALU.add)))
                for k in range(1, CK - 1):
                    steps_.append(lambda k=k: link(stt(cacc[:, 0:TP], u[:, k:k + TP], cw[:, j, k:k + 1], cacc[:, 0:TP], ALU.mult, ALU.add)))

                def last():
                    dve.wait_ge(small_done, ring_of[("ut", j)] + 1)
                    link(stt(u[:, CH:CH + TP], u[:, CH:CH + TP], cw[:, j, CH:CH + 1], cacc[:, 0:TP], ALU.mult, ALU.add))
                    ts(u[:, CH + TP:CH + T], cacc[:, TP:T], vec[:, CB + j:CB + j + 1], None, ALU.add).then_inc(uc_ready, 1)
                    dve.wait_ge(uc_ready, j + 1)
                steps_.append(last)
                return steps_

            def conv(n):
                for _ in range(min(n, len(conv_queue))):
                    conv_queue.pop(0)()

            def kv(h):
                dve.wait_ge(rt_ready, 1)
                wait_taken(dve, "rt")
                for q in range(3):
                    o = take(dve, ("kt", h, q))
                    if h and q == 0:
                        dve.wait_ge(small_done, ring_of[("u", h - 1, NB - 1)] + 1)
                    if q < 2:
                        chain.raised_by(ts(gk[:, 2 * q, :], o[:, 0:DH], rt[:, 2 * q, 64 + h:65 + h], None, ALU.mult))
                        ts(gk[:, 2 * q + 1, :], o[:, DH:2 * DH], rt[:, 2 * q + 1, 64 + h:65 + h], None, ALU.mult).then_inc(out_sem(("kt", h, q)), 1)
                    else:
                        ts(gk[0:TS, NI, :], o[0:TS, 0:DH], rt[0:TS, NI, 64 + h:65 + h], None, ALU.mult).then_inc(out_sem(("kt", h, q)), 1)

            def scores(h):
                for j in range(NI + 1):
                    dve.wait_ge(exp_ready, (NI + 1) * h + j + 1)
                    name = ("s", h, j) if j < NI else ("ss", h)
                    o = take(dve, name)
                    if j < NI:
                        tt(sT[:, j, P * j:TP], sT[:, j, P * j:TP], o[:, P * j:TP], ALU.mult).then_inc(out_sem(name), 1)
                    else:
                        tt(sTs[:, :], sTs[:, :], o[0:TS, 0:TS], ALU.mult).then_inc(out_sem(name), 1)
                wait_taken(dve, ("mbs", h))
                if h:
                    dve.wait_ge(held_done, h)
                else:
                    dve.wait_ge(consts_set, 3)
                for c in range(2):
                    dst = qm[:, c, :].rearrange("p (b s) -> p b s", s=36)[:, :, 0:NS]
                    t = tt(dst, vqT[:, c, TP:T].rearrange("p (b t) -> p b t", t=NS), mb[:, T:T + TS].rearrange("p (b t) -> p b t", t=NS), ALU.mult)
                    if c == 0:
                        chain.raised_by(t)
                t.then_inc(qm_ready, 1)

            def av(h):
                o = take(dve, ("n", h))
                if h:
                    dve.wait_ge(nout_out, 32 * h)
                wait_taken(dve, "rts")
                dve.wait_ge(consts_in[18], 16)
                chain.raised_by(dve.tensor_copy(nout[0:1, 0, :], o[0:1, 0:DH]))
                nready = stt(nout[:, 1, :], nh[:, h, :], gib[:, h:h + 1], o[0:NB, DH:2 * DH], ALU.mult, ALU.add)
                nready.then_inc(out_sem(("n", h)), 1)
                wait_taken(dve, ("kt", h, 2))

                def mask(b):
                    u = NB * h + b
                    if u >= 2:
                        b2, h2 = (b - 2) % NB, h - (b < 2)
                        dve.wait_ge(small_done, ring_of[("u", h2, b2)] + 1)
                    ts(km[:, u % 2, :], gk[0:TS, NI, :], bmask[:, b:b + 1], None, ALU.mult).then_inc(km_ready, 1)

                mask(0)
                mask(1)
                for b in range(NB):
                    u = NB * h + b
                    o = take(dve, ("u", h, b))
                    if u >= 2:
                        dve.wait_ge(cnew_out[u % 2], 16 * (u // 2))
                    dve.wait_ge(cin_in[u % 2], 16 * (u // 2 + 1))
                    stt(cnew[:, u % 2, :, :], cin[:, u % 2, :, :], mb[:, T + TS + b:T + TS + b + 1],
                        o.rearrange("p (c k) -> p c k", c=2), ALU.mult, ALU.add).then_inc(out_sem(("u", h, b)), 1)
                    if b + 2 < NB:
                        mask(b + 2)
                dve.wait_ge(em_ready, 1)
                if h == 0:
                    dve.wait_ge(consts_set, 2)
                for i in range(NI):
                    wait_taken(dve, ("h", h, i))
                dve.wait_ge(held_out, h + 1)
                for i in range(NI + 1):
                    n = P if i < NI else TS
                    link(stt(stat[0:n, i:i + 1], ht[0:n, i, DH:DH + 1], -1.0, ht[0:n, i, DH:DH + 1], ALU.mult, ALU.max))
                    link(tt(stat[0:n, i:i + 1], stat[0:n, i:i + 1], em[0:n, i, h:h + 1], ALU.max))
                    link(dve.bn_stats(junkst(n), ht[0:n, i, 0:DH]))
                    link(dve.bn_aggr(stat[0:n, 12 + 2 * i:14 + 2 * i], junkst(n)))
                link(dve.reciprocal(stat[:, 0:5], stat[:, 0:5]))
                var = stat[:, 12:22].rearrange("p (i q) -> p i q", q=2)[:, :, 1]
                link(tt(stat[:, 5:10], stat[:, 0:5], stat[:, 0:5], ALU.mult))
                link(tt(stat[:, 5:10], stat[:, 5:10], var, ALU.mult))
                ts(stat[:, 5:10], stat[:, 5:10], EPS, None, ALU.add).then_inc(hv_ready, 1)
                dve.wait_ge(hr_ready, h + 1)
                link(tt(stat[:, 0:5], stat[:, 0:5], stat[:, 5:10], ALU.mult))
                for i in range(NI + 1):
                    n = P if i < NI else TS
                    t = ts(ht[0:n, i, 0:DH], ht[0:n, i, 0:DH], stat[0:n, 12 + 2 * i:13 + 2 * i], stat[0:n, i:i + 1], ALU.subtract, ALU.mult)
                    if i < NI:
                        chain.raised_by(t)
                dve.wait_ge(dve_chain, chain.n)
                t.then_inc(hn_ready, 1)

            def junkst(n):
                return stat[0:n, 32:38]

            def headout(h):
                wait_acc_out(dve, index_of[("o", h)], 0)
                wait_acc_out(dve, index_of[("o", h)], 1)
                for c in range(2):
                    k = 2 * h + c
                    o = take(dve, ("hT", h, c))
                    stt(hab[:, k, 0:TP], o, vec[:, HEADG + k:HEADG + k + 1], hab[:, k, 0:TP], ALU.mult, ALU.mult).then_inc(out_sem(("hT", h, c)), 1)
                o = take(dve, ("hTs", h))
                for c in range(2):
                    k = 2 * h + c
                    t = stt(hab[:, k, TP:T], o[:, TS * c:TS * c + TS], vec[:, HEADG + k:HEADG + k + 1], hab[:, k, TP:T], ALU.mult, ALU.mult)
                    if c == 0:
                        chain.raised_by(t)
                t.then_inc(out_sem(("hTs", h)), 1)

            def convnorm():
                conv(len(conv_queue))
                dve.wait_ge(dve_chain, chain.n)
                for name, (a, b) in (("mua", HALVES[0]), ("mub", HALVES[1])):
                    o = take(dve, name)
                    if name == "mua":
                        dve.wait_ge(hhi_ready, 1)
                        wait_taken(dve, ("hTs", NH - 1))
                    ts(lnt[:, 0, a:b], o[:, 0:b - a], 1.0 / D, None, ALU.mult).then_inc(out_sem(name), 1)
                wait_taken(dve, "mua")
                wait_taken(dve, "mub")
                for j in range(KT):
                    tt(upad[:, j, CH:CH + T], upad[:, j, CH:CH + T], lnt[:, 0, :], ALU.subtract).then_inc(xc_ready, 1)
                for k in range(KT):
                    dve.wait_ge(hhi_ready, k + 1)
                    tt(hlo[:, k, :], hab[:, k, :], hhi[:, k, :].bitcast(F32), ALU.subtract).then_inc(hlo_ready, 1)
                wait_taken(dve, "vara")
                wait_taken(dve, "varb")
                dve.reciprocal(lnt[:, 1, :], lnt[:, 1, :]).then_inc(lnstd, 1)
                dve.wait_ge(lnstd, 1)
                dve.wait_ge(xc_ready, KT)
                dve.wait_ge(sqc_ready, KT)

                def normed(j):
                    if j >= 2:
                        dve.wait_ge(ysig, j - 1)
                    tt(lnt[:, 2 + j % 2, :], upad[:, j, CH:CH + T], lnt[:, 1, :], ALU.mult).then_inc(yln, 1)

                normed(0)
                for j in range(KT):
                    dve.wait_ge(yln, j + 1)
                    link(ts(upad[:, j, CH:CH + T], lnt[:, 2 + j % 2, :], vec[:, CLG + j:CLG + j + 1], vec[:, CLB + j:CLB + j + 1], ALU.mult, ALU.add))
                    if j + 1 < KT:
                        normed(j + 1)
                    dve.wait_ge(ysig, j + 1)
                    tt(upad[:, j, CH:CH + T], upad[:, j, CH:CH + T], lnt[:, 4 + j % 2, :], ALU.mult).then_inc(zs, 1)
                    dve.wait_ge(uhi_ready, j + 1)
                    tt(ulo[:, j, CH:CH + T], upad[:, j, CH:CH + T], uhi[:, j, :].bitcast(F32), ALU.subtract).then_inc(ulo_ready, 1)

            def norm2():
                wait_taken(dve, "qa")
                wait_taken(dve, "qb")
                dve.reciprocal(mb[:, 0:T], mb[:, 0:T]).then_inc(std2, 1)
                dve.wait_ge(std2, 1)
                dve.wait_ge(sq_ready, KT)
                for j in range(KT):
                    if j >= 4:
                        dve.wait_ge(hflo, j - 3)
                    stt(sq2[:, j % 4, :], x1[:, j, :], vec[:, FG + j:FG + j + 1], mb[:, 0:T], ALU.mult, ALU.mult).then_inc(hf_ready, 1)
                    if j:
                        lo2(j - 1)
                lo2(KT - 1)

            def lo2(j):
                dve.wait_ge(hfhi, j + 1)
                tt(alo[:, j, :], sq2[:, j % 4, :], ahi[:, j, :].bitcast(F32), ALU.subtract).then_inc(hflo, 1)

            def panel(kind, i):
                n = index_of[(kind, i)]
                if kind == "glu":
                    if i == 0:
                        wait_taken(dve, ("cst", 1, 1))
                        wait_taken(dve, ("cst", 1, 0))
                        dve.wait_ge(consts_set, 2)
                    p, s, done = acc_ready(dve, n, 0)
                    wait_acc_out(dve, n, 1)
                    dve.wait_ge(act_chain, 0) if False else None
                    new = upad[:, i, CH + TP:UPW].rearrange("p (b s) -> p b s", s=SEG)[:, :, CH:SEG]
                    chain.raised_by(tt(new, s.rearrange("p (b t) -> p b t", t=NS), sg[:, TP:T].rearrange("p (b t) -> p b t", t=NS), ALU.mult))
                    tt(upad[:, i, CH:CH + TP].rearrange("p (a t) -> p a t", a=2), p, sg[:, 0:TP].rearrange("p (a t) -> p a t", a=2), ALU.mult).then_inc(done, 1)
                    wait_acc_out(dve, n, 0)
                    dve.wait_ge(dve_chain, chain.n)
                    if i >= 2:
                        dve.wait_ge(small_done, ring_of[("ut", i - 2)] + 1)
                    dve.tensor_copy(unew[:, i % 2, :].rearrange("p (b t) -> p b t", t=NS), new).then_inc(unew_ready, 1)
                    if i == 0:
                        wait_taken(dve, "cw")
                    conv_queue.extend(conv_block(i))
                elif kind == "branch":
                    if i == 0:
                        dve.wait_ge(ysig, KT)
                    for c in range(2):
                        p, s, done = acc_ready(dve, n, c)
                        wait_acc_out(dve, index_of[("gate", i)], c)
                        g = sga[:, i % 2, c, :]
                        chain.raised_by(tt(g[:, TP:T], s, g[:, TP:T], ALU.mult))
                        tt(g[:, 0:TP].rearrange("p (a t) -> p a t", a=2), p, g[:, 0:TP].rearrange("p (a t) -> p a t", a=2), ALU.mult).then_inc(done, 1)
                    wait_acc_out(dve, n, 0)
                    wait_acc_out(dve, n, 1)
                    dve.wait_ge(dve_chain, chain.n)
                    tt(mix[:, i, :], sga[:, i % 2, 0, :], sga[:, i % 2, 1, :], ALU.add).then_inc(mix_ready, 1)
                    if i == KT - 1:
                        dve.wait_ge(mix_ready, KT)
                        for k in range(KT):
                            dve.wait_ge(mhi_ready, k + 1)
                            tt(alo[:, k, :], mix[:, k, :], ahi[:, k, :].bitcast(F32), ALU.subtract).then_inc(mlo_ready, 1)
                elif kind in ("out", "down"):
                    if kind == "out" or i[1] == 2:
                        for c in range(2):
                            k = 2 * (i if kind == "out" else i[0]) + c
                            if kind == "out" and k == 0:
                                wait_taken(dve, "xrs")
                                for m in range(KT):
                                    wait_taken(dve, ("xr", m))
                            if kind == "down":
                                down_lo(n) if c == 0 else None
                            p, s, done = acc_ready(dve, n, c)
                            chain.raised_by(tt(x1[:, k, TP:T], s, x1[:, k, TP:T], ALU.add))
                            tt(x1[:, k, 0:TP].rearrange("p (a t) -> p a t", a=2), p, x1[:, k, 0:TP].rearrange("p (a t) -> p a t", a=2), ALU.add).then_inc(done, 1)
                    else:
                        down_lo(n)
                elif kind == "up":
                    wait_taken(dve, ("fs", i))
                    wait_acc_out(dve, n, 0)
                    wait_acc_out(dve, n, 1)
                    for c in range(2):
                        k = KF * c + i
                        if i == 0 and c == 0:
                            dve.wait_ge(consts_set, 4)
                            wait_taken(dve, ("vec", 1))
                            wait_taken(dve, ("vec", 2))
                        link(ts(upc[:, c, :], up[:, c, 0:FOUT], fcw[:, 0, k:k + 1], vec[:, FB + k:FB + k + 1], ALU.mult, ALU.add))
                        link(stt(upc[:, c, :], up[:, c, 1:1 + FOUT], fcw[:, 1, k:k + 1], upc[:, c, :], ALU.mult, ALU.add))
                        t = stt(upc[:, c, :], up[:, c, 2:2 + FOUT], fcw[:, 2, k:k + 1], upc[:, c, :], ALU.mult, ALU.add)
                        if c == 0:
                            t.then_inc(sig_ready, 1)
                        else:
                            link(t)
                    dve.wait_ge(sig_ready, 2 * i + 2)
                    link(tt(usig[:, :], usig[:, :], upc[:, 0, :], ALU.mult))
                    dst = act_tile(i)
                    tt(dst[:, 0:TP], usig[:, 0:TP], upc[:, 1, 0:TP], ALU.mult).then_inc(act_ready, 1)

                    def cut(x):
                        return x[:, TP:TP + NB * FSEG].rearrange("p (b s) -> p b s", s=FSEG)[:, :, 2:FSEG]
                    tt(dst[:, TP:T].rearrange("p (b t) -> p b t", t=NS), cut(usig), cut(upc[:, 1, :]), ALU.mult).then_inc(act_ready, 1)
                    dve.wait_ge(act_ready, 2 * i + 2)
                if n + 2 < len(panels):
                    split_lo(n + 2)
                conv({"glu": 6, "k": 8, "v": 8, "q": 8, "o": 8, "gate": 10}.get(kind, 0))

            def down_lo(n):
                g, s = panels[n][1]
                for k in range(ktiles(n)):
                    kt = 8 * s + k
                    u = KF * g + kt
                    if u >= 3:
                        wait_down(dve, u - 3)
                    dve.wait_ge(dhi_ready, u + 1)
                    tt(dlo[:, u % 3, :], act_tile(kt), dhi[:, u % 3, :].bitcast(F32), ALU.subtract).then_inc(dlo_ready, 1)

            def final():
                dve.wait_ge(fg_in, 16)
                dve.wait_ge(yrs, 1)
                for q in range(2 * (NI + 1)):
                    wait_taken(dve, ("y", q // 2, q % 2))
                for i in range(NI + 1):
                    n = P if i < NI else TS
                    stt(yt[0:n, i, :], yt[0:n, i, :], stat[0:n, 8 + i:9 + i], fgb[0:n, :], ALU.mult, ALU.mult).then_inc(y_ready, 1)

            for s in steps:
                {"setup": lambda: setup(), "gates": lambda: gates_step(), "tail": lambda: None,
                 "kv": lambda: kv(s[1]), "scores": lambda: scores(s[1]), "av": lambda: av(s[1]),
                 "headout": lambda: headout(s[1]), "convnorm": lambda: convnorm(),
                 "residual": lambda: None, "norm2": lambda: norm2(), "fstate": lambda: None,
                 "ftail": lambda: None, "final": lambda: final(),
                 "panel": lambda: panel(*s[1:])}[s[0]]()

        @block.gpsimd
        def _(pool):
            chain = Count(pool_chain)

            def link(ins):
                chain.raised_by(ins)
                pool.wait_ge(pool_chain, chain.n)

            def column_rows(v, n):
                return v[0].rearrange("(r c) -> r c", c=P)

            def setup():
                pool.memset(raw[:, 0, 0:KT * P], 0.0).then_inc(raw_zeroed, 1)
                link(pool.memset(ident[:, :], 0.0))
                link(pool.affine_select(out=ident[:, :], in_=ident[:, :], compare_op=ALU.not_equal, fill=1.0,
                                        base=0, pattern=[[-1, P]], channel_multiplier=1))
                link(pool.memset(epsc[:, 0:1], EPS))
                link(pool.memset(epsc[:, 1:2], -0.5))
                link(pool.memset(stat[:, :], 1.0))
                pool.memset(ones[:, :], 1.0).then_inc(consts_set, 1)
                loads = [(vrow[48:92, 0, :], ffn_conv_b[0].rearrange("(r c) -> r c", c=P), 0),
                         (vrow[0:44, 1, :], ffn_conv_w[0, 0].rearrange("(r c) -> r c", c=P), 1),
                         (vrow[0:44, 2, :], ffn_conv_w[0, 2].rearrange("(r c) -> r c", c=P), 2),
                         (cwrow[:, :], conv_w[0], 3),
                         (cst[:, 0, :], state_conv[0, 0:4].rearrange("b r d -> (b r) d"), 4),
                         (cst[:, 1, :], state_conv[0, 4:8].rearrange("b r d -> (b r) d"), 5),
                         (nin[:, :], state_n[0].rearrange("b h k -> (b h) k"), 6),
                         (vrow[0:8, 0, :], column_rows(mix_norm_g, 8), 8),
                         (vrow[8:16, 0, :], column_rows(head_norm_g, 8), 9),
                         (vrow[16:24, 0, :], column_rows(conv_b, 8), 10),
                         (vrow[24:32, 0, :], column_rows(conv_ln_g, 8), 11),
                         (vrow[32:40, 0, :], column_rows(conv_ln_b, 8), 12),
                         (vrow[40:48, 0, :], column_rows(ffn_norm_g, 8), 13),
                         (vrow[44:88, 1, :], ffn_conv_w[0, 1].rearrange("(r c) -> r c", c=P), 15)]
                for dst, src, s in loads:
                    pool.dma_start(dst, src).then_inc(consts_in[s], 16)
                pool.wait_ge(consts_set, 1)
                pool.dma_start(stat[0:4, 38:39], b_if[0, 0:NH].rearrange("(a b) -> a b", b=1)).then_inc(consts_in[7], 16)
                pool.dma_start(stat[32:36, 38:39], b_if[0, NH:2 * NH].rearrange("(a b) -> a b", b=1)).then_inc(consts_in[16], 16)
                pool.wait_ge(ssq_ready, 1)
                link(pool.tensor_scalar(stat[:, 8:13], stat[:, 0:5], 1.0 / D, EPS, ALU.mult, ALU.add))
                pool.tensor_tensor(stat[:, 8:13], stat[:, 8:13], epsc[:, 1:2].broadcast_to([P, 5]), ALU.pow).then_inc(rs_ready, 1)
                pool.dma_start(stat[0:4, 22:30], state_m[0].rearrange("b h -> h b"), allow_slow_non_contiguous=True).then_inc(consts_in[17], 16)
                pool.dma_start(nh[:, :, :], state_n[0]).then_inc(consts_in[18], 16)
                link(pool.memset(sel[:, :, :], 0.0))
                link(pool.affine_select(out=sel[:, :, :], in_=sel[:, :, :], compare_op=ALU.not_equal, fill=1.0,
                                        base=0, pattern=[[-1, NH], [0, P]], channel_multiplier=1))
                link(pool.memset(bmask[:, :], 1.0))
                link(pool.affine_select(out=bmask[:, :], in_=bmask[:, :], compare_op=ALU.is_ge, fill=0.0,
                                        base=0, pattern=[[-NS, NB]], channel_multiplier=1))
                link(pool.affine_select(out=bmask[:, :], in_=bmask[:, :], compare_op=ALU.is_ge, fill=0.0,
                                        base=NS - 1, pattern=[[NS, NB]], channel_multiplier=-1))
                link(pool.memset(rows[:, :], 0.0))
                link(pool.memset(rt[:, NI, :], 0.0))
                link(pool.memset(gates[0:4, 3, :], 1.0))
                pool.memset(upad[:, :, 0:CH], 0.0).then_inc(consts_set, 1)
                pool.wait_ge(consts_set, 2)

            def gates_step():
                pool.wait_ge(m_out, 1)
                pool.dma_start(m_prompt[0].rearrange("b h -> h b"), rows[32:36, TP - 1:TP], allow_slow_non_contiguous=True).then_inc(rowcopy_out, 16)
                pool.dma_start(m_sample[0].rearrange("b h -> h b"),
                               rows[32:36, TP:T].rearrange("p (b t) -> p b t", t=NS)[:, :, NS - 1], allow_slow_non_contiguous=True).then_inc(rowcopy_out, 16)
                pool.dma_start(conv_sample[0, :, 0:CH - NS, :], state_conv[0, :, NS:CH, :]).then_inc(rowcopy_out, 16)

            def tail(j):
                wait_taken(pool, ("ut", j))
                pool.dma_start(conv_prompt[0, 0, :, P * j:P * j + P], cstage[0:CH, j % 2, 0:P]).then_inc(cstage_out[j % 2], 16)
                pool.dma_start(conv_sample[0, :, CH - NS:CH, P * j:P * j + P],
                               cstage[:, j % 2, P:2 * P]).then_inc(cstage_out[j % 2], 16)

            def kv(h):
                if h == 0:
                    wait_taken(pool, "xTs")
                    wait_taken(pool, ("cst", 1, 1))
                    wait_taken(pool, ("cst", 1, 0))
                    pool.wait_ge(gates_dve, 2)
                    pool.wait_ge(rows_ready, 1)
                    wait_taken(pool, "rts")
                    link(pool.memset(vk[:, :, DH:DH + 1], 1.0))
                    pool.memset(qm[:, :, :], 0.0).then_inc(consts_set, 1)

            def load_state(u):
                h, b = u // NB, u % NB
                if u >= 2:
                    v = u - 2
                    k = ring_of[("u", v // NB, v % NB)]
                    pool.wait_ge(small_out[k % RING], k // RING + 1)
                    pool.wait_ge(small_done, ring_of[("ct", v // NB, v % NB)] + 1)
                pool.dma_start(cin[:, u % 2, :, :], state_C[0, b, h].rearrange("(c p) k -> p c k", p=P)).then_inc(cin_in[u % 2], 16)

            def scores(h):
                if h == 0:
                    for u in range(2):
                        load_state(u)
                for j in range(NI):
                    wait_taken(pool, ("s", h, j))
                    blk = sT[:, j, P * j:P * j + P]
                    pool.affine_select(out=blk, in_=blk, compare_op=ALU.is_ge, fill=0.0, base=0,
                                       pattern=[[1, P]], channel_multiplier=-1).then_inc(st_masked, 1)
                wait_taken(pool, ("ss", h))
                v = sTs[:, :].rearrange("p (b t) -> p b t", t=NS)
                pool.affine_select(out=v, in_=v, compare_op=ALU.is_ge, fill=0.0, base=0,
                                   pattern=[[NS, NB], [1, NS]], channel_multiplier=-1).then_inc(st_masked, 1)
                pool.wait_ge(st_masked, (NI + 2) * h + NI + 1)
                pool.affine_select(out=v, in_=v, compare_op=ALU.is_ge, fill=0.0, base=0,
                                   pattern=[[-NS, NB], [0, NS]], channel_multiplier=1).then_inc(st_masked, 1)

            def av(h):
                wait_taken(pool, ("C", h))
                pool.dma_start(C_prompt[0, 0, h].rearrange("(c p) k -> p c k", p=P), cout[:, :, :]).then_inc(cout_out, 16)
                wait_taken(pool, ("n", h))
                pool.dma_start(n_prompt[0, 0, h:h + 1, :], nout[0:1, 0, :]).then_inc(nout_out, 16)
                pool.dma_start(n_sample[0, :, h, :], nout[:, 1, :]).then_inc(nout_out, 16)
                wait_taken(pool, "nT")
                if h == 0:
                    for q in range(2):
                        pool.wait_ge(cstage_out[q], 32 * KT // 2)
                for b in range(NB):
                    u = NB * h + b
                    if u >= 2:
                        if b >= 2:
                            pool.wait_ge(down_kt, (NB - 1) * h + b - 1)
                        else:
                            pool.wait_ge(held_done, h)
                    pool.tensor_copy(cT[:, u % 2, :, DH:DH + 1], nT[:, :, NH * b + h:NH * b + h + 1]).then_inc(ncol_ready, 1)
                    wait_taken(pool, ("u", h, b))
                    pool.dma_start(C_sample[0, b, h].rearrange("(c p) k -> p c k", p=P), cnew[:, u % 2, :, :]).then_inc(cnew_out[u % 2], 16)
                    if u + 2 < NB * NH:
                        load_state(u + 2)
                pool.wait_ge(hv_ready, h + 1)
                pool.tensor_tensor(stat[:, 5:10], stat[:, 5:10], epsc[:, 1:2].broadcast_to([P, 5]), ALU.pow).then_inc(hr_ready, 1)

            def branch_last():
                n = index_of[("branch", KT - 1)]
                wait_panel_used(pool, n)
                for i in range(NI):
                    pool.dma_start(xin2[:, i, :], x_prompt[0, P * i:P * i + P, :]).then_inc(xin2_in[i], 16)
                pool.dma_start(xin2[0:TS, NI, :], x_sample.rearrange("b t d -> (b t) d")).then_inc(xin2_in[NI], 16)

            def load_fstate(i):
                if i >= 2:
                    pool.wait_ge(small_done, ring_of[("fs", i - 2)] + 1)
                src = state_ffn[0].rearrange("b t c -> (b t) c")
                for c in range(2):
                    pool.dma_start(fst[:, i % 2, P * c:P * c + P], src[:, DFF * c + P * i:DFF * c + P * i + P]).then_inc(fst_in[i % 2], 16)

            def norm2():
                wait_panel_used(pool, index_of[("out", 3)])
                link(pool.memset(up[:, :, 0:FK - 1], 0.0))
                pool.memset(up[:, :, FPW - 4:FPW], 0.0).then_inc(consts_set, 1)
                for i in range(2):
                    load_fstate(i)

            def ftail(i):
                wait_taken(pool, ("ft", i))
                for c in range(2):
                    cols = slice(DFF * c + P * i, DFF * c + P * i + P)
                    pool.dma_start(ffn_prompt[0, 0, :, cols], fout[0:2, i % 2, P * c:P * c + P]).then_inc(fout_out[i % 2], 16)
                    pool.dma_start(ffn_sample[0].rearrange("b t c -> (b t) c")[:, cols], fout[2:18, i % 2, P * c:P * c + P]).then_inc(fout_out[i % 2], 16)
                if i + 2 < KF:
                    load_fstate(i + 2)

            def final():
                wait_panel_used(pool, index_of[("down", (3, 1))])
                pool.wait_ge(dlo_ready, 4 * KF)
                pool.dma_start(fgb[:, :], final_norm_g.rearrange("(a d) -> a d", a=1).broadcast_to([P, D])).then_inc(fg_in, 16)
                for i in range(NI + 1):
                    wait_taken(pool, ("y", i, 1))
                wait_taken(pool, ("y", NI, 0))
                pair = stat[:, 16:26].rearrange("p (i q) -> p i q", q=2)
                link(pool.tensor_tensor(stat[:, 8:13], pair[:, :, 0], pair[:, :, 1], ALU.add))
                link(pool.tensor_scalar(stat[:, 8:13], stat[:, 8:13], 1.0 / D, EPS, ALU.mult, ALU.add))
                pool.tensor_tensor(stat[:, 8:13], stat[:, 8:13], epsc[:, 1:2].broadcast_to([P, 5]), ALU.pow).then_inc(yrs, 1)
                for i in range(NI + 1):
                    pool.wait_ge(y_ready, i + 1)
                    if i < NI:
                        pool.dma_start(y_prompt[0, P * i:P * i + P, :], yt[:, i, :]).then_inc(y_out, 16)
                    else:
                        pool.dma_start(y_sample.rearrange("b t d -> (b t) d"), yt[0:TS, NI, :]).then_inc(y_out, 16)
                pool.wait_ge(y_out, 16 * (NI + 1))
                pool.wait_ge(rowcopy_out, 48)
                pool.wait_ge(cout_out, 16 * NH)
                pool.wait_ge(nout_out, 32 * NH)
                for q in range(2):
                    pool.wait_ge(cnew_out[q], 16 * NB * NH // 2)
                    pool.wait_ge(cstage_out[q], 32 * KT // 2)
                    pool.wait_ge(fout_out[q], 64 * KF // 2)

            for s in steps:
                if s[0] == "panel":
                    if s[1:] == ("branch", KT - 1):
                        branch_last()
                    continue
                {"setup": lambda: setup(), "gates": lambda: gates_step(), "tail": lambda: tail(s[1]),
                 "kv": lambda: kv(s[1]), "scores": lambda: scores(s[1]), "av": lambda: av(s[1]),
                 "headout": lambda: None, "convnorm": lambda: None,
                 "residual": lambda: None, "norm2": lambda: norm2(), "fstate": lambda: None,
                 "ftail": lambda: ftail(s[1]), "final": lambda: final()}[s[0]]()


_INS = ['x_prompt', 'x_sample', 'state_C', 'state_n', 'state_m', 'state_conv', 'state_ffn', 'mix_norm_g',
        'w_in', 'b_if', 'head_norm_g', 'w_mlstm_out', 'conv_w', 'conv_b', 'conv_ln_g', 'conv_ln_b',
        'w_conv_out', 'w_out', 'ffn_norm_g', 'w_up', 'ffn_conv_w', 'ffn_conv_b', 'w_down', 'final_norm_g']
_OUTS = [(1, TP, D), (NB, NS, D), (1, 1, NH, DH, DH), (1, 1, NH, DH), (1, 1, NH), (1, 1, CH, D),
         (1, 1, FK - 1, 2 * DFF), (1, NB, NH, DH, DH), (1, NB, NH, DH), (1, NB, NH), (1, NB, CH, D),
         (1, NB, FK - 1, 2 * DFF)]


def kernel(**inputs):
    import numpy as _np
    import concourse.bacc as _bacc
    from concourse import mybir as _mybir
    from concourse.bass_utils import run_bass_kernel_spmd as _run

    nc = _bacc.Bacc("TRN2", target_bir_lowering=False, num_devices=1)
    arrays, args = {}, []
    for name in _INS:
        a = _np.ascontiguousarray(inputs[name])
        arrays[f"in_{name}"] = a
        args.append(nc.dram_tensor(f"in_{name}", a.shape, _mybir.dt.from_np(a.dtype), kind="ExternalInput").ap())
    for i, shape in enumerate(_OUTS):
        args.append(nc.dram_tensor(f"out_{i}", shape, _mybir.dt.float32, kind="ExternalOutput").ap())
    build(nc, *args)
    r = _run(nc, [arrays], core_ids=[0])
    return tuple(r.results[0][f"out_{i}"] for i in range(len(_OUTS)))
```

```python
from contextlib import ExitStack

import concourse.bass as bass
from concourse import mybir

F32 = mybir.dt.float32
F32R = mybir.dt.float32r
ALU = mybir.AluOpType
ACT = mybir.ActivationFunctionType

P = 128
D = 1024
KT = D // P
TP = 512
NB, NS = 8, 4
TS = NB * NS
T = TP + TS
HALVES = ((0, 256), (256, T))
NH, DH = 4, 256
NI = TP // P
CK = 31
CH = CK - 1
SEG = CH + NS
DFF = 2816
KF = DFF // P
FK = 3
FSEG = FK - 1 + NS
UPW = CH + TP + NB * SEG
FPW = FK - 1 + TP + NB * FSEG + 4
RESIDUAL = (range(0, 2), range(2, 5), range(5, KT))
BEFORE = {"glu": 5, "k": 5, "v": 5, "q": 5, "o": 4}
BEHIND = {"glu": 5, "v": 5, "q": 5}
FOUT = TP + NB * FSEG
EPS = 1e-6
NRAW = 3
RING = 3
COLS = 256


class Count:

    def __init__(self, sem):
        self.sem, self.n = sem, 0

    def raised_by(self, ins):
        ins.then_inc(self.sem, 1)
        self.n += 1


def plan():
    steps = [("setup", 0), ("panel", "if", 0), ("gates", 0)]
    for j in range(KT):
        steps.append(("panel", "glu", j))
        if j == 1:
            steps.append(("gateturn", 0))
        if j:
            steps.append(("tail", j - 1))
    for h in range(NH):
        steps.append(("panel", "k", h))
        if h == 0:
            steps.append(("tail", KT - 1))
        if h >= 2:
            steps.append(("headout", h - 2))
        if h:
            steps += [("av", h - 1), ("state", h - 1, 0)]
        steps.append(("panel", "v", h))
        if h:
            steps += [("state", h - 1, b) for b in (1, 2, 3)]
        steps += [("kv", h), ("weights", h), ("panel", "q", h)]
        if h:
            steps += [("state", h - 1, b) for b in (4, 5, 6, 7)]
        steps.append(("scores", h))
        if h:
            steps.append(("headnorm", h - 1))
    last = NH - 1
    steps += [("panel", "o", last), ("headout", last - 1), ("av", last), ("state", last, 0),
              ("panel", "o", 0), ("state", last, 1), ("state", last, 2), ("convmean", 0),
              ("panel", "o", 1), ("state", last, 3), ("state", last, 4), ("convvar", 0),
              ("panel", "o", 2), ("state", last, 5), ("state", last, 6), ("state", last, 7), ("convapply", 0),
              ("panel", "gate", 0), ("headnorm", last), ("panel", "gate", 1), ("headout", last), ("split", 0)]
    for i in range(KT):
        steps.append(("panel", "branch", i))
        if i + 2 < KT:
            steps.append(("panel", "gate", i + 2))
    steps += [("panel", "out", 0), ("panel", "out", 1), ("residual", 0), ("panel", "out", 2), ("residual", 1),
              ("panel", "out", 3), ("residual", 2), ("norm2", 0)]
    for i in range(KF):
        steps += [("fstate", i), ("panel", "up", i)]
        if i:
            steps.append(("ftail", i - 1))
    steps.append(("ftail", KF - 1))
    for g in range(4):
        steps += [("panel", "down", (g, q)) for q in range(3)]
    steps.append(("final", 0))
    return steps


def build(nc, x_prompt, x_sample, state_C, state_n, state_m, state_conv, state_ffn, mix_norm_g,
          w_in, b_if, head_norm_g, w_mlstm_out, conv_w, conv_b, conv_ln_g, conv_ln_b, w_conv_out,
          w_out, ffn_norm_g, w_up, ffn_conv_w, ffn_conv_b, w_down, final_norm_g,
          y_prompt, y_sample, C_prompt, n_prompt, m_prompt, conv_prompt, ffn_prompt,
          C_sample, n_sample, m_sample, conv_sample, ffn_sample):
    ctx = ExitStack()
    steps = plan()

    at = [16512]

    def sb(name, shape, dt=F32, offset=None):
        size = 4
        for n in shape[1:]:
            size *= n
        if offset is None:
            offset = at[0]
            at[0] += (size + 31) // 32 * 32
        assert offset + size <= nc.sbuf_usable_end, (name, offset + size)
        return nc.alloc_sbuf_tensor_at(name, shape, dt, offset=offset)

    def after(offset, *shape):
        size = 4
        for n in shape:
            size *= n
        return offset + (size + 31) // 32 * 32

    raw = sb("raw", [P, NRAW, KT * COLS])
    whi = sb("whi", [P, 2, KT * COLS], F32R)
    wlo = sb("wlo", [P, 2, KT * COLS], F32R)
    ahi = sb("ahi", [P, KT, T], F32R)
    alo = sb("alo", [P, KT, T], F32R)
    ident = sb("ident", [P, P])
    ones = sb("ones", [P, P])
    vec = sb("vec", [P, 92])
    fcw = sb("fcw", [P, FK, KF * 2])
    cw = sb("cw", [P, KT, CK])
    stat = sb("stat", [P, 40])
    epsc = sb("epsc", [P, 2])
    sel_at = at[0]
    sel = sb("sel", [NH, NH, P])
    bmask = sb("bmask", [TS, NB])
    rows = sb("rows", [P, T])
    mrow = sb("mrow", [NH, T + TS + NB])
    rt = sb("rt", [P, NI + 1, P])
    em = sb("em", [P, NI + 1, NH])
    bst = sb("bst", [P, NI + 1, 6])
    gib = sb("gib", [NB, NH])
    mb = sb("mb", [P, T + TS + NB])
    fsm_end = at[0]

    MIXG, HEADG, CB, CLG, CLB, FG, FB = 0, 8, 16, 24, 32, 40, 48

    arena = at[0]
    upad = sb("upad", [P, KT, UPW])
    ulo = sb("ulo", [P, KT, UPW], F32R, offset=arena)
    hab_at = at[0]
    hab = sb("hab", [P, KT, T])
    hlo = sb("hlo", [P, KT, T], F32R, offset=hab_at)
    x1 = sb("x1", [P, KT, T], offset=hab_at)
    work = at[0]
    kT = sb("kT", [P, 2, T])
    vqT = sb("vqT", [P, 2, T])
    gk = sb("gk", [P, NI, DH])
    vk = sb("vk", [P, NI, DH + 1])
    sT = sb("sT", [P, NI, TP])
    gks = sb("gks", [TS, 2, DH])
    vks = sb("vks", [TS, 2, DH + 1])
    sTs = sb("sTs", [TS, TS])
    gic = sb("gic", [P, 2, NB])
    ht = sb("ht", [P, NI + 1, DH + 1])
    cin = sb("cin", [P, 2, 2, DH])
    cT_at = at[0]
    cT = sb("cT", [P, 2, 2, DH + 1])
    cnew_at = at[0]
    cnew = sb("cnew", [P, 2, 2, DH])
    qm = sb("qm", [P, 2, 36 * NB])
    km_nout = sb("km_nout", [P, 2, DH])
    km, nout = km_nout[0:TS], km_nout[64:64 + NB]
    nT = sb("nT", [P, 2, TS])
    nh = sb("nh", [NB, DH])
    cout = sb("cout", [P, 2, DH])
    cacc = sb("cacc", [P, T])
    prod_at = at[0]
    prod = sb("prod", [P, NB, 2, CK])
    sg = sb("sg", [P, T], offset=cnew_at)
    cstage = sb("cstage", [TS, 2, 2 * P], offset=cT_at)
    unew = sb("unew", [P, 2, TS], offset=cnew_at + 4 * T)
    xin = sb("xin", [P, NI + 1, D], offset=work)
    s1 = after(work, NI + 1, D)
    cst = sb("cst", [NB // 2 * CH, 2, D], offset=s1)
    s2 = after(s1, 2, D)
    vrow = sb("vrow", [P, 3, P], offset=s2)
    cwrow = sb("cwrow", [CK, D], offset=after(s2, 3, P))
    gates = sb("gates", [P, 6, T], offset=after(after(s2, 3, P), D))
    nin = sb("nin", [TS, DH], offset=after(after(after(s2, 3, P), D), 6, T))
    assert after(after(after(after(s2, 3, P), D), 6, T), DH) <= prod_at
    sga = sb("sga", [P, 2, 2, T], offset=work)
    b1 = after(work, 4, T)
    uhi = sb("uhi", [P, KT, T], F32R, offset=after(b1, KT, T))
    hhi = sb("hhi", [P, KT, T], F32R, offset=after(after(b1, KT, T), KT, T))
    mix = sb("mix", [P, KT, T], offset=b1)
    lnt = sb("lnt", [P, 6, T], offset=b1)
    xin2 = sb("xin2", [P, NI + 1, D], offset=arena)
    sq2 = sb("sq2", [P, 4, T], offset=work)
    xrs = sb("xrs", [P, KT * TS], offset=after(after(work, 4, T), T))
    sqsum = sb("sqsum", [P, T], offset=after(work, 4, T))
    f0 = arena
    hact = sb("hact", [P, 17, T], offset=work)
    hact2 = sb("hact2", [P, KF - 17, T], offset=f0)
    f1 = after(f0, KF - 17, T)
    dhi = sb("dhi", [P, 3, T], F32R, offset=f1)
    dlo_at = after(f1, 3, T)
    f3 = sel_at
    fst = sb("fst", [NB * 2, 2, 2 * P], offset=after(work, 17, T))
    f4 = after(after(work, 17, T), 2, 2 * P)
    fout = sb("fout", [NB * 2 + 2, 2, 2 * P], offset=f4)
    f5 = after(f4, 2, 2 * P)
    up = sb("up", [P, 2, FPW], offset=f5)
    f6 = after(f5, 2, FPW)
    upc = sb("upc", [P, 2, FOUT], offset=f6)
    f7 = after(f6, 2, FOUT)
    usig = sb("usig", [P, FOUT], offset=f7)
    flast = sb("flast", [P, 2, 2, 18], offset=after(f7, FOUT))
    dlo = sb("dlo", [P, 3, T], F32R, offset=dlo_at)
    assert after(dlo_at, 3, T) <= hab_at
    x2 = sb("x2", [P, KT, T], offset=hab_at)
    yt = sb("yt", [P, NI + 1, D], offset=work)
    fgb = sb("fgb", [P, D], offset=after(work, NI + 1, D))
    junk = sb("junk", [P, TP], offset=after(after(work, NI + 1, D), D))

    with ctx:
        acc = ctx.enter_context(nc.psum_tensor("acc", [P, 2, 2, 512], F32))
        small = ctx.enter_context(nc.psum_tensor("small", [P, RING, 512], F32))
        held = ctx.enter_context(nc.psum_tensor("held", [P, 512], F32))

        def sem(name):
            return ctx.enter_context(nc.semaphore(name))

        raw_in = [sem(f"raw_in{i}") for i in range(NRAW)]
        raw_zeroed = sem("raw_zeroed")
        w_hi, w_lo_dve, w_lo_pool = sem("w_hi"), sem("w_lo_dve"), sem("w_lo_pool")
        down_part = sem("down_part")
        acc_done = sem("acc_done")
        acc_out = [sem("acc_out0"), sem("acc_out1")]
        small_done = sem("small_done")
        small_out = [sem(f"small_out{i}") for i in range(RING)]
        held_done, held_out = sem("held_done"), sem("held_out")
        x_in = [sem(f"x_in{i}") for i in range(NI + 1)]
        consts_in = [sem(f"consts_in{i}") for i in range(22)]
        consts_set = sem("consts_set")
        rs_ready, xs_ready, xn_hi = sem("rs_ready"), sem("xs_ready"), sem("xn_hi")
        ssq_ready = sem("ssq_ready")
        gates_act, gates_dve, rows_ready, rt_ready, sqc_used = (sem(x) for x in ("gates_act", "gates_dve", "rows_ready", "rt_ready", "sqc_used"))
        em_ready = sem("em_ready")
        cstage_out = [sem("cstage_out0"), sem("cstage_out1")]
        uc_ready = sem("uc_ready")
        unew_ready, flast_ready = sem("unew_ready"), sem("flast_ready")
        exp_ready, st_ready, st_masked, qm_ready = sem("exp_ready"), sem("st_ready"), sem("st_masked"), sem("qm_ready")
        cin_in = [sem("cin_in0"), sem("cin_in1")]
        cnew_out = [sem("cnew_out0"), sem("cnew_out1")]
        nT_ready = sem("nT_ready")
        km_ready = sem("km_ready")
        ht_in, hv_ready, hr_ready, hn_ready = sem("ht_in"), sem("hv_ready"), sem("hr_ready"), sem("hn_ready")
        cout_ready, cout_out = sem("cout_ready"), sem("cout_out")
        nout_out = sem("nout_out")
        hab_gated, x1_raw, sqsum_ready = sem("hab_gated"), sem("x1_raw"), sem("sqsum_ready")
        hhi_ready, hlo_ready = sem("hhi_ready"), sem("hlo_ready")
        xc_ready, sqc_ready, lnstd, yln, ysig, zs, uhi_ready, ulo_ready = (
            sem(x) for x in ("xc_ready", "sqc_ready", "lnstd", "yln", "ysig", "zs", "uhi_ready", "ulo_ready"))
        mix_ready, mhi_ready, mlo_ready = sem("mix_ready"), sem("mhi_ready"), sem("mlo_ready")
        sq2_used = sem("sq2_used")
        x1_ready, sq_ready, std2, hf_ready, hfhi, hflo = (sem(x) for x in ("x1_ready", "sq_ready", "std2", "hf_ready", "hfhi", "hflo"))
        xin2_in = [sem(f"xin2_in{i}") for i in range(NI + 1)]
        fst_in = [sem("fst_in0"), sem("fst_in1")]
        fout_out = [sem("fout_out0"), sem("fout_out1")]
        sig_ready, act_ready, dhi_ready, dlo_ready = sem("sig_ready"), sem("act_ready"), sem("dhi_ready"), sem("dlo_ready")
        act_used = sem("act_used")
        state_used = sem("state_used")
        fg_in = sem("fg_in")
        yssq, yrs, y_ready, y_out = sem("yssq"), sem("yrs"), sem("y_ready"), sem("y_out")
        rowcopy_out, m_out = sem("rowcopy_out"), sem("m_out")
        act_chain, dve_chain, pool_chain = sem("act_chain"), sem("dve_chain"), sem("pool_chain")

        panels = [s[1:] for s in steps if s[0] == "panel"]
        index_of = {p: n for n, p in enumerate(panels)}

        def block_count(p):
            if p[0] == "if":
                return 1
            return 2 if p[0] != "down" or p[1][1] == 2 else 0

        first_block, raw_value, n_blocks = [], [], 0
        raw_total = [0] * NRAW
        sources = []
        OQ = 0
        OK_, OV, OO = D, 2 * D, 3 * D
        OI = 4 * D
        OGV = OI + 2 * NH
        OGG, OGA, OGB = OGV + D, OGV + 2 * D, OGV + 3 * D
        for n, (kind, i) in enumerate(panels):
            first_block.append(n_blocks)
            n_blocks += block_count((kind, i))
            if kind == "if":
                src = [(w_in, 0, KT, OI, NH, 0), (w_in, 0, KT, OI + NH, NH, 32)]
            elif kind == "glu":
                src = [(w_in, 0, KT, OGG + P * i, P, 0), (w_in, 0, KT, OGV + P * i, P, P)]
            elif kind in "kvqo":
                base = {"q": OQ, "k": OK_, "v": OV, "o": OO}[kind]
                src = [(w_in, 0, KT, base + COLS * i, COLS, 0)]
            elif kind == "gate":
                src = [(w_in, 0, KT, OGA + P * i, P, 0), (w_in, 0, KT, OGB + P * i, P, P)]
            elif kind == "branch":
                src = [(w_mlstm_out, 0, KT, P * i, P, 0), (w_conv_out, 0, KT, P * i, P, P)]
            elif kind == "out":
                src = [(w_out, 0, KT, COLS * i, COLS, 0)]
            elif kind == "up":
                src = [(w_up, 0, KT, P * i, P, 0), (w_up, 0, KT, DFF + P * i, P, P)]
            else:
                g, s = i
                src = [(w_down, s * 8, min(8, KF - 8 * s), COLS * g, COLS, 0)]
            sources.append(src)
            raw_total[n % NRAW] += 16 * len(src)
            raw_value.append(raw_total[n % NRAW])

        first_pool, last_pool = index_of[("glu", 3)], index_of[("gate", 2)]

        def on_pool(n):
            return first_pool <= n <= last_pool

        def wait_lo(eng, n):
            if on_pool(n):
                eng.wait_ge(w_lo_pool, n - first_pool + 1)
            else:
                eng.wait_ge(w_lo_dve, n + 1 if n < first_pool else n - (last_pool - first_pool))

        def width(n):
            return P if panels[n][0] == "if" else COLS

        def ktiles(n):
            return sources[n][0][2]

        def panel_view(tile, slot, n):
            return tile[:, slot, 0:ktiles(n) * width(n)].rearrange("p (k c) -> p k c", c=width(n))

        def wait_panel_used(eng, n):
            kind, i = panels[n]
            if kind == "down" and i[1] < 2:
                eng.wait_ge(down_part, 2 * i[0] + i[1] + 1)
            else:
                eng.wait_ge(acc_done, first_block[n] + block_count(panels[n]))

        def acc_ready(eng, n, c):
            b = first_block[n] + c
            eng.wait_ge(acc_done, b + 1)
            return acc[:, b % 2, :, 0:256], acc[:, b % 2, 1, 256:256 + TS], acc_out[b % 2]

        def wait_acc_out(eng, n, c):
            b = first_block[n] + c
            eng.wait_ge(acc_out[b % 2], b // 2 + 1)

        ring_of = {}

        def small_at(name):
            return small[:, ring_of[name] % RING, :]

        def take(eng, name):
            eng.wait_ge(small_done, ring_of[name] + 1)
            return small_at(name)

        def out_sem(name):
            return small_out[ring_of[name] % RING]

        def wait_taken(eng, name):
            k = ring_of[name]
            eng.wait_ge(small_out[k % RING], k // RING + 1)

        def skip(*_):
            pass

        def act_tile(k):
            return hact[:, k, :] if k < 17 else hact2[:, k - 17, :]

        def wait_down(eng, u):
            g, k = u // KF, u % KF
            if k in (7, 15):
                eng.wait_ge(down_part, 2 * g + (k + 1) // 8)
            elif k == KF - 1:
                eng.wait_ge(acc_done, first_block[index_of[("down", (g, 2))]] + 2)
            else:
                eng.wait_ge(act_used, (KF - 3) * g + k + 1 - (k > 7) - (k > 15))

        block = ctx.enter_context(nc.Block())

        @block.tensor
        def _(pe):
            held_n = [0]

            def begin(name):
                k = len(ring_of)
                ring_of[name] = k
                if k >= RING:
                    pe.wait_ge(small_out[k % RING], k // RING)
                return small[:, k % RING, :]

            def end(ins):
                ins.then_inc(small_done, 1)

            def turn(out, src, n):
                return pe.transpose(out, src, ident[0:n, 0:n])

            def setup(_):
                pe.wait_ge(consts_set, 1)
                for i, w in enumerate((92, 88, 44)):
                    pe.wait_ge(consts_in[i], 16)
                    if i == 0:
                        for q in range(8, 14):
                            pe.wait_ge(consts_in[q], 16)
                    if i == 1:
                        pe.wait_ge(consts_in[15], 16)
                    o = begin(("vec", i))
                    end(turn(o[:, 0:w], vrow[0:w, i, :], w))
                pe.wait_ge(consts_in[3], 16)
                o = begin("cw")
                for j in range(KT):
                    t = turn(o[:, CK * j:CK * j + CK], cwrow[:, P * j:P * j + P], CK)
                end(t)
                for s in range(2):
                    pe.wait_ge(consts_in[4 + s], 16)
                    for q in range(2):
                        o = begin(("cst", s, q))
                        for j in range(4):
                            t = turn(o[:, 120 * j:120 * j + 120], cst[:, s, P * (4 * q + j):P * (4 * q + j) + P], 120)
                        end(t)
                pe.wait_ge(consts_in[6], 16)
                o = begin("nT")
                for c in range(2):
                    t = turn(o[:, TS * c:TS * c + TS], nin[:, P * c:P * c + P], TS)
                end(t)
                for k in range(KT):
                    o = begin(("xT", k))
                    if k == 0:
                        pe.wait_ge(xs_ready, NI + 1)
                    for i in range(NI):
                        t = turn(o[:, P * i:P * i + P], xin[:, i, P * k:P * k + P], P)
                    end(t)
                o = begin("xTs")
                for k in range(KT):
                    t = turn(o[:, TS * k:TS * k + TS], xin[0:TS, NI, P * k:P * k + P], TS)
                end(t)

            def gateturn(_):
                pe.wait_ge(rows_ready, 1)
                o = begin("rt")
                for i in range(NI):
                    t = turn(o[:, P * i:P * i + P], rows[:, P * i:P * i + P], P)
                end(t)
                o = begin("rts")
                turn(o[0:TS, 0:P], rows[:, TP:T], P)
                end(turn(o[0:NB, P:P + NH], mrow[:, T + TS:T + TS + NB], NH))

            def tail(j):
                wait_acc_out(pe, index_of[("glu", j)], 1)
                o = begin(("ut", j))
                turn(o[0:CH, 0:P], upad[:, j, CH + TP - CH:CH + TP], P)
                pe.wait_ge(unew_ready, j + 1)
                end(turn(o[0:TS, P:2 * P], unew[:, j % 2, :], P))

            def kv(h):
                wait_acc_out(pe, index_of[("k", h)], 1)
                for what, src in (("kt", kT), ("vt", vqT)):
                    if what == "vt":
                        wait_acc_out(pe, index_of[("v", h)], 1)
                        wait_acc_out(pe, index_of[("v", h)], 0)
                    else:
                        wait_acc_out(pe, index_of[("k", h)], 0)
                    for q in range(3):
                        if what == "kt" and q == 0 and h == 0:
                            pass
                        o = begin((what, h, q))
                        for i in ((0, 1), (2, 3), (4,))[q]:
                            n = P if i < NI else TS
                            for c in range(2):
                                at_ = 256 * (i % 2) + P * c
                                t = turn(o[0:n, at_:at_ + P], src[:, c, P * i:P * i + n], P)
                        end(t)

            def weights(h):
                o = begin(("mb", h))
                end(pe.matmul(o, sel[:, h, :], mrow[:, 0:TP], start=True, stop=True))
                o = begin(("mbs", h))
                end(pe.matmul(o[:, 0:2 * TS + NB], sel[:, h, :], mrow[:, TP:], start=True, stop=True))

            def scores(h):
                wait_acc_out(pe, index_of[("q", h)], 0)
                wait_acc_out(pe, index_of[("q", h)], 1)
                for j in range(NI):
                    o = begin(("s", h, j))
                    for c in range(2):
                        t = pe.matmul(o[:, P * j:TP], kT[:, c, P * j:P * j + P], vqT[:, c, P * j:TP],
                                      start=(c == 0), stop=(c == 1))
                    end(t)
                o = begin(("ss", h))
                for c in range(2):
                    t = pe.matmul(o[0:TS, 0:TS], kT[:, c, TP:T], vqT[:, c, TP:T], start=(c == 0), stop=(c == 1))
                end(t)

            def av(h):
                pe.wait_ge(consts_set, 3)
                wait_taken(pe, ("vt", h, 0))
                wait_taken(pe, ("vt", h, 1))
                wait_taken(pe, ("vt", h, 2))
                pe.wait_ge(st_masked, (NI + 2) * h + NI)
                for i in range(NI):
                    o = begin(("h", h, i))
                    for j in range(i + 1):
                        t = pe.matmul(o[:, 0:DH + 1], sT[:, j, P * i:P * i + P], vk[:, j, :],
                                      start=(j == 0), stop=(j == i))
                    end(t)
                o = begin(("C", h))
                for c in range(2):
                    for j in range(NI):
                        t = pe.matmul(o[:, DH * c:DH * c + DH], vk[:, j, P * c:P * c + P], gk[:, j, :],
                                      start=(j == 0), stop=(j == NI - 1))
                end(t)
                o = begin(("n", h))
                for j in range(NI):
                    pe.matmul(o[0:1, 0:DH], vk[:, j, DH:DH + 1], gk[:, j, :], start=(j == 0), stop=(j == NI - 1))
                end(pe.matmul(o[0:NB, DH:2 * DH], bmask[:, :], gks[:, h % 2, :], start=True, stop=True))
                if h:
                    pe.wait_ge(held_out, h)
                pe.wait_ge(st_masked, (NI + 2) * (h + 1))
                pe.matmul(held[0:TS, 0:DH + 1], sTs[:, :], vks[:, h % 2, :], start=True, stop=False)
                pe.wait_ge(qm_ready, h + 1)
                state_turn(h, 0)

            def state_turn(h, b):
                u = NB * h + b
                pe.wait_ge(cin_in[u % 2], 16 * (u // 2 + 1))
                o = begin(("ct", h, b))
                for c in range(2):
                    for v in range(2):
                        t = turn(o[:, DH * c + P * v:DH * c + P * v + P], cin[:, u % 2, v, P * c:P * c + P], P)
                end(t)

            def state(h, b):
                u = NB * h + b
                pe.wait_ge(km_ready, u + 1)
                o = begin(("u", h, b))
                for c in range(2):
                    t = pe.matmul(o[:, DH * c:DH * c + DH], vks[:, h % 2, P * c:P * c + P], km[:, u % 2, :],
                                  start=True, stop=True)
                end(t)
                if b + 1 < NB:
                    state_turn(h, b + 1)
                wait_taken(pe, ("ct", h, b))
                for c in range(2):
                    t = pe.matmul(held[0:TS, 0:DH + 1], qm[:, c, TS * b:TS * b + TS], cT[:, u % 2, c, :],
                                  start=False, stop=(b == NB - 1 and c == 1))
                if b < NB - 1:
                    t.then_inc(state_used, 1)
                else:
                    t.then_inc(held_done, 1)

            def headout(h):
                pe.wait_ge(hn_ready, h + 1)
                for c in range(2):
                    o = begin(("hT", h, c))
                    for i in range(NI):
                        t = turn(o[:, P * i:P * i + P], ht[:, i, P * c:P * c + P], P)
                    end(t)
                o = begin(("hTs", h))
                for c in range(2):
                    t = turn(o[:, TS * c:TS * c + TS], ht[0:TS, NI, P * c:P * c + P], TS)
                end(t)

            def convmean(_):
                oa, ob = begin("mua"), begin("mub")
                pe.wait_ge(uc_ready, KT)
                for o, (a, b) in ((oa, HALVES[0]), (ob, HALVES[1])):
                    for j in range(KT):
                        t = pe.matmul(o[:, 0:b - a], ones[:, :], upad[:, j, CH + a:CH + b],
                                      start=(j == 0), stop=(j == KT - 1))
                    end(t)

            def convvar(_):
                oa, ob = begin("vara"), begin("varb")
                for j in range(KT):
                    pe.wait_ge(sqc_ready, j + 1)
                    for o, (a, b) in ((oa, HALVES[0]), (ob, HALVES[1])):
                        t = pe.matmul(o[:, 0:b - a], ones[:, :], lnt[:, 2 + j % 4, a:b],
                                      start=(j == 0), stop=(j == KT - 1))
                        if j == KT - 1:
                            end(t)
                    if j < KT - 1:
                        t.then_inc(sqc_used, 1)

            def residual(part):
                if part == 0:
                    o = begin("xrs")
                    for i in range(NI + 1):
                        pe.wait_ge(xin2_in[i], 16)
                    for k in range(KT):
                        t = turn(o[:, TS * k:TS * k + TS], xin2[0:TS, NI, P * k:P * k + P], TS)
                    end(t)
                for k in RESIDUAL[part]:
                    o = begin(("xr", k))
                    for i in range(NI):
                        t = turn(o[:, P * i:P * i + P], xin2[:, i, P * k:P * k + P], P)
                    end(t)

            def norm2(_):
                oa, ob = begin("qa"), begin("qb")
                pe.wait_ge(sqsum_ready, KT)
                for o, (a, b) in ((oa, HALVES[0]), (ob, HALVES[1])):
                    end(pe.matmul(o[:, 0:b - a], ones[:, :], sqsum[:, a:b], start=True, stop=True))

            def fstate(i):
                pe.wait_ge(fst_in[i % 2], 32 * (i // 2 + 1))
                o = begin(("fs", i))
                for c in range(2):
                    t = turn(o[:, 16 * c:16 * c + 16], fst[:, i % 2, P * c:P * c + P], 16)
                end(t)

            def ftail(i):
                pe.wait_ge(flast_ready, i + 1)
                o = begin(("ft", i))
                for c in range(2):
                    t = turn(o[0:18, P * c:P * c + P], flast[:, i % 2, c, :], P)
                end(t)

            def final(_):
                for i in range(NI + 1):
                    n = P if i < NI else TS
                    for q in range(2):
                        o = begin(("y", i, q))
                        for j in range(4):
                            k = 4 * q + j
                            if i == 0:
                                wait_acc_out(pe, index_of[("down", (k // 2, 2))], k % 2)
                            t = turn(o[0:n, P * j:P * j + P], x2[:, k, P * i:P * i + n], P)
                        end(t)

            def panel(kind, i):
                n = index_of[(kind, i)]
                pe.wait_ge(w_hi, n + 1)
                wait_lo(pe, n)
                hi, lo = panel_view(whi, n % 2, n), panel_view(wlo, n % 2, n)
                if kind == "down":
                    g, s = i
                    kt0 = 8 * s
                    for k in range(ktiles(n)):
                        u = KF * g + kt0 + k
                        pe.wait_ge(dhi_ready, u + 1)
                        pe.wait_ge(dlo_ready, u + 1)
                        for c in range(2):
                            b = first_block[n] + c
                            if s == 0 and k == 0:
                                pe.wait_ge(acc_out[b % 2], b // 2)
                            for q, (w, x) in enumerate(((hi, dhi), (hi, dlo), (lo, dhi))):
                                for a, (t0, t1) in enumerate(HALVES):
                                    t = pe.matmul(acc[:, b % 2, a, 0:t1 - t0], w[:, k, P * c:P * c + P],
                                                  x[:, u % 3, t0:t1],
                                                  start=(s == 0 and k == 0 and q == 0),
                                                  stop=(s == 2 and k == ktiles(n) - 1 and q == 2))
                            if k == ktiles(n) - 1 and s == 2:
                                t.then_inc(acc_done, 1)
                        if not (k == ktiles(n) - 1):
                            t.then_inc(act_used, 1)
                    if s < 2:
                        t.then_inc(down_part, 1)
                    return
                for c in range(block_count((kind, i))):
                    xh, xl = ahi, alo
                    cut = 0
                    if kind == "if":
                        for k in range(KT):
                            wait_taken(pe, ("xT", k))
                        wait_taken(pe, "xTs")
                    if kind == "branch":
                        xh, xl = (hhi, hlo) if c == 0 else (uhi, ulo)
                        cut = 0 if c == 0 else CH
                    b = first_block[n] + c
                    if b >= 2:
                        pe.wait_ge(acc_out[b % 2], b // 2)
                    for k in range(KT):
                        if kind == "branch" and i == 0:
                            pe.wait_ge(hlo_ready if c == 0 else ulo_ready, k + 1)
                        if kind == "out" and i == 0 and c == 0:
                            pe.wait_ge(mlo_ready, k + 1)
                        if kind == "up" and i == 0 and c == 0:
                            pe.wait_ge(hflo, k + 1)
                        for q, (w, x, off) in enumerate(((hi, xh, 0), (hi, xl, cut), (lo, xh, 0))):
                            for a, (t0, t1) in enumerate(HALVES):
                                t = pe.matmul(acc[:, b % 2, a, 0:t1 - t0], w[:, k, P * c:P * c + P],
                                              x[:, k, off + t0:off + t1],
                                              start=(k == 0 and q == 0), stop=(k == KT - 1 and q == 2))
                    t.then_inc(acc_done, 1)

            for s in steps:
                {"setup": setup,
                 "gates": skip,
                 "gateturn": gateturn,
                 "tail": tail,
                 "kv": kv,
                 "weights": weights,
                 "scores": scores,
                 "av": av,
                 "state": state,
                 "headnorm": skip,
                 "headout": headout,
                 "convmean": convmean,
                 "convvar": convvar,
                 "convapply": skip,
                 "split": skip,
                 "residual": residual,
                 "norm2": norm2,
                 "fstate": fstate,
                 "ftail": ftail,
                 "final": final,
                 "panel": panel}[s[0]](*s[1:])

        @block.sync
        def _(sp):
            xp, xs = x_prompt[0], x_sample.rearrange("b t d -> (b t) d")
            for i in range(NI):
                sp.dma_start(xin[:, i, :], xp[P * i:P * i + P, :]).then_inc(x_in[i], 16)
            sp.dma_start(xin[0:TS, NI, :], xs).then_inc(x_in[NI], 16)

            def load(n):
                slot = n % NRAW
                if n == 0:
                    sp.wait_ge(raw_zeroed, 1)
                if n >= NRAW:
                    sp.wait_ge(w_hi, n - NRAW + 1)
                    wait_lo(sp, n - NRAW)
                view = panel_view(raw, slot, n)
                for mat, k0, kn, c0, cn, to in sources[n]:
                    src = mat[0, P * k0:P * (k0 + kn), c0:c0 + cn].rearrange("(k p) c -> p k c", p=P)
                    sp.dma_start(view[:, :, to:to + cn], src).then_inc(raw_in[slot], 16)

            def setup(_):
                load(0)
                load(1)
                rows_of = lambda v: v[0].rearrange("(r c) -> r c", c=P)
                loads = [(vrow[48:92, 0, :], rows_of(ffn_conv_b), 0),
                         (vrow[0:8, 0, :], rows_of(mix_norm_g), 8),
                         (vrow[8:16, 0, :], rows_of(head_norm_g), 9),
                         (vrow[16:24, 0, :], rows_of(conv_b), 10),
                         (vrow[24:32, 0, :], rows_of(conv_ln_g), 11),
                         (vrow[32:40, 0, :], rows_of(conv_ln_b), 12),
                         (vrow[40:48, 0, :], rows_of(ffn_norm_g), 13),
                         (vrow[0:44, 1, :], ffn_conv_w[0, 0].rearrange("(r c) -> r c", c=P), 1),
                         (vrow[44:88, 1, :], ffn_conv_w[0, 1].rearrange("(r c) -> r c", c=P), 15),
                         (vrow[0:44, 2, :], ffn_conv_w[0, 2].rearrange("(r c) -> r c", c=P), 2),
                         (cwrow[:, :], conv_w[0], 3),
                         (cst[:, 0, :], state_conv[0, 0:4].rearrange("b r d -> (b r) d"), 4),
                         (cst[:, 1, :], state_conv[0, 4:8].rearrange("b r d -> (b r) d"), 5),
                         (nin[:, :], state_n[0].rearrange("b h k -> (b h) k"), 6)]
                for dst, src, q in loads:
                    sp.dma_start(dst, src).then_inc(consts_in[q], 16)
                load(2)
                sp.dma_start(nh[:, :], state_n[0, :, 0, :]).then_inc(consts_in[18], 16)

            def gates_step(_):
                sp.wait_ge(m_out, 1)
                sp.dma_start(m_prompt[0].rearrange("b h -> h b"), rows[32:36, TP - 1:TP], allow_slow_non_contiguous=True).then_inc(rowcopy_out, 16)
                sp.dma_start(m_sample[0].rearrange("b h -> h b"),
                             rows[32:36, TP:T].rearrange("p (b t) -> p b t", t=NS)[:, :, NS - 1],
                             allow_slow_non_contiguous=True).then_inc(rowcopy_out, 16)
                sp.dma_start(conv_sample[0, :, 0:CH - NS, :], state_conv[0, :, NS:CH, :]).then_inc(rowcopy_out, 16)

            def tail(j):
                wait_taken(sp, ("ut", j))
                sp.dma_start(conv_prompt[0, 0, :, P * j:P * j + P], cstage[0:CH, j % 2, 0:P]).then_inc(cstage_out[j % 2], 16)
                sp.dma_start(conv_sample[0, :, CH - NS:CH, P * j:P * j + P],
                             cstage[:, j % 2, P:2 * P]).then_inc(cstage_out[j % 2], 16)

            def load_state(u):
                h, b = u // NB, u % NB
                if u >= 2:
                    v = u - 2
                    wait_taken(sp, ("u", v // NB, v % NB))
                    sp.wait_ge(small_done, ring_of[("ct", v // NB, v % NB)] + 1)
                sp.dma_start(cin[:, u % 2, :, :], state_C[0, b, h].rearrange("(c p) k -> p c k", p=P)).then_inc(cin_in[u % 2], 16)

            def scores(h):
                if h == 0:
                    for u in range(2):
                        load_state(u)

            def av(h):
                wait_taken(sp, ("C", h))
                sp.dma_start(C_prompt[0, 0, h].rearrange("(c p) k -> p c k", p=P), cout[:, :, :]).then_inc(cout_out, 16)
                wait_taken(sp, ("n", h))
                sp.dma_start(n_prompt[0, 0, h:h + 1, :], nout[0:1, 0, :]).then_inc(nout_out, 16)
                sp.dma_start(n_sample[0, :, h, :], nout[:, 1, :]).then_inc(nout_out, 16)
                if h + 1 < NH:
                    sp.dma_start(nh[:, :], state_n[0, :, h + 1, :]).then_inc(consts_in[18], 16)

            def state(h, b):
                u = NB * h + b
                wait_taken(sp, ("u", h, b))
                sp.dma_start(C_sample[0, b, h].rearrange("(c p) k -> p c k", p=P), cnew[:, u % 2, :, :]).then_inc(cnew_out[u % 2], 16)
                if u + 2 < NB * NH:
                    load_state(u + 2)

            def load_fstate(i):
                if i >= 2:
                    sp.wait_ge(small_done, ring_of[("fs", i - 2)] + 1)
                src = state_ffn[0].rearrange("b t c -> (b t) c")
                for c in range(2):
                    sp.dma_start(fst[:, i % 2, P * c:P * c + P], src[:, DFF * c + P * i:DFF * c + P * i + P]).then_inc(fst_in[i % 2], 16)

            def residual(part):
                if part == 2:
                    sp.wait_ge(mlo_ready, KT)
                    for i in range(2):
                        load_fstate(i)

            def fstate(i):
                if i + 2 < KF:
                    load_fstate(i + 2)

            def ftail(i):
                wait_taken(sp, ("ft", i))
                for c in range(2):
                    cols = slice(DFF * c + P * i, DFF * c + P * i + P)
                    sp.dma_start(ffn_prompt[0, 0, :, cols], fout[0:2, i % 2, P * c:P * c + P]).then_inc(fout_out[i % 2], 16)
                    sp.dma_start(ffn_sample[0].rearrange("b t c -> (b t) c")[:, cols], fout[2:18, i % 2, P * c:P * c + P]).then_inc(fout_out[i % 2], 16)

            def final(_):
                wait_panel_used(sp, index_of[("down", (3, 1))])
                sp.wait_ge(dlo_ready, 4 * KF)
                sp.dma_start(fgb[:, :], final_norm_g.rearrange("(a d) -> a d", a=1).broadcast_to([P, D])).then_inc(fg_in, 16)
                for i in range(NI + 1):
                    sp.wait_ge(y_ready, i + 1)
                    if i < NI:
                        sp.dma_start(y_prompt[0, P * i:P * i + P, :], yt[:, i, :]).then_inc(y_out, 16)
                    else:
                        sp.dma_start(y_sample.rearrange("b t d -> (b t) d"), yt[0:TS, NI, :]).then_inc(y_out, 16)
                sp.wait_ge(y_out, 16 * (NI + 1))
                sp.wait_ge(rowcopy_out, 48)
                sp.wait_ge(cout_out, 16 * NH)
                sp.wait_ge(nout_out, 32 * NH)
                for q in range(2):
                    sp.wait_ge(cnew_out[q], 16 * NB * NH // 2)
                    sp.wait_ge(cstage_out[q], 32 * KT // 2)
                    sp.wait_ge(fout_out[q], 64 * KF // 2)

            def panel(kind, i):
                n = index_of[(kind, i)]
                if n + NRAW < len(panels):
                    load(n + NRAW)
                if (kind, i) == ("branch", KT - 1):
                    wait_panel_used(sp, n)
                    for q in range(NI):
                        sp.dma_start(xin2[:, q, :], x_prompt[0, P * q:P * q + P, :]).then_inc(xin2_in[q], 16)
                    sp.dma_start(xin2[0:TS, NI, :], xs).then_inc(xin2_in[NI], 16)

            for s in steps:
                {"setup": setup,
                 "gates": gates_step,
                 "gateturn": skip,
                 "tail": tail,
                 "kv": skip,
                 "weights": skip,
                 "scores": scores,
                 "av": av,
                 "state": state,
                 "headnorm": skip,
                 "headout": skip,
                 "convmean": skip,
                 "convvar": skip,
                 "convapply": skip,
                 "split": skip,
                 "residual": residual,
                 "norm2": skip,
                 "fstate": fstate,
                 "ftail": ftail,
                 "final": final,
                 "panel": panel}[s[0]](*s[1:])

        @block.scalar
        def _(act):
            chain = Count(act_chain)

            def link(ins):
                chain.raised_by(ins)
                act.wait_ge(act_chain, chain.n)

            def split_hi(n):
                act.wait_ge(raw_in[n % NRAW], raw_value[n])
                if n >= 2:
                    wait_panel_used(act, n - 2)
                act.activation(panel_view(whi, n % 2, n), panel_view(raw, n % NRAW, n), ACT.Copy).then_inc(w_hi, 1)

            def out_of(n, c, dst, func, scale=1.0, last=True):
                p, s, done = acc_ready(act, n, c)
                chain.raised_by(act.activation(dst[:, TP:T], s, func, scale=scale))
                act.activation(dst[:, 0:TP].rearrange("p (a t) -> p a t", a=2), p, func, scale=scale).then_inc(done, 1)

            def setup(_):
                for i in range(NI + 1):
                    n = P if i < NI else TS
                    act.wait_ge(x_in[i], 16)
                    if i == 0:
                        act.wait_ge(consts_set, 1)
                    link(act.activation(gates[0:n, 0:2, 0:512], xin[0:n, i, :].rearrange("p (a b) -> p a b", a=2), ACT.Square,
                                        accum_out=stat[0:n, i:i + 1]))
                act.activation(stat[:, 30:31], epsc[:, 0:1], ACT.Copy).then_inc(ssq_ready, 1)
                for n in range(2):
                    split_hi(n)
                for i, w in enumerate((92, 88, 44)):
                    o = take(act, ("vec", i))
                    dst = vec[:, 0:92] if i == 0 else (fcw[:, 0:2, :] if i == 1 else fcw[:, 2, :])
                    src = o[:, 0:w] if i != 1 else o[:, 0:w].rearrange("p (a b) -> p a b", a=2)
                    act.activation(dst, src, ACT.Copy).then_inc(out_sem(("vec", i)), 1)
                o = take(act, "cw")
                act.activation(cw[:, :, :], o[:, 0:KT * CK].rearrange("p (j k) -> p j k", j=KT), ACT.Copy).then_inc(out_sem("cw"), 1)
                for s in range(2):
                    for q in range(2):
                        o = take(act, ("cst", s, q))
                        for j in range(4):
                            dst = upad[:, 4 * q + j, CH + TP:UPW].rearrange("p (b s) -> p b s", s=SEG)[:, 4 * s:4 * s + 4, 0:CH]
                            t = act.activation(dst, o[:, 120 * j:120 * j + 120].rearrange("p (b s) -> p b s", s=CH), ACT.Copy)
                            if j < 3:
                                chain.raised_by(t)
                        t.then_inc(out_sem(("cst", s, q)), 1)
                o = take(act, "nT")
                act.activation(nT[:, :, :], o[:, 0:2 * TS].rearrange("p (c t) -> p c t", c=2), ACT.Copy).then_inc(out_sem("nT"), 1)
                wait_taken(act, ("vec", 0))
                for k in range(KT):
                    o = take(act, ("xT", k))
                    act.activation(ahi[:, k, 0:TP], o, ACT.Copy, scale=vec[:, MIXG + k:MIXG + k + 1]).then_inc(xn_hi, 1)
                o = take(act, "xTs")
                for k in range(KT):
                    act.activation(ahi[:, k, TP:T], o[:, TS * k:TS * k + TS], ACT.Copy,
                                   scale=vec[:, MIXG + k:MIXG + k + 1]).then_inc(xn_hi, 1)

            def gates_step(_):
                act.wait_ge(gates_dve, 1)
                link(act.activation(gates[32:36, 2, :], gates[32:36, 1, :], ACT.Exp))
                act.activation(gates[32:36, 3, :], gates[32:36, 2, :], ACT.Ln, bias=1.0).then_inc(gates_act, 1)
                act.wait_ge(gates_dve, 2)
                chain.raised_by(act.activation(rows[64:68, :], gates[0:4, 4, :], ACT.Exp))
                chain.raised_by(act.activation(mrow[:, T:T + TS + NB], gates[0:4, 5, 0:TS + NB], ACT.Exp))
                act.activation(rows[96:100, TP:T], gates[0:4, 5, 0:TS], ACT.Exp).then_inc(rows_ready, 1)
                act.wait_ge(act_chain, chain.n)
                act.wait_ge(rows_ready, 1)

            def gateturn(_):
                o = take(act, "rt")
                act.activation(rt[:, 0:NI, :], o.rearrange("p (i c) -> p i c", i=NI), ACT.Copy).then_inc(out_sem("rt"), 1)
                o = take(act, "rts")
                act.activation(rt[0:TS, NI, :], o[0:TS, 0:P], ACT.Copy).then_inc(rt_ready, 1)
                act.activation(gib[:, :], o[0:NB, P:P + NH], ACT.Copy).then_inc(out_sem("rts"), 1)
                wait_taken(act, "rt")
                wait_taken(act, "rts")
                act.wait_ge(rt_ready, 1)
                act.activation(em[:, :, :], rt[:, :, 32:32 + NH], ACT.Exp, scale=-1.0).then_inc(em_ready, 1)

            def tail(j):
                o = take(act, ("ut", j))
                if j >= 2:
                    act.wait_ge(cstage_out[j % 2], 32 * (j // 2))
                chain.raised_by(act.activation(cstage[0:CH, j % 2, 0:P], o[0:CH, 0:P], ACT.Copy))
                act.activation(cstage[:, j % 2, P:2 * P], o[0:TS, P:2 * P], ACT.Copy).then_inc(out_sem(("ut", j)), 1)

            def kv(h):
                for q in range(3):
                    o = take(act, ("vt", h, q))
                    if q < 2:
                        act.activation(vk[:, 2 * q:2 * q + 2, 0:DH], o.rearrange("p (i c) -> p i c", i=2), ACT.Copy).then_inc(out_sem(("vt", h, q)), 1)
                    else:
                        act.activation(vks[:, h % 2, 0:DH], o[0:TS, 0:DH], ACT.Copy).then_inc(out_sem(("vt", h, q)), 1)

            def weights(h):
                o = take(act, ("mb", h))
                if h:
                    act.wait_ge(small_done, ring_of[("n", h - 1)] + 1)
                    act.wait_ge(qm_ready, h)
                act.activation(mb[:, 0:TP], o, ACT.Copy).then_inc(out_sem(("mb", h)), 1)
                o = take(act, ("mbs", h))
                chain.raised_by(act.activation(gic[:, h % 2, :], o[:, 2 * TS:2 * TS + NB], ACT.Copy))
                act.activation(mb[:, TP:T + TS], o[:, 0:2 * TS], ACT.Copy).then_inc(out_sem(("mbs", h)), 1)
                wait_taken(act, ("mb", h))
                wait_taken(act, ("mbs", h))
                for j in range(NI):
                    act.activation(sT[:, j, P * j:TP], mb[:, P * j:TP], ACT.Exp, bias=rt[:, j, h:h + 1], scale=-1.0).then_inc(exp_ready, 1)
                if h:
                    act.wait_ge(state_used, (NB - 1) * (h - 1) + 1)
                act.activation(sTs[:, :], mb[0:TS, TP:T], ACT.Exp, bias=rt[0:TS, NI, h:h + 1], scale=-1.0).then_inc(exp_ready, 1)

            def av(h):
                if h:
                    act.wait_ge(small_done, ring_of[("hTs", h - 2)] + 1) if h >= 2 else None
                for i in range(NI):
                    o = take(act, ("h", h, i))
                    act.activation(ht[:, i, :], o[:, 0:DH + 1], ACT.Copy).then_inc(out_sem(("h", h, i)), 1)
                o = take(act, ("C", h))
                if h:
                    act.wait_ge(cout_out, 16 * h)
                act.activation(cout[:, :, :], o.rearrange("p (c k) -> p c k", c=2), ACT.Copy).then_inc(out_sem(("C", h)), 1)
                if h == 0:
                    for q in range(2):
                        act.wait_ge(cstage_out[q], 32 * KT // 2)
                turned(h, 0)

            def turned(h, b):
                u = NB * h + b
                o = take(act, ("ct", h, b))
                if u >= 2:
                    if b >= 2:
                        act.wait_ge(state_used, (NB - 1) * h + b - 1)
                    elif b == 1:
                        act.wait_ge(held_done, h)
                    else:
                        act.wait_ge(state_used, (NB - 1) * h)
                chain.raised_by(act.activation(cT[:, u % 2, :, DH:DH + 1], nT[:, :, NH * b + h:NH * b + h + 1], ACT.Copy))
                act.activation(cT[:, u % 2, :, 0:DH], o.rearrange("p (c k) -> p c k", c=2), ACT.Copy).then_inc(out_sem(("ct", h, b)), 1)

            def state(h, b):
                if b + 1 < NB:
                    turned(h, b + 1)
                if b == NB - 1:
                    act.wait_ge(held_done, h + 1)
                    act.activation(ht[0:TS, NI, :], held[0:TS, 0:DH + 1], ACT.Copy).then_inc(held_out, 1)

            def centred_squares(js):
                for j in js:
                    act.wait_ge(xc_ready, j + 1)
                    if j >= 4:
                        act.wait_ge(sqc_used, j - 3)
                    act.activation(lnt[:, 2 + j % 4, :], upad[:, j, CH:CH + T], ACT.Square).then_inc(sqc_ready, 1)

            def convmean(_):
                centred_squares(range(4))

            def convvar(_):
                centred_squares(range(4, KT))
                for name, (a, b) in (("vara", HALVES[0]), ("varb", HALVES[1])):
                    o = take(act, name)
                    act.activation(lnt[:, 1, a:b], o[:, 0:b - a], ACT.Sqrt, scale=1.0 / D, bias=epsc[:, 0:1]).then_inc(out_sem(name), 1)

            def convapply(_):
                for j in range(KT):
                    act.wait_ge(yln, j + 1)
                    if j >= 2:
                        act.wait_ge(zs, j - 1)
                    act.activation(lnt[:, 4 + j % 2, :], lnt[:, 2 + j % 2, :], ACT.Sigmoid,
                                   bias=vec[:, CLB + j:CLB + j + 1], scale=vec[:, CLG + j:CLG + j + 1]).then_inc(ysig, 1)

            def split(_):
                for name in (("hTs", NH - 1), ("hT", NH - 1, 0), ("hT", NH - 1, 1), ("u", NH - 1, NB - 1), ("n", NH - 1)):
                    wait_taken(act, name)
                wait_taken(act, ("ct", NH - 1, NB - 1))
                act.wait_ge(hab_gated, NH - 1)
                act.wait_ge(uc_ready, KT)
                for q in range(2):
                    act.wait_ge(cnew_out[q], 16 * NB * NH // 2)
                act.wait_ge(cout_out, 16 * NH)
                act.wait_ge(nout_out, 32 * NH)
                for k in range(KT):
                    act.activation(hhi[:, k, :], hab[:, k, :], ACT.Copy).then_inc(hhi_ready, 1)
                act.wait_ge(zs, KT)
                for j in range(KT):
                    act.activation(uhi[:, j, :], upad[:, j, CH:CH + T], ACT.Copy).then_inc(uhi_ready, 1)

            def residual(part):
                for j in RESIDUAL[part]:
                    act.wait_ge(x1_ready, j + 1)
                    if j >= 4:
                        act.wait_ge(sqsum_ready, j - 3)
                    act.activation(sq2[:, j % 4, :], x1[:, j, :], ACT.Square).then_inc(sq_ready, 1)

            def norm2(_):
                for name, (a, b) in (("qa", HALVES[0]), ("qb", HALVES[1])):
                    o = take(act, name)
                    act.activation(mb[:, a:b], o[:, 0:b - a], ACT.Sqrt, scale=1.0 / D, bias=epsc[:, 0:1]).then_inc(out_sem(name), 1)
                for j in range(KT):
                    act.wait_ge(hf_ready, j + 1)
                    act.activation(ahi[:, j, :], sq2[:, j % 4, :], ACT.Copy).then_inc(hfhi, 1)

            def fstate(i):
                o = take(act, ("fs", i))
                if i:
                    act.wait_ge(act_ready, 2 * i)
                    act.wait_ge(flast_ready, i)
                dst = up[:, :, FK - 1 + TP:FK - 1 + TP + NB * FSEG].rearrange("p c (b s) -> p c b s", s=FSEG)
                for c in range(2):
                    t = act.activation(dst[:, c, :, 0:2], o[:, 16 * c:16 * c + 16].rearrange("p (b s) -> p b s", s=2), ACT.Copy)
                    if c == 0:
                        chain.raised_by(t)
                t.then_inc(out_sem(("fs", i)), 1)

            def ftail(i):
                o = take(act, ("ft", i))
                if i >= 2:
                    act.wait_ge(fout_out[i % 2], 64 * (i // 2))
                act.activation(fout[:, i % 2, :], o[0:18, 0:2 * P], ACT.Copy).then_inc(out_sem(("ft", i)), 1)

            def final(_):
                for i in range(NI + 1):
                    n = P if i < NI else TS
                    for q in range(2):
                        o = take(act, ("y", i, q))
                        chain.raised_by(act.activation(yt[0:n, i, 512 * q:512 * q + 512], o[0:n, :], ACT.Copy))
                        if i or q:
                            act.wait_ge(yssq, 2 * i + q)
                        link(act.activation(junk[0:n, :], o[0:n, :], ACT.Square, accum_out=stat[0:n, 16 + 2 * i + q:17 + 2 * i + q]))
                        act.activation(stat[0:n, 31:32], epsc[0:n, 0:1], ACT.Copy).then_inc(yssq, 1)
                        act.wait_ge(yssq, 2 * i + q + 1)
                        act.activation(stat[0:n, 32:33], epsc[0:n, 0:1], ACT.Copy).then_inc(out_sem(("y", i, q)), 1)

            def panel(kind, i):
                n = index_of[(kind, i)]
                if kind == "glu":
                    if i:
                        wait_acc_out(act, index_of[("glu", i - 1)], 1)
                    out_of(n, 0, sg[:, :], ACT.Sigmoid)
                elif kind == "k":
                    if i == 0:
                        for m in range(NI + 1):
                            pass
                        wait_taken(act, "xTs")
                        wait_taken(act, "rts")
                        act.wait_ge(gates_dve, 2)
                        wait_taken(act, ("cst", 1, 1))
                    for c in range(2):
                        out_of(n, c, kT[:, c, :], ACT.Copy, scale=DH ** -0.5)
                elif kind in "vq":
                    for c in range(2):
                        out_of(n, c, vqT[:, c, :], ACT.Copy)
                elif kind == "o":
                    if i == 0:
                        act.wait_ge(small_done, ring_of[("ss", NH - 1)] + 1)
                        act.wait_ge(qm_ready, NH)
                    if i == 2:
                        act.wait_ge(hab_gated, 1)
                    for c in range(2):
                        out_of(n, c, hab[:, 2 * i + c, :] if i == NH - 1 else sga[:, i % 2, c, :], ACT.Sigmoid)
                elif kind == "gate":
                    if i < 2:
                        act.wait_ge(hab_gated, 3 - i)
                    if i >= 2:
                        act.wait_ge(mix_ready, i - 1)
                    for c in range(2):
                        out_of(n, c, sga[:, i % 2, c, :], ACT.Sigmoid)
                elif kind == "branch":
                    for k in {KT - 2: range(KT - 2), KT - 1: range(KT - 2, KT)}.get(i, ()):
                        act.wait_ge(mix_ready, k + 1)
                        wait_panel_used(act, index_of[("gate", KT - 1)])
                        act.activation(ahi[:, k, :], mix[:, k, :], ACT.Copy).then_inc(mhi_ready, 1)
                elif kind == "out":
                    if i == 0:
                        wait_panel_used(act, index_of[("branch", KT - 1)])
                    for c in range(2):
                        p, sm, done = acc_ready(act, n, c)
                        chain.raised_by(act.activation(x1[:, 2 * i + c, TP:T], sm, ACT.Copy))
                        act.activation(x1[:, 2 * i + c, 0:TP].rearrange("p (a t) -> p a t", a=2), p, ACT.Copy).then_inc(done, 1)
                elif kind == "up":
                    for c in range(2):
                        p, s, done = acc_ready(act, n, c)
                        dst = up[:, c, FK - 1 + TP:FK - 1 + TP + NB * FSEG].rearrange("p (b s) -> p b s", s=FSEG)[:, :, 2:FSEG]
                        chain.raised_by(act.activation(dst, s.rearrange("p (b s) -> p b s", s=NS), ACT.Copy))
                        act.activation(up[:, c, FK - 1:FK - 1 + TP].rearrange("p (a t) -> p a t", a=2), p, ACT.Copy).then_inc(done, 1)
                    wait_acc_out(act, n, 0)
                    wait_acc_out(act, n, 1)
                    act.wait_ge(act_chain, chain.n)
                    ends = up[:, :, TP:TP + 9 * FSEG].rearrange("p c (b s) -> p c b s", s=FSEG)[:, :, :, 0:2]
                    if i >= 2:
                        act.wait_ge(small_done, ring_of[("ft", i - 2)] + 1)
                    act.activation(flast[:, i % 2, :, :].rearrange("p c (b s) -> p c b s", s=2), ends, ACT.Copy).then_inc(flast_ready, 1)
                    act.wait_ge(sig_ready, 2 * i + 1)
                    act.activation(usig[:, :], upc[:, 0, :], ACT.Sigmoid).then_inc(sig_ready, 1)
                elif kind == "down":
                    g, s = i
                    for k in range(ktiles(n)):
                        kt = 8 * s + k
                        u = KF * g + kt
                        if u >= 3:
                            wait_down(act, u - 3)
                        if u == 0:
                            act.wait_ge(act_ready, 2 * KF)
                        act.activation(dhi[:, u % 3, :], act_tile(kt), ACT.Copy).then_inc(dhi_ready, 1)
                if n + 2 < len(panels):
                    split_hi(n + 2)

            for s in steps:
                {"setup": setup,
                 "gates": gates_step,
                 "gateturn": gateturn,
                 "tail": tail,
                 "kv": kv,
                 "weights": weights,
                 "scores": skip,
                 "av": av,
                 "state": state,
                 "headnorm": skip,
                 "headout": skip,
                 "convmean": convmean,
                 "convvar": convvar,
                 "convapply": convapply,
                 "split": split,
                 "residual": residual,
                 "norm2": norm2,
                 "fstate": fstate,
                 "ftail": ftail,
                 "final": final,
                 "panel": panel}[s[0]](*s[1:])

        @block.vector
        def _(dve):
            chain = Count(dve_chain)
            tt, stt, ts = dve.tensor_tensor, dve.scalar_tensor_tensor, dve.tensor_scalar

            def link(ins):
                chain.raised_by(ins)
                dve.wait_ge(dve_chain, chain.n)

            def split_lo(n):
                dve.wait_ge(w_hi, n + 1)
                tt(panel_view(wlo, n % 2, n), panel_view(raw, n % NRAW, n), panel_view(whi, n % 2, n).bitcast(F32),
                   ALU.subtract).then_inc(w_lo_dve, 1)

            def setup(_):
                dve.wait_ge(rs_ready, 1)
                for i in range(NI + 1):
                    m = P if i < NI else TS
                    dve.wait_ge(x_in[i], 16)
                    ts(xin[0:m, i, :], xin[0:m, i, :], stat[0:m, 8 + i:9 + i], None, ALU.mult).then_inc(xs_ready, 1)
                for n in range(2):
                    split_lo(n)
                wait_taken(dve, ("vec", 0))
                for k in range(KT):
                    o = take(dve, ("xT", k))
                    dve.wait_ge(xn_hi, k + 1)
                    stt(alo[:, k, 0:TP], o, vec[:, MIXG + k:MIXG + k + 1], ahi[:, k, 0:TP].bitcast(F32),
                        ALU.mult, ALU.subtract).then_inc(out_sem(("xT", k)), 1)
                o = take(dve, "xTs")
                dve.wait_ge(xn_hi, 2 * KT)
                for k in range(KT):
                    t = stt(alo[:, k, TP:T], o[:, TS * k:TS * k + TS], vec[:, MIXG + k:MIXG + k + 1],
                            ahi[:, k, TP:T].bitcast(F32), ALU.mult, ALU.subtract)
                    if k < KT - 1:
                        chain.raised_by(t)
                t.then_inc(out_sem("xTs"), 1)

            def gates_step(_):
                n = index_of[("if", 0)]
                p, s, done = acc_ready(dve, n, 0)
                dve.wait_ge(consts_in[7], 16)
                dve.wait_ge(consts_in[16], 16)
                dve.wait_ge(consts_in[17], 16)
                dve.wait_ge(consts_set, 2)
                dve.wait_ge(ssq_ready, 1)
                G = gates
                zi, zf = G[0:4, 0, :], G[32:36, 0, :]
                for r, b in ((0, 0), (32, 1)):
                    link(ts(G[r:r + 4, 0, 0:TP].rearrange("p (a t) -> p a t", a=2), p[r:r + 4], stat[r:r + 4, 38:39], None, ALU.add))
                    if b == 0:
                        link(ts(G[r:r + 4, 0, TP:T], s[r:r + 4], stat[r:r + 4, 38:39], None, ALU.add))
                    else:
                        ts(G[r:r + 4, 0, TP:T], s[r:r + 4], stat[r:r + 4, 38:39], None, ALU.add).then_inc(done, 1)
                        wait_acc_out(dve, n, 0)
                link(ts(G[32:36, 2, :], zf, -1.0, None, ALU.mult))
                tt(G[32:36, 1, :], zf, G[32:36, 2, :], ALU.min).then_inc(gates_dve, 1)
                dve.wait_ge(gates_act, 1)
                link(stt(G[0:4, 1, :], zf, 0.0, G[32:36, 3, :], ALU.min, ALU.subtract))
                link(dve.tensor_tensor_scan(G[0:4, 2, 0:TP], ones4(), G[0:4, 1, 0:TP], 0.0, ALU.mult, ALU.add))
                sb_ = G[0:4, 2, TP:T].rearrange("p (b t) -> p b t", t=NS)
                lf_ = G[0:4, 1, TP:T].rearrange("p (b t) -> p b t", t=NS)
                link(dve.tensor_copy(sb_[:, :, 0], lf_[:, :, 0]))
                for t in range(1, NS):
                    link(tt(sb_[:, :, t], sb_[:, :, t - 1], lf_[:, :, t], ALU.add))
                link(tt(rows[0:4, :], zi, G[0:4, 2, :], ALU.subtract))
                link(dve.tensor_tensor_scan(mrow[:, 0:TP], ones4(), rows[0:4, 0:TP], 0.0, ALU.mult, ALU.max))
                sm_ = mrow[:, TP:T].rearrange("p (b t) -> p b t", t=NS)
                a_ = rows[0:4, TP:T].rearrange("p (b t) -> p b t", t=NS)
                m0 = stat[0:4, 22:30]
                link(tt(sm_[:, :, 0], m0, a_[:, :, 0], ALU.max))
                for t in range(1, NS):
                    link(tt(sm_[:, :, t], sm_[:, :, t - 1], a_[:, :, t], ALU.max))
                tt(rows[32:36, :], G[0:4, 2, :], mrow[:, 0:T], ALU.add).then_inc(m_out, 1)
                link(ts(G[0:4, 4, 0:TP], rows[0:4, 0:TP], mrow[:, TP - 1:TP], None, ALU.subtract))
                last = sm_[:, :, NS - 1:NS]
                link(tt(G[0:4, 4, TP:T].rearrange("p (b t) -> p b t", t=NS), a_, last.broadcast_to([NH, NB, NS]), ALU.subtract))
                m0b = m0.rearrange("p (b t) -> p b t", t=1)
                link(tt(G[0:4, 5, 0:TS].rearrange("p (b t) -> p b t", t=NS), m0b.broadcast_to([NH, NB, NS]), sm_, ALU.subtract))
                dve.wait_ge(m_out, 1)
                tt(G[0:4, 5, TS:TS + NB], m0, sm_[:, :, NS - 1], ALU.subtract).then_inc(gates_dve, 1)

            def ones4():
                return gates[0:4, 3, 0:TP]

            conv_queue = []

            def conv_block(j):
                u = upad[:, j, :]
                steps_ = []
                seg = u[:, CH + TP:UPW].rearrange("p (b s) -> p b s", s=SEG)

                def window(q):
                    w = seg[:, :, 2 * q:2 * q + 2]
                    ap = [list(x) for x in w.ap]
                    return bass.AP(w.tensor, w.offset, [ap[0], ap[1], [1, 2], [1, CK]])

                steps_.append(lambda: link(ts(cacc[:, 0:TP], u[:, 0:TP], cw[:, j, 0:1], vec[:, CB + j:CB + j + 1], ALU.mult, ALU.add)))
                for q in range(2):
                    steps_.append(lambda q=q: link(tt(prod[:, :, :, :], window(q),
                                                      cw[:, j, :].rearrange("p (b t k) -> p b t k", b=1, t=1).broadcast_to([P, NB, 2, CK]), ALU.mult)))
                    steps_.append(lambda q=q: link(dve.tensor_reduce(cacc[:, TP:T].rearrange("p (b t) -> p b t", t=NS)[:, :, 2 * q:2 * q + 2],
                                                                     prod[:, :, :, :], mybir.AxisListType.X, ALU.add)))
                for k in range(1, CK - 1):
                    steps_.append(lambda k=k: link(stt(cacc[:, 0:TP], u[:, k:k + TP], cw[:, j, k:k + 1], cacc[:, 0:TP], ALU.mult, ALU.add)))

                def last():
                    dve.wait_ge(small_done, ring_of[("ut", j)] + 1)
                    link(stt(u[:, CH:CH + TP], u[:, CH:CH + TP], cw[:, j, CH:CH + 1], cacc[:, 0:TP], ALU.mult, ALU.add))
                    ts(u[:, CH + TP:CH + T], cacc[:, TP:T], vec[:, CB + j:CB + j + 1], None, ALU.add).then_inc(uc_ready, 1)
                    dve.wait_ge(uc_ready, j + 1)
                steps_.append(last)
                return steps_

            def conv(n):
                for _ in range(min(n, len(conv_queue))):
                    conv_queue.pop(0)()

            def kv(h):
                dve.wait_ge(rt_ready, 1)
                wait_taken(dve, "rt")
                for q in range(3):
                    o = take(dve, ("kt", h, q))
                    if q < 2:
                        chain.raised_by(ts(gk[:, 2 * q, :], o[:, 0:DH], rt[:, 2 * q, 64 + h:65 + h], None, ALU.mult))
                        ts(gk[:, 2 * q + 1, :], o[:, DH:2 * DH], rt[:, 2 * q + 1, 64 + h:65 + h], None, ALU.mult).then_inc(out_sem(("kt", h, q)), 1)
                    else:
                        ts(gks[:, h % 2, :], o[0:TS, 0:DH], rt[0:TS, NI, 64 + h:65 + h], None, ALU.mult).then_inc(out_sem(("kt", h, q)), 1)

            def scores(h):
                for j in range(NI + 1):
                    dve.wait_ge(exp_ready, (NI + 1) * h + j + 1)
                    name = ("s", h, j) if j < NI else ("ss", h)
                    o = take(dve, name)
                    if j < NI:
                        tt(sT[:, j, P * j:TP], sT[:, j, P * j:TP], o[:, P * j:TP], ALU.mult).then_inc(out_sem(name), 1)
                    else:
                        tt(sTs[:, :], sTs[:, :], o[0:TS, 0:TS], ALU.mult).then_inc(out_sem(name), 1)
                wait_taken(dve, ("mbs", h))
                if h:
                    dve.wait_ge(held_done, h)
                else:
                    dve.wait_ge(consts_set, 3)
                for c in range(2):
                    dst = qm[:, c, :].rearrange("p (b s) -> p b s", s=36)[:, :, 0:NS]
                    t = tt(dst, vqT[:, c, TP:T].rearrange("p (b t) -> p b t", t=NS), mb[:, T:T + TS].rearrange("p (b t) -> p b t", t=NS), ALU.mult)
                    if c == 0:
                        chain.raised_by(t)
                t.then_inc(qm_ready, 1)

            def av(h):
                o = take(dve, ("n", h))
                if h:
                    dve.wait_ge(nout_out, 32 * h)
                wait_taken(dve, "rts")
                dve.wait_ge(consts_in[18], 16 * (h + 1))
                chain.raised_by(dve.tensor_copy(nout[0:1, 0, :], o[0:1, 0:DH]))
                nready = stt(nout[:, 1, :], nh[:, :], gib[:, h:h + 1], o[0:NB, DH:2 * DH], ALU.mult, ALU.add)
                nready.then_inc(out_sem(("n", h)), 1)
                wait_taken(dve, ("kt", h, 2))

                mask(h, 0)

            def mask(h, b):
                u = NB * h + b
                if u >= 2:
                    v = u - 2
                    dve.wait_ge(small_done, ring_of[("u", v // NB, v % NB)] + 1)
                ts(km[:, u % 2, :], gks[:, h % 2, :], bmask[:, b:b + 1], None, ALU.mult).then_inc(km_ready, 1)

            def state(h, b):
                u = NB * h + b
                if b + 1 < NB:
                    mask(h, b + 1)
                o = take(dve, ("u", h, b))
                if u >= 2:
                    dve.wait_ge(cnew_out[u % 2], 16 * (u // 2))
                dve.wait_ge(cin_in[u % 2], 16 * (u // 2 + 1))
                stt(cnew[:, u % 2, :, :], cin[:, u % 2, :, :], gic[:, h % 2, b:b + 1],
                    o.rearrange("p (c k) -> p c k", c=2), ALU.mult, ALU.add).then_inc(out_sem(("u", h, b)), 1)
                conv(2)

            def headnorm(h):
                dve.wait_ge(em_ready, 1)
                for i in range(NI):
                    wait_taken(dve, ("h", h, i))
                dve.wait_ge(held_out, h + 1)
                for i in range(NI + 1):
                    n = P if i < NI else TS
                    chain.raised_by(stt(stat[0:n, i:i + 1], ht[0:n, i, DH:DH + 1], -1.0, ht[0:n, i, DH:DH + 1], ALU.mult, ALU.max))
                    chain.raised_by(dve.bn_stats(bst[0:n, i, :], ht[0:n, i, 0:DH]))
                dve.wait_ge(dve_chain, chain.n)
                for i in range(NI + 1):
                    n = P if i < NI else TS
                    chain.raised_by(dve.bn_aggr(stat[0:n, 12 + 2 * i:14 + 2 * i], bst[0:n, i, :]))
                link(tt(stat[:, 0:5], stat[:, 0:5], em[:, :, h], ALU.max))
                link(dve.reciprocal(stat[:, 0:5], stat[:, 0:5]))
                var = stat[:, 12:22].rearrange("p (i q) -> p i q", q=2)[:, :, 1]
                link(tt(stat[:, 5:10], stat[:, 0:5], stat[:, 0:5], ALU.mult))
                link(tt(stat[:, 5:10], stat[:, 5:10], var, ALU.mult))
                ts(stat[:, 5:10], stat[:, 5:10], EPS, None, ALU.add).then_inc(hv_ready, 1)
                conv(3)
                dve.wait_ge(hr_ready, h + 1)
                link(tt(stat[:, 0:5], stat[:, 0:5], stat[:, 5:10], ALU.mult))
                for i in range(NI + 1):
                    n = P if i < NI else TS
                    t = ts(ht[0:n, i, 0:DH], ht[0:n, i, 0:DH], stat[0:n, 12 + 2 * i:13 + 2 * i], stat[0:n, i:i + 1], ALU.subtract, ALU.mult)
                    if i < NI:
                        chain.raised_by(t)
                dve.wait_ge(dve_chain, chain.n)
                t.then_inc(hn_ready, 1)

            def headout(h):
                last_head = h == NH - 1
                if last_head:
                    wait_acc_out(dve, index_of[("o", h)], 0)
                    wait_acc_out(dve, index_of[("o", h)], 1)

                def gained(dst, src, k, name):
                    gain = vec[:, HEADG + k:HEADG + k + 1]
                    if last_head:
                        return stt(dst, src, gain, dst, ALU.mult, ALU.mult)
                    return ts(dst, src, gain, None, ALU.mult)

                for c in range(2):
                    k = 2 * h + c
                    o = take(dve, ("hT", h, c))
                    gained(hab[:, k, 0:TP], o, k, None).then_inc(out_sem(("hT", h, c)), 1)
                o = take(dve, ("hTs", h))
                for c in range(2):
                    k = 2 * h + c
                    t = gained(hab[:, k, TP:T], o[:, TS * c:TS * c + TS], k, None)
                    if c == 0:
                        chain.raised_by(t)
                t.then_inc(out_sem(("hTs", h)), 1)
                conv(5)

            def convmean(_):
                conv(len(conv_queue))
                dve.wait_ge(dve_chain, chain.n)
                for name, (a, b) in (("mua", HALVES[0]), ("mub", HALVES[1])):
                    o = take(dve, name)
                    if name == "mua":
                        wait_taken(dve, ("n", NH - 1))
                        dve.wait_ge(small_done, ring_of[("n", NH - 1)] + 1)
                    ts(lnt[:, 0, a:b], o[:, 0:b - a], 1.0 / D, None, ALU.mult).then_inc(out_sem(name), 1)
                wait_taken(dve, "mua")
                wait_taken(dve, "mub")
                for j in range(KT):
                    tt(upad[:, j, CH:CH + T], upad[:, j, CH:CH + T], lnt[:, 0, :], ALU.subtract).then_inc(xc_ready, 1)

            def convapply(_):
                wait_taken(dve, "vara")
                wait_taken(dve, "varb")
                dve.reciprocal(lnt[:, 1, :], lnt[:, 1, :]).then_inc(lnstd, 1)
                dve.wait_ge(lnstd, 1)
                dve.wait_ge(xc_ready, KT)
                dve.wait_ge(sqc_ready, KT)

                def normed(j):
                    if j >= 2:
                        dve.wait_ge(ysig, j - 1)
                    tt(lnt[:, 2 + j % 2, :], upad[:, j, CH:CH + T], lnt[:, 1, :], ALU.mult).then_inc(yln, 1)

                normed(0)
                for j in range(KT):
                    dve.wait_ge(yln, j + 1)
                    link(ts(upad[:, j, CH:CH + T], lnt[:, 2 + j % 2, :], vec[:, CLG + j:CLG + j + 1], vec[:, CLB + j:CLB + j + 1], ALU.mult, ALU.add))
                    if j + 1 < KT:
                        normed(j + 1)
                    dve.wait_ge(ysig, j + 1)
                    tt(upad[:, j, CH:CH + T], upad[:, j, CH:CH + T], lnt[:, 4 + j % 2, :], ALU.mult).then_inc(zs, 1)

            def split(_):
                for k in range(KT):
                    dve.wait_ge(hhi_ready, k + 1)
                    tt(hlo[:, k, :], hab[:, k, :], hhi[:, k, :].bitcast(F32), ALU.subtract).then_inc(hlo_ready, 1)
                for j in range(KT):
                    dve.wait_ge(uhi_ready, j + 1)
                    tt(ulo[:, j, CH:CH + T], upad[:, j, CH:CH + T], uhi[:, j, :].bitcast(F32), ALU.subtract).then_inc(ulo_ready, 1)

            def residual(part):
                if part == 0:
                    o = take(dve, "xrs")
                    ts(xrs[:, :], o[:, 0:KT * TS], 1.0, None, ALU.mult).then_inc(out_sem("xrs"), 1)
                    wait_taken(dve, "xrs")
                for k in RESIDUAL[part]:
                    o = take(dve, ("xr", k))
                    wait_acc_out(dve, index_of[("out", k // 2)], k % 2)
                    link(tt(x1[:, k, TP:T], x1[:, k, TP:T], xrs[:, TS * k:TS * k + TS], ALU.add))
                    tt(x1[:, k, 0:TP], x1[:, k, 0:TP], o, ALU.add).then_inc(out_sem(("xr", k)), 1)
                    wait_taken(dve, ("xr", k))
                    dve.tensor_copy(stat[:, 39:40], stat[:, 38:39]).then_inc(x1_ready, 1)
                    if k:
                        add_square(k - 1)

            def add_square(k):
                dve.wait_ge(sq_ready, k + 1)
                if k == 0:
                    dve.tensor_copy(sqsum[:, :], sq2[:, 0, :]).then_inc(sqsum_ready, 1)
                else:
                    dve.wait_ge(sqsum_ready, k)
                    tt(sqsum[:, :], sqsum[:, :], sq2[:, k % 4, :], ALU.add).then_inc(sqsum_ready, 1)

            def norm2(_):
                add_square(KT - 1)
                wait_taken(dve, "qa")
                wait_taken(dve, "qb")
                dve.reciprocal(mb[:, 0:T], mb[:, 0:T]).then_inc(std2, 1)
                dve.wait_ge(std2, 1)
                dve.wait_ge(sq_ready, KT)
                for j in range(KT):
                    if j >= 4:
                        dve.wait_ge(hflo, j - 3)
                    stt(sq2[:, j % 4, :], x1[:, j, :], vec[:, FG + j:FG + j + 1], mb[:, 0:T], ALU.mult, ALU.mult).then_inc(hf_ready, 1)
                    if j:
                        lo2(j - 1)
                lo2(KT - 1)

            def lo2(j):
                dve.wait_ge(hfhi, j + 1)
                tt(alo[:, j, :], sq2[:, j % 4, :], ahi[:, j, :].bitcast(F32), ALU.subtract).then_inc(hflo, 1)

            def panel(kind, i):
                n = index_of[(kind, i)]
                conv(BEFORE.get(kind, 0))
                if kind == "glu":
                    if i == 0:
                        wait_taken(dve, ("cst", 1, 1))
                        wait_taken(dve, ("cst", 1, 0))
                        dve.wait_ge(consts_set, 2)
                    p, s, done = acc_ready(dve, n, 1)
                    wait_acc_out(dve, n, 0)
                    new = upad[:, i, CH + TP:UPW].rearrange("p (b s) -> p b s", s=SEG)[:, :, CH:SEG]
                    chain.raised_by(tt(new, s.rearrange("p (b t) -> p b t", t=NS), sg[:, TP:T].rearrange("p (b t) -> p b t", t=NS), ALU.mult))
                    tt(upad[:, i, CH:CH + TP].rearrange("p (a t) -> p a t", a=2), p, sg[:, 0:TP].rearrange("p (a t) -> p a t", a=2), ALU.mult).then_inc(done, 1)
                    wait_acc_out(dve, n, 1)
                    dve.wait_ge(dve_chain, chain.n)
                    if i >= 2:
                        dve.wait_ge(small_done, ring_of[("ut", i - 2)] + 1)
                    dve.tensor_copy(unew[:, i % 2, :].rearrange("p (b t) -> p b t", t=NS), new).then_inc(unew_ready, 1)
                    if i == 0:
                        wait_taken(dve, "cw")
                    conv_queue.extend(conv_block(i))
                elif kind == "branch":
                    if i == 0:
                        dve.wait_ge(ysig, KT)
                        dve.wait_ge(zs, KT)
                    for c in range(2):
                        p, s, done = acc_ready(dve, n, c)
                        wait_acc_out(dve, index_of[("gate", i)], c)
                        g = sga[:, i % 2, c, :]
                        chain.raised_by(tt(g[:, TP:T], s, g[:, TP:T], ALU.mult))
                        tt(g[:, 0:TP].rearrange("p (a t) -> p a t", a=2), p, g[:, 0:TP].rearrange("p (a t) -> p a t", a=2), ALU.mult).then_inc(done, 1)
                    wait_acc_out(dve, n, 0)
                    wait_acc_out(dve, n, 1)
                    dve.wait_ge(dve_chain, chain.n)
                    tt(mix[:, i, :], sga[:, i % 2, 0, :], sga[:, i % 2, 1, :], ALU.add).then_inc(mix_ready, 1)
                    if i >= KT - 2:
                        wait_panel_used(dve, index_of[("gate", KT - 1)])
                        for k in range(KT - 2) if i == KT - 2 else range(KT - 2, KT):
                            dve.wait_ge(mix_ready, k + 1)
                            dve.wait_ge(mhi_ready, k + 1)
                            tt(alo[:, k, :], mix[:, k, :], ahi[:, k, :].bitcast(F32), ALU.subtract).then_inc(mlo_ready, 1)
                elif kind == "o" and i < NH - 1:
                    if i == 0:
                        wait_taken(dve, ("hTs", NH - 2))
                    for c in range(2):
                        wait_acc_out(dve, n, c)
                        wait_acc_out(dve, n, 0)
                        k = 2 * i + c
                        t = tt(hab[:, k, :], hab[:, k, :], sga[:, i % 2, c, :], ALU.mult)
                        if c == 0:
                            chain.raised_by(t)
                    t.then_inc(hab_gated, 1)
                elif kind == "down":
                    down_lo(n)
                    if i[1] == 2:
                        for c in range(2):
                            k = 2 * i[0] + c
                            p, s, done = acc_ready(dve, n, c)
                            chain.raised_by(tt(x1[:, k, TP:T], s, x1[:, k, TP:T], ALU.add))
                            tt(x1[:, k, 0:TP].rearrange("p (a t) -> p a t", a=2), p, x1[:, k, 0:TP].rearrange("p (a t) -> p a t", a=2), ALU.add).then_inc(done, 1)
                elif kind == "up":
                    wait_taken(dve, ("fs", i))
                    wait_acc_out(dve, n, 0)
                    wait_acc_out(dve, n, 1)
                    for c in range(2):
                        k = KF * c + i
                        if i == 0 and c == 0:
                            dve.wait_ge(consts_set, 4)
                            wait_taken(dve, ("vec", 1))
                            wait_taken(dve, ("vec", 2))
                        link(ts(upc[:, c, :], up[:, c, 0:FOUT], fcw[:, 0, k:k + 1], vec[:, FB + k:FB + k + 1], ALU.mult, ALU.add))
                        link(stt(upc[:, c, :], up[:, c, 1:1 + FOUT], fcw[:, 1, k:k + 1], upc[:, c, :], ALU.mult, ALU.add))
                        t = stt(upc[:, c, :], up[:, c, 2:2 + FOUT], fcw[:, 2, k:k + 1], upc[:, c, :], ALU.mult, ALU.add)
                        if c == 0:
                            t.then_inc(sig_ready, 1)
                        else:
                            link(t)
                    dve.wait_ge(sig_ready, 2 * i + 2)
                    link(tt(usig[:, :], usig[:, :], upc[:, 0, :], ALU.mult))
                    dst = act_tile(i)
                    tt(dst[:, 0:TP], usig[:, 0:TP], upc[:, 1, 0:TP], ALU.mult).then_inc(act_ready, 1)

                    def cut(x):
                        return x[:, TP:TP + NB * FSEG].rearrange("p (b s) -> p b s", s=FSEG)[:, :, 2:FSEG]
                    tt(dst[:, TP:T].rearrange("p (b t) -> p b t", t=NS), cut(usig), cut(upc[:, 1, :]), ALU.mult).then_inc(act_ready, 1)
                    dve.wait_ge(act_ready, 2 * i + 2)
                if n + 2 < len(panels) and not on_pool(n + 2):
                    split_lo(n + 2)
                conv(BEHIND.get(kind, 0))

            def down_lo(n):
                g, s = panels[n][1]
                for k in range(ktiles(n)):
                    kt = 8 * s + k
                    u = KF * g + kt
                    if u >= 3:
                        wait_down(dve, u - 3)
                    dve.wait_ge(dhi_ready, u + 1)
                    tt(dlo[:, u % 3, :], act_tile(kt), dhi[:, u % 3, :].bitcast(F32), ALU.subtract).then_inc(dlo_ready, 1)

            def final(_):
                dve.wait_ge(fg_in, 16)
                dve.wait_ge(yrs, 1)
                for q in range(2 * (NI + 1)):
                    wait_taken(dve, ("y", q // 2, q % 2))
                for i in range(NI + 1):
                    n = P if i < NI else TS
                    stt(yt[0:n, i, :], yt[0:n, i, :], stat[0:n, 8 + i:9 + i], fgb[0:n, :], ALU.mult, ALU.mult).then_inc(y_ready, 1)

            for s in steps:
                {"setup": setup,
                 "gates": gates_step,
                 "gateturn": skip,
                 "tail": skip,
                 "kv": kv,
                 "weights": skip,
                 "scores": scores,
                 "av": av,
                 "state": state,
                 "headnorm": headnorm,
                 "headout": headout,
                 "convmean": convmean,
                 "convvar": skip,
                 "convapply": convapply,
                 "split": split,
                 "residual": residual,
                 "norm2": norm2,
                 "fstate": skip,
                 "ftail": skip,
                 "final": final,
                 "panel": panel}[s[0]](*s[1:])

        @block.gpsimd
        def _(pool):
            chain = Count(pool_chain)

            def link(ins):
                chain.raised_by(ins)
                pool.wait_ge(pool_chain, chain.n)

            def column_rows(v, n):
                return v[0].rearrange("(r c) -> r c", c=P)

            def setup(_):
                pool.memset(raw[:, 0, 0:KT * P], 0.0).then_inc(raw_zeroed, 1)
                link(pool.memset(ident[:, :], 0.0))
                link(pool.affine_select(out=ident[:, :], in_=ident[:, :], compare_op=ALU.not_equal, fill=1.0,
                                        base=0, pattern=[[-1, P]], channel_multiplier=1))
                link(pool.memset(epsc[:, 0:1], EPS))
                link(pool.memset(epsc[:, 1:2], -0.5))
                link(pool.memset(stat[:, :], 1.0))
                pool.memset(ones[:, :], 1.0).then_inc(consts_set, 1)
                pool.wait_ge(consts_set, 1)
                pool.dma_start(stat[0:4, 38:39], b_if[0, 0:NH].rearrange("(a b) -> a b", b=1)).then_inc(consts_in[7], 16)
                pool.dma_start(stat[32:36, 38:39], b_if[0, NH:2 * NH].rearrange("(a b) -> a b", b=1)).then_inc(consts_in[16], 16)
                pool.wait_ge(ssq_ready, 1)
                link(pool.tensor_scalar(stat[:, 8:13], stat[:, 0:5], 1.0 / D, EPS, ALU.mult, ALU.add))
                pool.tensor_tensor(stat[:, 8:13], stat[:, 8:13], epsc[:, 1:2].broadcast_to([P, 5]), ALU.pow).then_inc(rs_ready, 1)
                pool.dma_start(stat[0:4, 22:30], state_m[0].rearrange("b h -> h b"), allow_slow_non_contiguous=True).then_inc(consts_in[17], 16)
                link(pool.memset(sel[:, :, :], 0.0))
                link(pool.affine_select(out=sel[:, :, :], in_=sel[:, :, :], compare_op=ALU.not_equal, fill=1.0,
                                        base=0, pattern=[[-1, NH], [0, P]], channel_multiplier=1))
                link(pool.memset(bmask[:, :], 1.0))
                link(pool.affine_select(out=bmask[:, :], in_=bmask[:, :], compare_op=ALU.is_ge, fill=0.0,
                                        base=0, pattern=[[-NS, NB]], channel_multiplier=1))
                link(pool.affine_select(out=bmask[:, :], in_=bmask[:, :], compare_op=ALU.is_ge, fill=0.0,
                                        base=NS - 1, pattern=[[NS, NB]], channel_multiplier=-1))
                link(pool.memset(rows[:, :], 0.0))
                link(pool.memset(rt[:, NI, :], 0.0))
                link(pool.memset(gates[0:4, 3, :], 1.0))
                pool.memset(upad[:, :, 0:CH], 0.0).then_inc(consts_set, 1)
                pool.wait_ge(consts_set, 2)

            def kv(h):
                if h == 0:
                    wait_taken(pool, "xTs")
                    wait_taken(pool, ("cst", 1, 1))
                    wait_taken(pool, ("cst", 1, 0))
                    pool.wait_ge(gates_dve, 2)
                    pool.wait_ge(rows_ready, 1)
                    wait_taken(pool, "rts")
                    link(pool.memset(vk[:, :, DH:DH + 1], 1.0))
                    link(pool.memset(vks[:, :, DH:DH + 1], 1.0))
                    pool.memset(qm[:, :, :], 0.0).then_inc(consts_set, 1)

            def scores(h):
                for j in range(NI):
                    wait_taken(pool, ("s", h, j))
                    blk = sT[:, j, P * j:P * j + P]
                    pool.affine_select(out=blk, in_=blk, compare_op=ALU.is_ge, fill=0.0, base=0,
                                       pattern=[[1, P]], channel_multiplier=-1).then_inc(st_masked, 1)
                wait_taken(pool, ("ss", h))
                v = sTs[:, :].rearrange("p (b t) -> p b t", t=NS)
                pool.affine_select(out=v, in_=v, compare_op=ALU.is_ge, fill=0.0, base=0,
                                   pattern=[[NS, NB], [1, NS]], channel_multiplier=-1).then_inc(st_masked, 1)
                pool.wait_ge(st_masked, (NI + 2) * h + NI + 1)
                pool.affine_select(out=v, in_=v, compare_op=ALU.is_ge, fill=0.0, base=0,
                                   pattern=[[-NS, NB], [0, NS]], channel_multiplier=1).then_inc(st_masked, 1)

            def headnorm(h):
                pool.wait_ge(hv_ready, h + 1)
                pool.tensor_tensor(stat[:, 5:10], stat[:, 5:10], epsc[:, 1:2].broadcast_to([P, 5]), ALU.pow).then_inc(hr_ready, 1)

            def panel(kind, i):
                n = index_of[(kind, i)] + 2
                if n < len(panels) and on_pool(n):
                    pool.wait_ge(w_hi, n + 1)
                    pool.tensor_tensor(panel_view(wlo, n % 2, n), panel_view(raw, n % NRAW, n),
                                       panel_view(whi, n % 2, n).bitcast(F32), ALU.subtract).then_inc(w_lo_pool, 1)

            def norm2(_):
                wait_panel_used(pool, index_of[("out", 3)])
                link(pool.memset(up[:, :, 0:FK - 1], 0.0))
                pool.memset(up[:, :, FPW - 4:FPW], 0.0).then_inc(consts_set, 1)

            def final(_):
                for i in range(NI + 1):
                    wait_taken(pool, ("y", i, 1))
                wait_taken(pool, ("y", NI, 0))
                pair = stat[:, 16:26].rearrange("p (i q) -> p i q", q=2)
                link(pool.tensor_tensor(stat[:, 8:13], pair[:, :, 0], pair[:, :, 1], ALU.add))
                link(pool.tensor_scalar(stat[:, 8:13], stat[:, 8:13], 1.0 / D, EPS, ALU.mult, ALU.add))
                pool.tensor_tensor(stat[:, 8:13], stat[:, 8:13], epsc[:, 1:2].broadcast_to([P, 5]), ALU.pow).then_inc(yrs, 1)

            for s in steps:
                {"setup": setup,
                 "gates": skip,
                 "gateturn": skip,
                 "tail": skip,
                 "kv": kv,
                 "weights": skip,
                 "scores": scores,
                 "av": skip,
                 "state": skip,
                 "headnorm": headnorm,
                 "headout": skip,
                 "convmean": skip,
                 "convvar": skip,
                 "convapply": skip,
                 "split": skip,
                 "residual": skip,
                 "norm2": norm2,
                 "fstate": skip,
                 "ftail": skip,
                 "final": final,
                 "panel": panel}[s[0]](*s[1:])


_INS = ['x_prompt', 'x_sample', 'state_C', 'state_n', 'state_m', 'state_conv', 'state_ffn', 'mix_norm_g',
        'w_in', 'b_if', 'head_norm_g', 'w_mlstm_out', 'conv_w', 'conv_b', 'conv_ln_g', 'conv_ln_b',
        'w_conv_out', 'w_out', 'ffn_norm_g', 'w_up', 'ffn_conv_w', 'ffn_conv_b', 'w_down', 'final_norm_g']
_OUTS = [(1, TP, D), (NB, NS, D), (1, 1, NH, DH, DH), (1, 1, NH, DH), (1, 1, NH), (1, 1, CH, D),
         (1, 1, FK - 1, 2 * DFF), (1, NB, NH, DH, DH), (1, NB, NH, DH), (1, NB, NH), (1, NB, CH, D),
         (1, NB, FK - 1, 2 * DFF)]


def kernel(**inputs):
    import numpy as _np
    import concourse.bacc as _bacc
    from concourse import mybir as _mybir
    from concourse.bass_utils import run_bass_kernel_spmd as _run

    nc = _bacc.Bacc("TRN2", target_bir_lowering=False, num_devices=1)
    arrays, args = {}, []
    for name in _INS:
        a = _np.ascontiguousarray(inputs[name])
        arrays[f"in_{name}"] = a
        args.append(nc.dram_tensor(f"in_{name}", a.shape, _mybir.dt.from_np(a.dtype), kind="ExternalInput").ap())
    for i, shape in enumerate(_OUTS):
        args.append(nc.dram_tensor(f"out_{i}", shape, _mybir.dt.float32, kind="ExternalOutput").ap())
    build(nc, *args)
    r = _run(nc, [arrays], core_ids=[0])
    return tuple(r.results[0][f"out_{i}"] for i in range(len(_OUTS)))
```

```python
from contextlib import ExitStack

import concourse.bass as bass
from concourse import mybir

F32 = mybir.dt.float32
F32R = mybir.dt.float32r
ALU = mybir.AluOpType
ACT = mybir.ActivationFunctionType

P = 128
D = 1024
KT = D // P
TP = 512
NB, NS = 8, 4
TS = NB * NS
T = TP + TS
HALVES = ((0, 256), (256, T))
NH, DH = 4, 256
NI = TP // P
CK = 31
CH = CK - 1
SEG = CH + NS
DFF = 2816
KF = DFF // P
FK = 3
FSEG = FK - 1 + NS
UPW = CH + TP + NB * SEG
FPW = FK - 1 + TP + NB * FSEG + 4
RESIDUAL = (range(0, 2), range(2, 5), range(5, KT))
BEFORE = {"glu": 6, "v": 7, "q": 7}
BEHIND = {"glu": 7, "v": 5, "q": 5}
CONV_PARTS = CK + 4
SPLIT_IN = {("o", 0): (NH - 1, 1), ("o", 1): (NH - 1, 3), ("o", 2): (NH - 1, 5)}
SPLIT_IN.update({("v", h): (h - 1, 3) for h in range(1, NH)})
SPLIT_IN.update({("q", h): (h - 1, 7) for h in range(1, NH)})
APPLY = (range(0, 4), range(4, KT))
TURNOUT = (range(0, 2), range(2, 4), range(4, NI + 1))
PRE = 2
FOUT = TP + NB * FSEG
EPS = 1e-6
NRAW = 3
RING = 3
COLS = 256


class Count:

    def __init__(self, sem):
        self.sem, self.n = sem, 0

    def raised_by(self, ins):
        ins.then_inc(self.sem, 1)
        self.n += 1


def plan():
    steps = [("setup", 0), ("panel", "if", 0), ("constants", 0)]
    for j in range(KT):
        steps.append(("panel", "glu", j))
        if j == 0:
            steps += [("constants", 1), ("gates", 0)]
        if j == 1:
            steps.append(("gates", 1))
        if j == 2:
            steps.append(("gateturn", 0))
        if j:
            steps.append(("tail", j - 1))
    for h in range(NH):
        steps.append(("panel", "k", h))
        if h == 0:
            steps.append(("tail", KT - 1))
        if h >= 2:
            steps.append(("headout", h - 2))
        if h:
            steps.append(("av", h - 1))
        steps.append(("panel", "v", h))
        if h:
            steps += [("state", h - 1, b) for b in (0, 1, 2)]
        steps += [("kv", h), ("weights", h)]
        if h:
            steps.append(("state", h - 1, 3))
        steps.append(("panel", "q", h))
        if h:
            steps += [("state", h - 1, b) for b in (4, 5, 6, 7)]
        steps.append(("scores", h))
        if h:
            steps.append(("headnorm", h - 1))
    last = NH - 1
    steps += [("panel", "o", last), ("headout", last - 1), ("av", last),
              ("panel", "o", 0), ("state", last, 0), ("state", last, 1), ("convmean", 0),
              ("panel", "o", 1), ("state", last, 2), ("state", last, 3), ("convvar", 0), ("convapply", 0),
              ("panel", "o", 2), ("state", last, 4), ("state", last, 5), ("state", last, 6), ("state", last, 7),
              ("convapply", 1), ("headnorm", last), ("panel", "gate", 0), ("headout", last), ("split", 0),
              ("panel", "gate", 1)]
    for i in range(KT):
        steps.append(("panel", "branch", i))
        if i + 2 < KT:
            steps.append(("panel", "gate", i + 2))
    steps += [("panel", "out", 0), ("panel", "out", 1), ("residual", 0), ("panel", "out", 2), ("residual", 1),
              ("panel", "out", 3), ("residual", 2), ("norm2", 0)]
    for i in range(KF):
        steps += [("fstate", i), ("panel", "up", i)]
        if i:
            steps.append(("ftail", i - 1))
    for g in range(4):
        for q in range(3):
            steps.append(("panel", "down", (g, q)))
            if (g, q) == (0, 0):
                steps.append(("ftail", KF - 1))
            if g == 2:
                steps.append(("turnout", q))
    steps.append(("final", 0))
    return steps


def build(nc, x_prompt, x_sample, state_C, state_n, state_m, state_conv, state_ffn, mix_norm_g,
          w_in, b_if, head_norm_g, w_mlstm_out, conv_w, conv_b, conv_ln_g, conv_ln_b, w_conv_out,
          w_out, ffn_norm_g, w_up, ffn_conv_w, ffn_conv_b, w_down, final_norm_g,
          y_prompt, y_sample, C_prompt, n_prompt, m_prompt, conv_prompt, ffn_prompt,
          C_sample, n_sample, m_sample, conv_sample, ffn_sample):
    ctx = ExitStack()
    steps = plan()

    at = [16512]

    def sb(name, shape, dt=F32, offset=None):
        size = 4
        for n in shape[1:]:
            size *= n
        if offset is None:
            offset = at[0]
            at[0] += (size + 31) // 32 * 32
        assert offset + size <= nc.sbuf_usable_end, (name, offset + size)
        return nc.alloc_sbuf_tensor_at(name, shape, dt, offset=offset)

    def after(offset, *shape):
        size = 4
        for n in shape:
            size *= n
        return offset + (size + 31) // 32 * 32

    raw = sb("raw", [P, NRAW, KT * COLS])
    whi = sb("whi", [P, 2, KT * COLS], F32R)
    wlo = sb("wlo", [P, 2, KT * COLS], F32R)
    ahi_at = at[0]
    ahi = sb("ahi", [P, KT, T], F32R)
    alo = sb("alo", [P, KT, T], F32R)
    ident = sb("ident", [P, P])
    ones = sb("ones", [P, P])
    vec = sb("vec", [P, 92])
    fcw = sb("fcw", [P, FK, KF * 2])
    cw = sb("cw", [P, KT, CK])
    stat = sb("stat", [P, 40])
    epsc = sb("epsc", [P, 2])
    sel = sb("sel", [NH, NH, P])
    bmask = sb("bmask", [TS, NB])
    bm3 = sb("bm3", [3 * TS, NB], F32R)
    rows = sb("rows", [P, T])
    mrow = sb("mrow", [NH, T + TS + NB])
    rt = sb("rt", [P, NI + 1, 4 * NH])
    em = sb("em", [P, NI + 1, NH])
    bst = sb("bst", [P, NI + 1, 6])
    gib = sb("gib", [NB, NH])
    mb = sb("mb", [P, T + TS + NB])

    MIXG, HEADG, CB, CLG, CLB, FG, FB = 0, 8, 16, 24, 32, 40, 48

    arena = at[0]
    upad = sb("upad", [P, KT, UPW])
    ulo = sb("ulo", [P, KT, UPW], F32R, offset=arena)
    hab_at = at[0]
    hab = sb("hab", [P, KT, T])
    hlo = sb("hlo", [P, KT, T], F32R, offset=hab_at)
    x1 = sb("x1", [P, KT, T], offset=hab_at)
    work = at[0]
    kT = sb("kT", [P, 2, T])
    vqT = sb("vqT", [P, 2, T])
    gk = sb("gk", [P, NI, DH])
    vk = sb("vk", [P, NI, DH + 1])
    sT = sb("sT", [P, NI, TP])
    gks3 = sb("gks3", [3 * TS, 2, DH], F32R)
    vks3 = sb("vks3", [3 * TS, 2, DH], F32R)
    gsum = sb("gsum", [P, DH])
    vks = sb("vks", [TS, 2, DH + 1])
    sTs = sb("sTs", [TS, TS])
    gic = sb("gic", [P, 2, NB])
    ht = sb("ht", [P, NI + 1, DH + 1])
    cin = sb("cin", [P, 2, 2, DH])
    cT_at = at[0]
    cT = sb("cT", [P, 2, 2, DH + 1])
    cnew_at = at[0]
    cnew = sb("cnew", [P, 2, 2, DH])
    qm = sb("qm", [P, 2, 36 * NB])
    km_at = at[0]
    km = sb("km", [3 * TS, 2, DH], F32R)
    nout = nc.alloc_sbuf_tensor_at("nout", [P, 2, DH], F32, offset=km_at)[96:96 + NB]
    nT = sb("nT", [P, 2, TS])
    nh = sb("nh", [NB, DH])
    cout = sb("cout", [P, 2, DH])
    cacc_at = at[0]
    cacc = sb("cacc", [P, T])
    prod_at = at[0]
    prod = sb("prod", [P, NB, 2, CK])
    usum = sb("usum", [P, T])
    sg = sb("sg", [P, T], offset=cnew_at)
    cstage = sb("cstage", [TS, 2, 2 * P], offset=cT_at)
    unew = sb("unew", [P, 2, TS])
    xsg = sb("xsg", [P, KT, TS], offset=cacc_at)
    xin = sb("xin", [P, NI + 1, D], offset=work)
    s1 = after(work, NI + 1, D)
    cst = sb("cst", [NB // 2 * CH, 2, D], offset=s1)
    s2 = after(s1, 2, D)
    vrow = sb("vrow", [P, 3, P], offset=s2)
    cwrow = sb("cwrow", [CK, D], offset=after(s2, 3, P))
    gates = sb("gates", [P, 6, T], offset=after(after(s2, 3, P), D))
    nin = sb("nin", [TS, DH], offset=after(after(after(s2, 3, P), D), 6, T))
    assert after(after(after(after(s2, 3, P), D), 6, T), DH) <= prod_at
    sga = sb("sga", [P, 2, 2, T], offset=work)
    b1 = after(work, 4, T)
    uhi = sb("uhi", [P, KT, T], F32R, offset=after(b1, KT, T))
    hhi = sb("hhi", [P, KT, T], F32R, offset=after(after(b1, KT, T), KT, T))
    mix = sb("mix", [P, KT, T], offset=b1)
    lnt = sb("lnt", [P, 6, T], offset=b1)
    xin2 = sb("xin2", [P, NI + 1, D], offset=arena)
    sq2 = sb("sq2", [P, 4, T], offset=work)
    xrs = sb("xrs", [P, KT * TS], offset=after(after(work, 4, T), T))
    sqsum = sb("sqsum", [P, T], offset=after(work, 4, T))
    fhi, flo = uhi, hhi
    hact = sb("hact", [P, 2 * KT, T], offset=ahi_at)
    hact2 = sb("hact2", [P, KF - 2 * KT, T], offset=arena)
    pre_hi = sb("pre_hi", [P, PRE, T], F32R, offset=after(arena, KF - 2 * KT, T))
    pre_lo_at = after(after(arena, KF - 2 * KT, T), PRE, T)
    pre_lo = sb("pre_lo", [P, PRE, T], F32R, offset=pre_lo_at)
    junk_at = after(pre_lo_at, PRE, T)
    junk = sb("junk", [P, TP], offset=junk_at)
    assert after(junk_at, TP) <= hab_at
    upc = sb("upc", [P, 2, FOUT], offset=work)
    f4 = after(after(after(work, 4, T), T), KT * TS)
    fst = sb("fst", [NB * 2, 2, 2 * P], offset=f4)
    f5 = after(f4, 2, 2 * P)
    fout = sb("fout", [NB * 2 + 2, 2, 2 * P], offset=f5)
    f6 = after(f5, 2, 2 * P)
    up = sb("up", [P, 2, FPW], offset=f6)
    f7 = after(f6, 2, FPW)
    usig = sb("usig", [P, FOUT], offset=f7)
    flast = sb("flast", [P, 2, 2, 18], offset=after(f7, FOUT))
    assert after(after(f7, FOUT), 2, 2, 18) <= after(b1, KT, T)
    x2 = sb("x2", [P, KT, T], offset=hab_at)
    yt = sb("yt", [P, NI + 1, D], offset=work)
    fgb = sb("fgb", [P, D], offset=after(work, NI + 1, D))
    assert after(after(work, NI + 1, D), D) <= after(b1, KT, T)

    with ctx:
        acc = ctx.enter_context(nc.psum_tensor("acc", [P, 2, 2, 512], F32))
        small = ctx.enter_context(nc.psum_tensor("small", [P, RING, 512], F32))
        held = ctx.enter_context(nc.psum_tensor("held", [P, 512], F32))

        def sem(name):
            return ctx.enter_context(nc.semaphore(name))

        raw_in = [sem(f"raw_in{i}") for i in range(NRAW)]
        raw_zeroed = sem("raw_zeroed")
        w_hi, w_lo_dve, w_lo_pool = sem("w_hi"), sem("w_lo_dve"), sem("w_lo_pool")
        down_part = sem("down_part")
        acc_done = sem("acc_done")
        acc_out = [sem("acc_out0"), sem("acc_out1")]
        small_done = sem("small_done")
        small_out = [sem(f"small_out{i}") for i in range(RING)]
        held_done, held_out = sem("held_done"), sem("held_out")
        x_in = [sem(f"x_in{i}") for i in range(NI + 1)]
        consts_in = {name: sem(f"{name}_in") for name in (
            "mix_norm_g", "head_norm_g", "conv_b", "conv_ln_g", "conv_ln_b", "ffn_norm_g", "ffn_conv_b",
            "ffn_tap0", "ffn_tap1", "ffn_tap2", "conv_w", "history0", "history1", "n", "n_head", "m", "bias_i", "bias_f")}
        consts_set = sem("consts_set")
        rs_ready, xs_ready, xn_hi = sem("rs_ready"), sem("xs_ready"), sem("xn_hi")
        ssq_ready, ssq_dve = sem("ssq_ready"), sem("ssq_dve")
        xs_gained, xs_hi = sem("xs_gained"), sem("xs_hi")
        gates_act, gates_dve, rows_ready, rt_ready = (sem(x) for x in ("gates_act", "gates_dve", "rows_ready", "rt_ready"))
        u_added, usq_added = sem("u_added"), sem("usq_added")
        em_ready = sem("em_ready")
        cstage_out = [sem("cstage_out0"), sem("cstage_out1")]
        uc_ready = sem("uc_ready")
        unew_ready, flast_ready = sem("unew_ready"), sem("flast_ready")
        exp_ready, st_masked, qm_ready = sem("exp_ready"), sem("st_masked"), sem("qm_ready")
        cin_in = [sem("cin_in0"), sem("cin_in1")]
        cnew_out = [sem("cnew_out0"), sem("cnew_out1")]
        km_ready = sem("km_ready")
        vks3_ready, gsum_ready, even_new = sem("vks3_ready"), sem("gsum_ready"), sem("even_new")
        hv_ready, hr_ready, hn_ready = sem("hv_ready"), sem("hr_ready"), sem("hn_ready")
        cout_out = sem("cout_out")
        nout_out = sem("nout_out")
        hab_gated, sqsum_ready = sem("hab_gated"), sem("sqsum_ready")
        hhi_ready, hlo_ready = sem("hhi_ready"), sem("hlo_ready")
        xc_ready, sqc_ready, lnstd, yln, ysig, zs, uhi_ready, ulo_ready = (
            sem(x) for x in ("xc_ready", "sqc_ready", "lnstd", "yln", "ysig", "zs", "uhi_ready", "ulo_ready"))
        mix_ready, mhi_ready, mlo_ready = sem("mix_ready"), sem("mhi_ready"), sem("mlo_ready")
        sq_ready, std2, hfhi, hflo = (sem(x) for x in ("sq_ready", "std2", "hfhi", "hflo"))
        xin2_in = [sem(f"xin2_in{i}") for i in range(NI + 1)]
        fst_in = [sem("fst_in0"), sem("fst_in1")]
        fout_out = [sem("fout_out0"), sem("fout_out1")]
        sig_ready, act_ready, dhi_ready, dlo_ready = sem("sig_ready"), sem("act_ready"), sem("dhi_ready"), sem("dlo_ready")
        act_used = sem("act_used")
        state_used = sem("state_used")
        fg_in = sem("fg_in")
        y0_ready, y_out = sem("y0_ready"), sem("y_out")
        y0_copied, y0_gained = sem("y0_copied"), sem("y0_gained")
        yssq1, ysum, yroot, yrs = (sem(x) for x in ("yssq1", "ysum", "yroot", "yrs"))
        rowcopy_out, m_out = sem("rowcopy_out"), sem("m_out")
        act_chain, dve_chain, pool_chain = sem("act_chain"), sem("dve_chain"), sem("pool_chain")

        panels = [s[1:] for s in steps if s[0] == "panel"]
        index_of = {p: n for n, p in enumerate(panels)}

        def block_count(p):
            if p[0] == "if":
                return 1
            return 2 if p[0] != "down" or p[1][1] == 2 else 0

        first_block, raw_value, n_blocks = [], [], 0
        raw_total = [0] * NRAW
        sources = []
        OQ = 0
        OK_, OV, OO = D, 2 * D, 3 * D
        OI = 4 * D
        OGV = OI + 2 * NH
        OGG, OGA, OGB = OGV + D, OGV + 2 * D, OGV + 3 * D
        for n, (kind, i) in enumerate(panels):
            first_block.append(n_blocks)
            n_blocks += block_count((kind, i))
            if kind == "if":
                src = [(w_in, 0, KT, OI, NH, 0), (w_in, 0, KT, OI + NH, NH, 32)]
            elif kind == "glu":
                src = [(w_in, 0, KT, OGG + P * i, P, 0), (w_in, 0, KT, OGV + P * i, P, P)]
            elif kind in "kvqo":
                base = {"q": OQ, "k": OK_, "v": OV, "o": OO}[kind]
                src = [(w_in, 0, KT, base + COLS * i, COLS, 0)]
            elif kind == "gate":
                src = [(w_in, 0, KT, OGA + P * i, P, 0), (w_in, 0, KT, OGB + P * i, P, P)]
            elif kind == "branch":
                src = [(w_mlstm_out, 0, KT, P * i, P, 0), (w_conv_out, 0, KT, P * i, P, P)]
            elif kind == "out":
                src = [(w_out, 0, KT, COLS * i, COLS, 0)]
            elif kind == "up":
                src = [(w_up, 0, KT, P * i, P, 0), (w_up, 0, KT, DFF + P * i, P, P)]
            else:
                g, s = i
                src = [(w_down, s * 8, min(8, KF - 8 * s), COLS * g, COLS, 0)]
            sources.append(src)
            raw_total[n % NRAW] += 16 * len(src)
            raw_value.append(raw_total[n % NRAW])

        first_pool, last_pool = index_of[("glu", 3)], index_of[("gate", 2)]

        def on_pool(n):
            return first_pool <= n <= last_pool or panels[n - 2][0] == "up"

        def wait_lo(eng, n):
            same = sum(on_pool(m) == on_pool(n) for m in range(n + 1))
            eng.wait_ge(w_lo_pool if on_pool(n) else w_lo_dve, same)

        def width(n):
            return P if panels[n][0] == "if" else COLS

        def ktiles(n):
            return sources[n][0][2]

        def panel_view(tile, slot, n):
            return tile[:, slot, 0:ktiles(n) * width(n)].rearrange("p (k c) -> p k c", c=width(n))

        def wait_panel_used(eng, n):
            kind, i = panels[n]
            if kind == "down" and i[1] < 2:
                eng.wait_ge(down_part, 2 * i[0] + i[1] + 1)
            else:
                eng.wait_ge(acc_done, first_block[n] + block_count(panels[n]))

        def acc_ready(eng, n, c):
            b = first_block[n] + c
            eng.wait_ge(acc_done, b + 1)
            return acc[:, b % 2, :, 0:256], acc[:, b % 2, 1, 256:256 + TS], acc_out[b % 2]

        def wait_acc_out(eng, n, c):
            b = first_block[n] + c
            eng.wait_ge(acc_out[b % 2], b // 2 + 1)

        ring_of = {}

        def small_at(name):
            return small[:, ring_of[name] % RING, :]

        def take(eng, name):
            eng.wait_ge(small_done, ring_of[name] + 1)
            return small_at(name)

        def out_sem(name):
            return small_out[ring_of[name] % RING]

        def wait_taken(eng, name):
            k = ring_of[name]
            eng.wait_ge(small_out[k % RING], k // RING + 1)

        def sigmoids(i):
            return usum[:, :] if i < 2 else sg[:, :]

        def skip(*_):
            pass

        def act_tile(k):
            return hact[:, k, :] if k < 2 * KT else hact2[:, k - 2 * KT, :]

        def split_act(u):
            return (pre_hi[:, u, :], pre_lo[:, u, :]) if u < PRE else (uhi[:, u % KT, :], hhi[:, u % KT, :])

        def wait_split_free(eng, u):
            if u >= PRE + KT:
                wait_down(eng, u - KT)
            elif u >= PRE:
                wait_panel_used(eng, index_of[("up", KF - 1)])

        def wait_down(eng, u):
            g, k = u // KF, u % KF
            if k in (7, 15):
                eng.wait_ge(down_part, 2 * g + (k + 1) // 8)
            elif k == KF - 1:
                eng.wait_ge(acc_done, first_block[index_of[("down", (g, 2))]] + 2)
            else:
                eng.wait_ge(act_used, (KF - 3) * g + k + 1 - (k > 7) - (k > 15))

        block = ctx.enter_context(nc.Block())

        @block.tensor
        def _(pe):

            def begin(name):
                k = len(ring_of)
                ring_of[name] = k
                if k >= RING:
                    pe.wait_ge(small_out[k % RING], k // RING)
                return small[:, k % RING, :]

            def end(ins):
                ins.then_inc(small_done, 1)

            def turn(out, src, n):
                return pe.transpose(out, src, ident[0:n, 0:n])

            def setup(_):
                pe.wait_ge(consts_set, 1)
                for name in ("ffn_conv_b", "mix_norm_g", "head_norm_g", "conv_b", "conv_ln_g", "conv_ln_b", "ffn_norm_g"):
                    pe.wait_ge(consts_in[name], 16)
                turned_vectors(0, 92)
                pe.wait_ge(xs_ready, NI + 1)
                o = begin("xTs")
                for k in range(KT):
                    t = turn(o[:, TS * k:TS * k + TS], xin[0:TS, NI, P * k:P * k + P], TS)
                end(t)
                for k in range(KT):
                    o = begin(("xT", k))
                    for i in range(NI):
                        t = turn(o[:, P * i:P * i + P], xin[:, i, P * k:P * k + P], P)
                    end(t)

            def turned_vectors(i, w):
                o = begin(("vec", i))
                end(turn(o[:, 0:w], vrow[0:w, i, :], w))

            def constants(part):
                if part == 0:
                    pe.wait_ge(consts_in["ffn_tap0"], 16)
                    pe.wait_ge(consts_in["ffn_tap1"], 16)
                    turned_vectors(1, 88)
                    pe.wait_ge(consts_in["ffn_tap2"], 16)
                    turned_vectors(2, 44)
                    pe.wait_ge(consts_in["conv_w"], 16)
                    o = begin("cw")
                    for j in range(KT):
                        t = turn(o[:, CK * j:CK * j + CK], cwrow[:, P * j:P * j + P], CK)
                    end(t)
                    return
                for s in range(2):
                    pe.wait_ge(consts_in[f"history{s}"], 16)
                    for q in range(2):
                        o = begin(("cst", s, q))
                        for j in range(4):
                            t = turn(o[:, 120 * j:120 * j + 120], cst[:, s, P * (4 * q + j):P * (4 * q + j) + P], 120)
                        end(t)
                pe.wait_ge(consts_in["n"], 16)
                o = begin("nT")
                for c in range(2):
                    t = turn(o[:, TS * c:TS * c + TS], nin[:, P * c:P * c + P], TS)
                end(t)

            def gateturn(_):
                pe.wait_ge(rows_ready, 1)
                o = begin("rt")
                for i in range(NI):
                    t = turn(o[:, P * i:P * i + P], rows[:, P * i:P * i + P], P)
                end(t)
                o = begin("rts")
                turn(o[0:TS, 0:P], rows[:, TP:T], P)
                end(turn(o[0:NB, P:P + NH], mrow[:, T + TS:T + TS + NB], NH))

            def tail(j):
                wait_acc_out(pe, index_of[("glu", j)], 1)
                o = begin(("ut", j))
                turn(o[0:CH, 0:P], upad[:, j, CH + TP - CH:CH + TP], P)
                pe.wait_ge(unew_ready, j + 1)
                end(turn(o[0:TS, P:2 * P], unew[:, j % 2, :], P))

            def kv(h):
                for c in range(2):
                    wait_acc_out(pe, index_of[("k", h)], c)
                for q in range(3):
                    for what, src in (("kt", kT), ("vt", vqT)):
                        if q == 0 and what == "vt":
                            for c in range(2):
                                wait_acc_out(pe, index_of[("v", h)], c)
                        o = begin((what, h, q))
                        for i in ((0, 1), (2, 3), (4,))[q]:
                            n = P if i < NI else TS
                            for c in range(2):
                                at_ = 256 * (i % 2) + P * c
                                t = turn(o[0:n, at_:at_ + P], src[:, c, P * i:P * i + n], P)
                        end(t)

            def weights(h):
                o = begin(("mb", h))
                end(pe.matmul(o, sel[:, h, :], mrow[:, 0:TP], start=True, stop=True))
                o = begin(("mbs", h))
                end(pe.matmul(o[:, 0:2 * TS + NB], sel[:, h, :], mrow[:, TP:], start=True, stop=True))

            def scores(h):
                wait_acc_out(pe, index_of[("q", h)], 0)
                wait_acc_out(pe, index_of[("q", h)], 1)
                for j in range(NI):
                    o = begin(("s", h, j))
                    for c in range(2):
                        t = pe.matmul(o[:, P * j:TP], kT[:, c, P * j:P * j + P], vqT[:, c, P * j:TP],
                                      start=(c == 0), stop=(c == 1))
                    end(t)
                o = begin(("ss", h))
                for c in range(2):
                    t = pe.matmul(o[0:TS, 0:TS], kT[:, c, TP:T], vqT[:, c, TP:T], start=(c == 0), stop=(c == 1))
                end(t)

            def av(h):
                pe.wait_ge(consts_set, 3)
                wait_taken(pe, ("vt", h, 0))
                wait_taken(pe, ("vt", h, 1))
                wait_taken(pe, ("vt", h, 2))
                pe.wait_ge(st_masked, (NI + 2) * h + NI)
                for i in range(NI):
                    o = begin(("h", h, i))
                    for j in range(i + 1):
                        t = pe.matmul(o[:, 0:DH + 1], sT[:, j, P * i:P * i + P], vk[:, j, :],
                                      start=(j == 0), stop=(j == i))
                    end(t)
                o = begin(("C", h))
                for c in range(2):
                    for j in range(NI):
                        t = pe.matmul(o[:, DH * c:DH * c + DH], vk[:, j, P * c:P * c + P], gk[:, j, :],
                                      start=(j == 0), stop=(j == NI - 1))
                end(t)
                o = begin(("n", h))
                pe.wait_ge(gsum_ready, h + 1)
                pe.matmul(o[0:1, 0:DH], vk[:, 0, DH:DH + 1], gsum[:, :], start=True, stop=True)
                wait_taken(pe, ("kt", h, 2))
                end(pe.matmul(o[0:NB, DH:2 * DH], bm3[0:2 * TS, :], gks3[0:2 * TS, h % 2, :], start=True, stop=True))
                if h:
                    pe.wait_ge(held_out, h)
                pe.wait_ge(st_masked, (NI + 2) * (h + 1))
                pe.matmul(held[0:TS, 0:DH + 1], sTs[:, :], vks[:, h % 2, :], start=True, stop=False)
                pe.wait_ge(qm_ready, h + 1)
                state_turn(h, 0)
                outer_products(h, 0)

            def state_turn(h, b):
                u = NB * h + b
                pe.wait_ge(cin_in[u % 2], 16 * (u // 2 + 1))
                o = begin(("ct", h, b))
                for c in range(2):
                    for v in range(2):
                        t = turn(o[:, DH * c + P * v:DH * c + P * v + P], cin[:, u % 2, v, P * c:P * c + P], P)
                end(t)

            def outer_products(h, pair):
                pe.wait_ge(vks3_ready, h + 1)
                pe.wait_ge(km_ready, NB // 2 * h + pair + 1)
                for c in range(2):
                    o = begin(("u", h, pair, c))
                    end(pe.matmul(o, vks3[:, h % 2, P * c:P * c + P], km[:, :, :], start=True, stop=True))

            def state(h, b):
                u = NB * h + b
                if b + 1 < NB:
                    state_turn(h, b + 1)
                    if b % 2:
                        outer_products(h, (b + 1) // 2)
                wait_taken(pe, ("ct", h, b))
                for c in range(2):
                    t = pe.matmul(held[0:TS, 0:DH + 1], qm[:, c, TS * b:TS * b + TS], cT[:, u % 2, c, :],
                                  start=False, stop=(b == NB - 1 and c == 1))
                if b < NB - 1:
                    t.then_inc(state_used, 1)
                else:
                    t.then_inc(held_done, 1)

            def headout(h):
                pe.wait_ge(hn_ready, h + 1)
                for c in range(2):
                    o = begin(("hT", h, c))
                    for i in range(NI):
                        t = turn(o[:, P * i:P * i + P], ht[:, i, P * c:P * c + P], P)
                    end(t)
                o = begin(("hTs", h))
                for c in range(2):
                    t = turn(o[:, TS * c:TS * c + TS], ht[0:TS, NI, P * c:P * c + P], TS)
                end(t)

            def convmean(_):
                oa, ob = begin("mua"), begin("mub")
                pe.wait_ge(u_added, KT - 1)
                for o, (a, b) in ((oa, HALVES[0]), (ob, HALVES[1])):
                    end(pe.matmul(o[:, 0:b - a], ones[:, :], usum[:, a:b], start=True, stop=True))

            def convvar(_):
                oa, ob = begin("vara"), begin("varb")
                pe.wait_ge(usq_added, KT - 1)
                for o, (a, b) in ((oa, HALVES[0]), (ob, HALVES[1])):
                    end(pe.matmul(o[:, 0:b - a], ones[:, :], usum[:, a:b], start=True, stop=True))

            def residual(part):
                if part == 0:
                    o = begin("xrs")
                    for i in range(NI + 1):
                        pe.wait_ge(xin2_in[i], 16)
                    for k in range(KT):
                        t = turn(o[:, TS * k:TS * k + TS], xin2[0:TS, NI, P * k:P * k + P], TS)
                    end(t)
                for k in RESIDUAL[part]:
                    o = begin(("xr", k))
                    for i in range(NI):
                        t = turn(o[:, P * i:P * i + P], xin2[:, i, P * k:P * k + P], P)
                    end(t)

            def norm_sums():
                oa, ob = begin("qa"), begin("qb")
                pe.wait_ge(sqsum_ready, KT - 1)
                for o, (a, b) in ((oa, HALVES[0]), (ob, HALVES[1])):
                    end(pe.matmul(o[:, 0:b - a], ones[:, :], sqsum[:, a:b], start=True, stop=True))

            def fstate(i):
                pe.wait_ge(fst_in[i % 2], 32 * (i // 2 + 1))
                o = begin(("fs", i))
                for c in range(2):
                    t = turn(o[:, 16 * c:16 * c + 16], fst[:, i % 2, P * c:P * c + P], 16)
                end(t)

            def ftail(i):
                pe.wait_ge(flast_ready, i + 1)
                o = begin(("ft", i))
                for c in range(2):
                    t = turn(o[0:18, P * c:P * c + P], flast[:, i % 2, c, :], P)
                end(t)

            def turn_y(i, ks):
                n = P if i < NI else TS
                for k in ks:
                    t = turn(small_at(("y", i, k // 4))[0:n, P * (k % 4):P * (k % 4) + P], x2[:, k, P * i:P * i + n], P)
                return t

            def turnout(q):
                wait_acc_out(pe, index_of[("down", (1, 2))], 0)
                wait_acc_out(pe, index_of[("down", (1, 2))], 1)
                for i in TURNOUT[q]:
                    begin(("y", i, 0))
                    end(turn_y(i, range(4)))

            def final(_):
                wait_acc_out(pe, index_of[("down", (3, 2))], 0)
                for i in range(RING):
                    begin(("y", i, 1))
                    turn_y(i, range(4, KT - 1))
                wait_acc_out(pe, index_of[("down", (3, 2))], 1)
                for i in range(NI + 1):
                    if i >= RING:
                        begin(("y", i, 1))
                    end(turn_y(i, range(KT - 1 if i < RING else 4, KT)))

            def panel(kind, i):
                n = index_of[(kind, i)]
                pe.wait_ge(w_hi, n + 1)
                wait_lo(pe, n)
                hi, lo = panel_view(whi, n % 2, n), panel_view(wlo, n % 2, n)
                if kind == "down":
                    g, s = i
                    kt0 = 8 * s
                    for c in range(2):
                        b = first_block[n] + c
                        if s == 0:
                            pe.wait_ge(acc_out[b % 2], b // 2)
                        for k in range(ktiles(n)):
                            u = KF * g + kt0 + k
                            last_k = k == ktiles(n) - 1
                            if c == 0:
                                pe.wait_ge(dhi_ready, u + 1)
                                pe.wait_ge(dlo_ready, u + 1)
                            dhi, dlo = split_act(u)
                            for q, (w, x) in enumerate(((hi, dhi), (hi, dlo), (lo, dhi))):
                                for a, (t0, t1) in enumerate(HALVES):
                                    t = pe.matmul(acc[:, b % 2, a, 0:t1 - t0], w[:, k, P * c:P * c + P], x[:, t0:t1],
                                                  start=(s == 0 and k == 0 and q == 0),
                                                  stop=(s == 2 and last_k and q == 2))
                            if last_k and s == 2:
                                t.then_inc(acc_done, 1)
                            elif last_k and c == 1:
                                t.then_inc(down_part, 1)
                            elif c == 1:
                                t.then_inc(act_used, 1)
                    return
                for c in range(block_count((kind, i))):
                    xh, xl = ahi, alo
                    cut = 0
                    if kind == "if":
                        wait_taken(pe, "xTs")
                    if kind == "up":
                        xh, xl = fhi, flo
                        if i == 0 and c == 1:
                            norm_sums()
                    if kind == "branch":
                        xh, xl = (hhi, hlo) if c == 0 else (uhi, ulo)
                        cut = 0 if c == 0 else CH
                    b = first_block[n] + c
                    if b >= 2:
                        pe.wait_ge(acc_out[b % 2], b // 2)
                    for k in range(KT):
                        if kind == "if":
                            wait_taken(pe, ("xT", k))
                        if kind == "branch" and i == 0:
                            pe.wait_ge(hlo_ready if c == 0 else ulo_ready, k + 1)
                        if kind == "out" and i == 0 and c == 0:
                            pe.wait_ge(mlo_ready, k + 1)
                        if kind == "up" and i == 0 and c == 0:
                            pe.wait_ge(hflo, k + 1)
                        for q, (w, x, off) in enumerate(((hi, xh, 0), (hi, xl, cut), (lo, xh, 0))):
                            for a, (t0, t1) in enumerate(HALVES):
                                t = pe.matmul(acc[:, b % 2, a, 0:t1 - t0], w[:, k, P * c:P * c + P],
                                              x[:, k, off + t0:off + t1],
                                              start=(k == 0 and q == 0), stop=(k == KT - 1 and q == 2))
                    t.then_inc(acc_done, 1)

            for s in steps:
                {"setup": setup,
                 "gates": skip,
                 "gateturn": gateturn,
                 "tail": tail,
                 "kv": kv,
                 "weights": weights,
                 "scores": scores,
                 "av": av,
                 "state": state,
                 "headnorm": skip,
                 "headout": headout,
                 "convmean": convmean,
                 "convvar": convvar,
                 "convapply": skip,
                 "split": skip,
                 "residual": residual,
                 "norm2": skip,
                 "fstate": fstate,
                 "ftail": ftail,
                 "turnout": turnout,
                 "constants": constants,
                 "final": final,
                 "panel": panel}[s[0]](*s[1:])

        @block.sync
        def _(sp):
            xp, xs = x_prompt[0], x_sample.rearrange("b t d -> (b t) d")
            for i in range(NI):
                sp.dma_start(xin[:, i, :], xp[P * i:P * i + P, :]).then_inc(x_in[i], 16)
            sp.dma_start(xin[0:TS, NI, :], xs).then_inc(x_in[NI], 16)

            def load(n):
                slot = n % NRAW
                if n == 0:
                    sp.wait_ge(raw_zeroed, 1)
                if n >= NRAW:
                    sp.wait_ge(w_hi, n - NRAW + 1)
                    wait_lo(sp, n - NRAW)
                view = panel_view(raw, slot, n)
                for mat, k0, kn, c0, cn, to in sources[n]:
                    src = mat[0, P * k0:P * (k0 + kn), c0:c0 + cn].rearrange("(k p) c -> p k c", p=P)
                    sp.dma_start(view[:, :, to:to + cn], src).then_inc(raw_in[slot], 16)

            def setup(_):
                load(0)
                load(1)
                rows_of = lambda v: v[0].rearrange("(r c) -> r c", c=P)
                loads = [(vrow[48:92, 0, :], rows_of(ffn_conv_b), "ffn_conv_b"),
                         (vrow[0:8, 0, :], rows_of(mix_norm_g), "mix_norm_g"),
                         (vrow[8:16, 0, :], rows_of(head_norm_g), "head_norm_g"),
                         (vrow[16:24, 0, :], rows_of(conv_b), "conv_b"),
                         (vrow[24:32, 0, :], rows_of(conv_ln_g), "conv_ln_g"),
                         (vrow[32:40, 0, :], rows_of(conv_ln_b), "conv_ln_b"),
                         (vrow[40:48, 0, :], rows_of(ffn_norm_g), "ffn_norm_g"),
                         (vrow[0:44, 1, :], ffn_conv_w[0, 0].rearrange("(r c) -> r c", c=P), "ffn_tap0"),
                         (vrow[44:88, 1, :], ffn_conv_w[0, 1].rearrange("(r c) -> r c", c=P), "ffn_tap1"),
                         (vrow[0:44, 2, :], ffn_conv_w[0, 2].rearrange("(r c) -> r c", c=P), "ffn_tap2"),
                         (cwrow[:, :], conv_w[0], "conv_w"),
                         (cst[:, 0, :], state_conv[0, 0:4].rearrange("b r d -> (b r) d"), "history0"),
                         (cst[:, 1, :], state_conv[0, 4:8].rearrange("b r d -> (b r) d"), "history1"),
                         (nin[:, :], state_n[0].rearrange("b h k -> (b h) k"), "n")]
                for dst, src, name in loads:
                    sp.dma_start(dst, src).then_inc(consts_in[name], 16)
                load(2)
                sp.dma_start(nh[:, :], state_n[0, :, 0, :]).then_inc(consts_in["n_head"], 16)

            def gates_step(part):
                if part:
                    return
                sp.wait_ge(m_out, 1)
                sp.dma_start(m_prompt[0].rearrange("b h -> h b"), rows[32:36, TP - 1:TP], allow_slow_non_contiguous=True).then_inc(rowcopy_out, 16)
                sp.dma_start(m_sample[0].rearrange("b h -> h b"),
                             rows[32:36, TP:T].rearrange("p (b t) -> p b t", t=NS)[:, :, NS - 1],
                             allow_slow_non_contiguous=True).then_inc(rowcopy_out, 16)
                sp.dma_start(conv_sample[0, :, 0:CH - NS, :], state_conv[0, :, NS:CH, :]).then_inc(rowcopy_out, 16)

            def tail(j):
                wait_taken(sp, ("ut", j))
                sp.dma_start(conv_prompt[0, 0, :, P * j:P * j + P], cstage[0:CH, j % 2, 0:P]).then_inc(cstage_out[j % 2], 16)
                sp.dma_start(conv_sample[0, :, CH - NS:CH, P * j:P * j + P],
                             cstage[:, j % 2, P:2 * P]).then_inc(cstage_out[j % 2], 16)

            def wait_new(eng, u):
                h, b = u // NB, u % NB
                if b % 2:
                    wait_taken(eng, ("u", h, b // 2, 1))
                else:
                    eng.wait_ge(even_new, u // 2 + 1)

            def load_state(u):
                if u >= NB * NH:
                    return
                h, b = u // NB, u % NB
                if u >= 2:
                    v = u - 2
                    wait_new(sp, v)
                    sp.wait_ge(small_done, ring_of[("ct", v // NB, v % NB)] + 1)
                sp.dma_start(cin[:, u % 2, :, :], state_C[0, b, h].rearrange("(c p) k -> p c k", p=P)).then_inc(cin_in[u % 2], 16)

            def store_state(u):
                h, b = u // NB, u % NB
                wait_new(sp, u)
                sp.dma_start(C_sample[0, b, h].rearrange("(c p) k -> p c k", p=P), cnew[:, u % 2, :, :]).then_inc(cnew_out[u % 2], 16)

            def pair_of_states(h, pair):
                u = NB * h + 2 * pair
                store_state(u)
                load_state(u + 2)
                store_state(u + 1)

            def scores(h):
                if h == 0:
                    for u in range(2):
                        load_state(u)

            def av(h):
                wait_taken(sp, ("C", h))
                sp.dma_start(C_prompt[0, 0, h].rearrange("(c p) k -> p c k", p=P), cout[:, :, :]).then_inc(cout_out, 16)
                wait_taken(sp, ("n", h))
                sp.dma_start(n_prompt[0, 0, h:h + 1, :], nout[0:1, 0, :]).then_inc(nout_out, 16)
                sp.dma_start(n_sample[0, :, h, :], nout[:, 1, :]).then_inc(nout_out, 16)
                if h + 1 < NH:
                    sp.dma_start(nh[:, :], state_n[0, :, h + 1, :]).then_inc(consts_in["n_head"], 16)
                pair_of_states(h, 0)

            def state(h, b):
                if b % 2 == 0:
                    load_state(NB * h + b + 3)
                elif b + 1 < NB:
                    pair_of_states(h, (b + 1) // 2)

            def load_fstate(i):
                if i >= 2:
                    sp.wait_ge(small_done, ring_of[("fs", i - 2)] + 1)
                src = state_ffn[0].rearrange("b t c -> (b t) c")
                for c in range(2):
                    sp.dma_start(fst[:, i % 2, P * c:P * c + P], src[:, DFF * c + P * i:DFF * c + P * i + P]).then_inc(fst_in[i % 2], 16)

            def residual(part):
                if part == 2:
                    sp.wait_ge(mlo_ready, KT)
                    for i in range(2):
                        load_fstate(i)

            def fstate(i):
                if i + 2 < KF:
                    load_fstate(i + 2)

            def ftail(i):
                wait_taken(sp, ("ft", i))
                for c in range(2):
                    cols = slice(DFF * c + P * i, DFF * c + P * i + P)
                    sp.dma_start(ffn_prompt[0, 0, :, cols], fout[0:2, i % 2, P * c:P * c + P]).then_inc(fout_out[i % 2], 16)
                    sp.dma_start(ffn_sample[0].rearrange("b t c -> (b t) c")[:, cols], fout[2:18, i % 2, P * c:P * c + P]).then_inc(fout_out[i % 2], 16)

            def final(_):
                for i in range(NI + 1):
                    sp.wait_ge(y0_ready, i + 1)
                    wait_taken(sp, ("y", i, 1))
                    if i < NI:
                        sp.dma_start(y_prompt[0, P * i:P * i + P, :], yt[:, i, :]).then_inc(y_out, 16)
                    else:
                        sp.dma_start(y_sample.rearrange("b t d -> (b t) d"), yt[0:TS, NI, :]).then_inc(y_out, 16)
                sp.wait_ge(y_out, 16 * (NI + 1))
                sp.wait_ge(rowcopy_out, 48)
                sp.wait_ge(cout_out, 16 * NH)
                sp.wait_ge(nout_out, 32 * NH)
                for q in range(2):
                    sp.wait_ge(cnew_out[q], 16 * NB * NH // 2)
                    sp.wait_ge(cstage_out[q], 32 * KT // 2)
                    sp.wait_ge(fout_out[q], 64 * KF // 2)

            def panel(kind, i):
                n = index_of[(kind, i)]
                if n + NRAW < len(panels):
                    load(n + NRAW)
                if (kind, i) == ("down", (0, 2)):
                    for q in range(2):
                        sp.wait_ge(fout_out[q], 64 * KF // 2)
                    sp.wait_ge(act_ready, 2 * KF)
                    sp.dma_start(fgb[:, :], final_norm_g.rearrange("(a d) -> a d", a=1).broadcast_to([P, D])).then_inc(fg_in, 16)
                if (kind, i) == ("branch", KT - 1):
                    wait_panel_used(sp, n)
                    for q in range(NI):
                        sp.dma_start(xin2[:, q, :], x_prompt[0, P * q:P * q + P, :]).then_inc(xin2_in[q], 16)
                    sp.dma_start(xin2[0:TS, NI, :], xs).then_inc(xin2_in[NI], 16)

            for s in steps:
                {"setup": setup,
                 "gates": gates_step,
                 "gateturn": skip,
                 "tail": tail,
                 "kv": skip,
                 "weights": skip,
                 "scores": scores,
                 "av": av,
                 "state": state,
                 "headnorm": skip,
                 "headout": skip,
                 "convmean": skip,
                 "convvar": skip,
                 "convapply": skip,
                 "split": skip,
                 "residual": residual,
                 "norm2": skip,
                 "fstate": fstate,
                 "ftail": ftail,
                 "turnout": skip,
                 "constants": skip,
                 "final": final,
                 "panel": panel}[s[0]](*s[1:])

        @block.scalar
        def _(act):
            chain = Count(act_chain)

            def link(ins):
                chain.raised_by(ins)
                act.wait_ge(act_chain, chain.n)

            def split_hi(n):
                act.wait_ge(raw_in[n % NRAW], raw_value[n])
                if n >= 2:
                    wait_panel_used(act, n - 2)
                act.activation(panel_view(whi, n % 2, n), panel_view(raw, n % NRAW, n), ACT.Copy).then_inc(w_hi, 1)

            def out_of(n, c, dst, func, scale=1.0):
                p, s, done = acc_ready(act, n, c)
                chain.raised_by(act.activation(dst[:, TP:T], s, func, scale=scale))
                act.activation(dst[:, 0:TP].rearrange("p (a t) -> p a t", a=2), p, func, scale=scale).then_inc(done, 1)

            def setup(_):
                for i in (0, 2, 4):
                    n = P if i < NI else TS
                    act.wait_ge(x_in[i], 16)
                    if i == 0:
                        act.wait_ge(consts_set, 1)
                    link(act.activation(gates[0:n, 0:2, 0:512], xin[0:n, i, :].rearrange("p (a b) -> p a b", a=2), ACT.Square,
                                        accum_out=stat[0:n, i:i + 1]))
                act.activation(stat[:, 30:31], epsc[:, 0:1], ACT.Copy).then_inc(ssq_ready, 1)
                split_hi(0)
                act.wait_ge(rs_ready, 1)
                for i in range(3, NI + 1):
                    n = P if i < NI else TS
                    act.wait_ge(x_in[i], 16)
                    act.activation(xin[0:n, i, :], xin[0:n, i, :], ACT.Copy, scale=stat[0:n, 8 + i:9 + i]).then_inc(xs_ready, 1)
                split_hi(1)
                vectors_out(0)
                wait_taken(act, ("vec", 0))
                act.wait_ge(xs_gained, 1)
                act.activation(ahi[:, :, TP:T], xsg[:, :, :], ACT.Copy).then_inc(xs_hi, 1)
                for k in range(KT):
                    o = take(act, ("xT", k))
                    act.activation(ahi[:, k, 0:TP], o, ACT.Copy, scale=vec[:, MIXG + k:MIXG + k + 1]).then_inc(xn_hi, 1)

            def vectors_out(i):
                w = (92, 88, 44)[i]
                o = take(act, ("vec", i))
                dst = vec[:, 0:92] if i == 0 else (fcw[:, 0:2, :] if i == 1 else fcw[:, 2, :])
                src = o[:, 0:w] if i != 1 else o[:, 0:w].rearrange("p (a b) -> p a b", a=2)
                act.activation(dst, src, ACT.Copy).then_inc(out_sem(("vec", i)), 1)

            def constants(part):
                if part == 0:
                    vectors_out(1)
                    vectors_out(2)
                    o = take(act, "cw")
                    act.activation(cw[:, :, :], o[:, 0:KT * CK].rearrange("p (j k) -> p j k", j=KT), ACT.Copy).then_inc(out_sem("cw"), 1)
                    return
                for s in range(2):
                    for q in range(2):
                        o = take(act, ("cst", s, q))
                        for j in range(4):
                            dst = upad[:, 4 * q + j, CH + TP:UPW].rearrange("p (b s) -> p b s", s=SEG)[:, 4 * s:4 * s + 4, 0:CH]
                            t = act.activation(dst, o[:, 120 * j:120 * j + 120].rearrange("p (b s) -> p b s", s=CH), ACT.Copy)
                            if j < 3:
                                chain.raised_by(t)
                        t.then_inc(out_sem(("cst", s, q)), 1)
                o = take(act, "nT")
                act.activation(nT[:, :, :], o[:, 0:2 * TS].rearrange("p (c t) -> p c t", c=2), ACT.Copy).then_inc(out_sem("nT"), 1)

            def gates_step(part):
                if part:
                    gates_end()
                    return
                act.wait_ge(gates_dve, 1)
                link(act.activation(gates[32:36, 2, :], gates[32:36, 1, :], ACT.Exp))
                act.activation(gates[32:36, 3, :], gates[32:36, 2, :], ACT.Ln, bias=1.0).then_inc(gates_act, 1)

            def gates_end():
                act.wait_ge(gates_dve, 2)
                chain.raised_by(act.activation(rows[64:68, :], gates[0:4, 4, :], ACT.Exp))
                chain.raised_by(act.activation(mrow[:, T:T + TS + NB], gates[0:4, 5, 0:TS + NB], ACT.Exp))
                act.activation(rows[96:100, TP:T], gates[0:4, 5, 0:TS], ACT.Exp).then_inc(rows_ready, 1)
                act.wait_ge(act_chain, chain.n)
                act.wait_ge(rows_ready, 1)

            def gateturn(_):
                o = take(act, "rt")
                four = lambda x, n: x.rearrange("p (i g c) -> p i g c", i=n, g=4)[:, :, :, 0:NH]
                act.activation(rt[:, 0:NI, :].rearrange("p i (g c) -> p i g c", g=4), four(o, NI), ACT.Copy).then_inc(out_sem("rt"), 1)
                o = take(act, "rts")
                act.activation(rt[0:TS, NI:, :].rearrange("p i (g c) -> p i g c", g=4), four(o[0:TS, 0:P], 1), ACT.Copy).then_inc(rt_ready, 1)
                act.activation(gib[:, :], o[0:NB, P:P + NH], ACT.Copy).then_inc(out_sem("rts"), 1)
                wait_taken(act, "rt")
                wait_taken(act, "rts")
                act.wait_ge(rt_ready, 1)
                act.activation(em[:, :, :], rt[:, :, NH:2 * NH], ACT.Exp, scale=-1.0).then_inc(em_ready, 1)

            def tail(j):
                o = take(act, ("ut", j))
                if j >= 2:
                    act.wait_ge(cstage_out[j % 2], 32 * (j // 2))
                chain.raised_by(act.activation(cstage[0:CH, j % 2, 0:P], o[0:CH, 0:P], ACT.Copy))
                act.activation(cstage[:, j % 2, P:2 * P], o[0:TS, P:2 * P], ACT.Copy).then_inc(out_sem(("ut", j)), 1)

            def kv(h):
                for q in range(3):
                    o = take(act, ("vt", h, q))
                    if q < 2:
                        act.activation(vk[:, 2 * q:2 * q + 2, 0:DH], o.rearrange("p (i c) -> p i c", i=2), ACT.Copy).then_inc(out_sem(("vt", h, q)), 1)
                    else:
                        chain.raised_by(act.activation(vks3[0:TS, h % 2, :], o[0:TS, 0:DH], ACT.Copy))
                        chain.raised_by(act.activation(vks3[TS:2 * TS, h % 2, :], o[0:TS, 0:DH], ACT.Copy))
                        act.activation(vks[:, h % 2, 0:DH], o[0:TS, 0:DH], ACT.Copy).then_inc(out_sem(("vt", h, q)), 1)

            def weights(h):
                o = take(act, ("mb", h))
                if h:
                    act.wait_ge(small_done, ring_of[("n", h - 1)] + 1)
                    act.wait_ge(qm_ready, h)
                act.activation(mb[:, 0:TP], o, ACT.Copy).then_inc(out_sem(("mb", h)), 1)
                o = take(act, ("mbs", h))
                chain.raised_by(act.activation(gic[:, h % 2, :], o[:, 2 * TS:2 * TS + NB], ACT.Copy))
                act.activation(mb[:, TP:T + TS], o[:, 0:2 * TS], ACT.Copy).then_inc(out_sem(("mbs", h)), 1)
                wait_taken(act, ("mb", h))
                wait_taken(act, ("mbs", h))
                for j in range(NI):
                    act.activation(sT[:, j, P * j:TP], mb[:, P * j:TP], ACT.Exp, bias=rt[:, j, h:h + 1], scale=-1.0).then_inc(exp_ready, 1)
                if h:
                    act.wait_ge(state_used, (NB - 1) * (h - 1) + 1)
                act.activation(sTs[:, :], mb[0:TS, TP:T], ACT.Exp, bias=rt[0:TS, NI, h:h + 1], scale=-1.0).then_inc(exp_ready, 1)

            def av(h):
                if h >= 2:
                    act.wait_ge(small_done, ring_of[("hTs", h - 2)] + 1)
                for i in range(NI):
                    o = take(act, ("h", h, i))
                    act.activation(ht[:, i, :], o[:, 0:DH + 1], ACT.Copy).then_inc(out_sem(("h", h, i)), 1)
                o = take(act, ("C", h))
                if h:
                    act.wait_ge(cout_out, 16 * h)
                act.activation(cout[:, :, :], o.rearrange("p (c k) -> p c k", c=2), ACT.Copy).then_inc(out_sem(("C", h)), 1)
                if h == 0:
                    for q in range(2):
                        act.wait_ge(cstage_out[q], 32 * KT // 2)
                turned(h, 0)

            def turned(h, b):
                u = NB * h + b
                o = take(act, ("ct", h, b))
                if u >= 2:
                    if b >= 2:
                        act.wait_ge(state_used, (NB - 1) * h + b - 1)
                    elif b == 1:
                        act.wait_ge(held_done, h)
                    else:
                        act.wait_ge(state_used, (NB - 1) * h)
                chain.raised_by(act.activation(cT[:, u % 2, :, DH:DH + 1], nT[:, :, NH * b + h:NH * b + h + 1], ACT.Copy))
                act.activation(cT[:, u % 2, :, 0:DH], o.rearrange("p (c k) -> p c k", c=2), ACT.Copy).then_inc(out_sem(("ct", h, b)), 1)

            def state(h, b):
                if b + 1 < NB:
                    turned(h, b + 1)
                for p, behind in SPLIT_IN.items():
                    if behind == (h, b):
                        split_hi(index_of[p] + 2)
                if b == NB - 1:
                    act.wait_ge(held_done, h + 1)
                    act.activation(ht[0:TS, NI, :], held[0:TS, 0:DH + 1], ACT.Copy).then_inc(held_out, 1)

            def convmean(_):
                for j in range(KT):
                    act.wait_ge(xc_ready, j + 1)
                    if j >= 4:
                        act.wait_ge(usq_added, max(1, j - 4))
                    act.activation(lnt[:, 2 + j % 4, :], upad[:, j, CH:CH + T], ACT.Square).then_inc(sqc_ready, 1)

            def convvar(_):
                for name, (a, b) in (("vara", HALVES[0]), ("varb", HALVES[1])):
                    o = take(act, name)
                    act.activation(lnt[:, 1, a:b], o[:, 0:b - a], ACT.Sqrt, scale=1.0 / D, bias=epsc[:, 0:1]).then_inc(out_sem(name), 1)

            def convapply(part):
                for j in APPLY[part]:
                    act.wait_ge(yln, j + 1)
                    chain.raised_by(act.activation(upad[:, j, CH:CH + T], lnt[:, 2 + j % 4, :], ACT.Identity,
                                                   bias=vec[:, CLB + j:CLB + j + 1], scale=vec[:, CLG + j:CLG + j + 1]))
                    act.activation(lnt[:, 2 + j % 4, :], lnt[:, 2 + j % 4, :], ACT.Sigmoid,
                                   bias=vec[:, CLB + j:CLB + j + 1], scale=vec[:, CLG + j:CLG + j + 1]).then_inc(ysig, 1)

            def split(_):
                for name in (("hTs", NH - 1), ("hT", NH - 1, 0), ("hT", NH - 1, 1), ("u", NH - 1, NB // 2 - 1, 1), ("n", NH - 1)):
                    wait_taken(act, name)
                wait_taken(act, ("ct", NH - 1, NB - 1))
                act.wait_ge(hab_gated, NH - 1)
                act.wait_ge(uc_ready, KT)
                for q in range(2):
                    act.wait_ge(cnew_out[q], 16 * NB * NH // 2)
                act.wait_ge(cout_out, 16 * NH)
                act.wait_ge(nout_out, 32 * NH)
                for k in range(KT):
                    act.activation(hhi[:, k, :], hab[:, k, :], ACT.Copy).then_inc(hhi_ready, 1)
                act.wait_ge(zs, KT)
                for j in range(KT):
                    act.activation(uhi[:, j, :], upad[:, j, CH:CH + T], ACT.Copy).then_inc(uhi_ready, 1)

            def residual(part):
                for j in RESIDUAL[part]:
                    wait_taken(act, ("xr", j))
                    act.activation(fhi[:, j, :], x1[:, j, :], ACT.Copy, scale=vec[:, FG + j:FG + j + 1]).then_inc(hfhi, 1)
                    if j >= 4:
                        act.wait_ge(sqsum_ready, max(1, j - 4))
                    act.activation(sq2[:, j % 4, :], x1[:, j, :], ACT.Square).then_inc(sq_ready, 1)
                if part == 2:
                    split_hi(index_of[("out", 3)] + 2)

            def norm2(_):
                for name, (a, b) in (("qa", HALVES[0]), ("qb", HALVES[1])):
                    o = take(act, name)
                    act.activation(mb[:, a:b], o[:, 0:b - a], ACT.Sqrt, scale=1.0 / D, bias=epsc[:, 0:1]).then_inc(out_sem(name), 1)

            def fstate(i):
                o = take(act, ("fs", i))
                if i:
                    act.wait_ge(act_ready, 2 * i)
                    act.wait_ge(flast_ready, i)
                else:
                    act.wait_ge(consts_set, 4)
                dst = up[:, :, FK - 1 + TP:FK - 1 + TP + NB * FSEG].rearrange("p c (b s) -> p c b s", s=FSEG)
                for c in range(2):
                    t = act.activation(dst[:, c, :, 0:2], o[:, 16 * c:16 * c + 16].rearrange("p (b s) -> p b s", s=2), ACT.Copy)
                    if c == 0:
                        chain.raised_by(t)
                t.then_inc(out_sem(("fs", i)), 1)

            def ftail(i):
                o = take(act, ("ft", i))
                if i >= 2:
                    act.wait_ge(fout_out[i % 2], 64 * (i // 2))
                act.activation(fout[:, i % 2, :], o[0:18, 0:2 * P], ACT.Copy).then_inc(out_sem(("ft", i)), 1)

            def final(_):
                wait_taken(act, ("y", NI, 0))
                act.activation(stat[:, 31:32], epsc[:, 0:1], ACT.Sqrt)
                squares(0)
                for i in range(NI + 1):
                    n = P if i < NI else TS
                    if i < NI:
                        squares(i + 1)
                    act.wait_ge(ysum, i + 1)
                    act.activation(stat[0:n, 8 + i:9 + i], stat[0:n, 8 + i:9 + i], ACT.Sqrt,
                                   scale=1.0 / D, bias=epsc[0:n, 0:1]).then_inc(yroot, 1)
                    if i:
                        scale_first_half(i - 1)
                scale_first_half(NI)

            def scale_first_half(i):
                n = P if i < NI else TS
                act.wait_ge(yrs, i + 1)
                act.wait_ge(y0_gained, i + 1)
                act.activation(yt[0:n, i, 0:512], yt[0:n, i, 0:512], ACT.Copy, scale=stat[0:n, 8 + i:9 + i]).then_inc(y0_ready, 1)

            def squares(i):
                n = P if i < NI else TS
                o = take(act, ("y", i, 1))
                if i:
                    act.wait_ge(yssq1, i)
                act.activation(junk[0:n, :], o[0:n, :], ACT.Square, accum_out=stat[0:n, 17 + 2 * i:18 + 2 * i]).then_inc(yssq1, 1)

            def split_acts(n):
                g, q = panels[n][1]
                for k in range(ktiles(n)):
                    kt = KT * q + k
                    u = KF * g + kt
                    wait_split_free(act, u)
                    if g == 0:
                        act.wait_ge(act_ready, 2 * (kt + 1))
                    act.activation(split_act(u)[0], act_tile(kt), ACT.Copy).then_inc(dhi_ready, 1)

            def turnout(q):
                for i in TURNOUT[q]:
                    n = P if i < NI else TS
                    o = take(act, ("y", i, 0))
                    act.activation(yt[0:n, i, 0:512], o[0:n, :], ACT.Copy).then_inc(y0_copied, 1)
                    if i:
                        act.wait_ge(small_out[ring_of[("y", i - 1, 0)] % RING], ring_of[("y", i - 1, 0)] // RING + 1)
                    act.activation(junk[0:n, :], o[0:n, :], ACT.Square,
                                   accum_out=stat[0:n, 16 + 2 * i:17 + 2 * i]).then_inc(out_sem(("y", i, 0)), 1)

            def panel(kind, i):
                n = index_of[(kind, i)]
                if kind == "glu":
                    if i:
                        wait_acc_out(act, index_of[("glu", i - 1)], 1)
                    out_of(n, 0, sigmoids(i), ACT.Sigmoid)
                elif kind == "k":
                    if i == 0:
                        wait_taken(act, "xTs")
                        wait_taken(act, "rts")
                        act.wait_ge(gates_dve, 2)
                        wait_taken(act, ("cst", 1, 1))
                    for c in range(2):
                        out_of(n, c, kT[:, c, :], ACT.Copy, scale=DH ** -0.5)
                elif kind in "vq":
                    for c in range(2):
                        out_of(n, c, vqT[:, c, :], ACT.Copy)
                elif kind == "o":
                    if i == 0:
                        act.wait_ge(small_done, ring_of[("ss", NH - 1)] + 1)
                        act.wait_ge(qm_ready, NH)
                    if i == 2:
                        act.wait_ge(hab_gated, 1)
                    for c in range(2):
                        out_of(n, c, hab[:, 2 * i + c, :] if i == NH - 1 else sga[:, i % 2, c, :], ACT.Sigmoid)
                elif kind == "gate":
                    if i < 2:
                        act.wait_ge(hab_gated, 3 - i)
                    if i >= 2:
                        act.wait_ge(mix_ready, i - 1)
                    for c in range(2):
                        out_of(n, c, sga[:, i % 2, c, :], ACT.Sigmoid)
                elif kind == "branch":
                    for k in {KT - 2: range(KT - 2), KT - 1: range(KT - 2, KT)}.get(i, ()):
                        act.wait_ge(mix_ready, k + 1)
                        wait_panel_used(act, index_of[("gate", KT - 1)])
                        act.activation(ahi[:, k, :], mix[:, k, :], ACT.Copy).then_inc(mhi_ready, 1)
                elif kind == "out":
                    if i == 0:
                        wait_panel_used(act, index_of[("branch", KT - 1)])
                    for c in range(2):
                        p, sm, done = acc_ready(act, n, c)
                        chain.raised_by(act.activation(x1[:, 2 * i + c, TP:T], sm, ACT.Copy))
                        act.activation(x1[:, 2 * i + c, 0:TP].rearrange("p (a t) -> p a t", a=2), p, ACT.Copy).then_inc(done, 1)
                elif kind == "up":
                    act.wait_ge(sig_ready, 2 * i + 1)
                    act.activation(usig[:, :], upc[:, 0, :], ACT.Sigmoid).then_inc(sig_ready, 1)
                    if i == KF - 1:
                        split_acts(n + 1)
                    split_hi(n + 2)
                    wait_acc_out(act, n, 1)
                    ends = up[:, :, TP:TP + 9 * FSEG].rearrange("p c (b s) -> p c b s", s=FSEG)[:, :, :, 0:2]
                    if i >= 2:
                        act.wait_ge(small_done, ring_of[("ft", i - 2)] + 1)
                    act.activation(flast[:, i % 2, :, :].rearrange("p c (b s) -> p c b s", s=2), ends, ACT.Copy).then_inc(flast_ready, 1)
                    return
                elif kind == "down" and n + 1 < len(panels):
                    split_acts(n + 1)
                if (kind, i) == ("out", 3):
                    return
                if n + 2 < len(panels) and (kind, i) not in SPLIT_IN:
                    split_hi(n + 2)

            for s in steps:
                {"setup": setup,
                 "gates": gates_step,
                 "gateturn": gateturn,
                 "tail": tail,
                 "kv": kv,
                 "weights": weights,
                 "scores": skip,
                 "av": av,
                 "state": state,
                 "headnorm": skip,
                 "headout": skip,
                 "convmean": convmean,
                 "convvar": convvar,
                 "convapply": convapply,
                 "split": split,
                 "residual": residual,
                 "norm2": norm2,
                 "fstate": fstate,
                 "ftail": ftail,
                 "turnout": turnout,
                 "constants": constants,
                 "final": final,
                 "panel": panel}[s[0]](*s[1:])

        conv_done_in = {}

        @block.vector
        def _(dve):
            chain = Count(dve_chain)
            tt, stt, ts = dve.tensor_tensor, dve.scalar_tensor_tensor, dve.tensor_scalar

            def link(ins):
                chain.raised_by(ins)
                dve.wait_ge(dve_chain, chain.n)

            def split_lo(n):
                dve.wait_ge(w_hi, n + 1)
                tt(panel_view(wlo, n % 2, n), panel_view(raw, n % NRAW, n), panel_view(whi, n % 2, n).bitcast(F32),
                   ALU.subtract).then_inc(w_lo_dve, 1)

            def setup(_):
                for i in (1, 3):
                    dve.wait_ge(x_in[i], 16)
                    dve.wait_ge(consts_set, 1)
                    t = stt(gates[:, 2:4, 0:512], xin[:, i, :].rearrange("p (a b) -> p a b", a=2), 1.0,
                            xin[:, i, :].rearrange("p (a b) -> p a b", a=2), ALU.mult, ALU.mult, accum_out=stat[:, i:i + 1])
                    if i == 1:
                        link(t)
                t.then_inc(ssq_dve, 1)
                dve.wait_ge(rs_ready, 1)
                for i in range(3):
                    dve.wait_ge(x_in[i], 16)
                    ts(xin[:, i, :], xin[:, i, :], stat[:, 8 + i:9 + i], None, ALU.mult).then_inc(xs_ready, 1)
                split_lo(0)
                wait_taken(dve, ("vec", 0))
                o = take(dve, "xTs")
                tt(xsg[:, :, :], o[:, 0:KT * TS].rearrange("p (k t) -> p k t", k=KT),
                   vec[:, MIXG:MIXG + KT].rearrange("p (k t) -> p k t", t=1).broadcast_to([P, KT, TS]), ALU.mult).then_inc(xs_gained, 1)
                dve.wait_ge(xs_hi, 1)
                tt(alo[:, :, TP:T], xsg[:, :, :], ahi[:, :, TP:T].bitcast(F32), ALU.subtract).then_inc(out_sem("xTs"), 1)
                for k in range(KT):
                    o = take(dve, ("xT", k))
                    dve.wait_ge(xn_hi, k + 1)
                    stt(alo[:, k, 0:TP], o, vec[:, MIXG + k:MIXG + k + 1], ahi[:, k, 0:TP].bitcast(F32),
                        ALU.mult, ALU.subtract).then_inc(out_sem(("xT", k)), 1)
                split_lo(1)

            def logits():
                n = index_of[("if", 0)]
                p, s, done = acc_ready(dve, n, 0)
                dve.wait_ge(consts_in["bias_i"], 16)
                dve.wait_ge(consts_in["bias_f"], 16)
                dve.wait_ge(consts_set, 2)
                dve.wait_ge(ssq_ready, 1)
                dve.wait_ge(ssq_dve, 1)
                for r in (0, 32):
                    chain.raised_by(ts(gates[r:r + 4, 0, 0:TP].rearrange("p (a t) -> p a t", a=2), p[r:r + 4], stat[r:r + 4, 38:39], None, ALU.add))
                    t = ts(gates[r:r + 4, 0, TP:T], s[r:r + 4], stat[r:r + 4, 38:39], None, ALU.add)
                    if r == 0:
                        chain.raised_by(t)
                t.then_inc(done, 1)

            def gates_step(part):
                if part:
                    return
                for q in range(3):
                    chain.raised_by(dve.tensor_copy(bm3[TS * q:TS * q + TS, :], bmask[:, :]))
                dve.wait_ge(consts_in["m"], 16)
                wait_acc_out(dve, index_of[("if", 0)], 0)
                dve.wait_ge(dve_chain, chain.n)
                G = gates
                zi, zf = G[0:4, 0, :], G[32:36, 0, :]
                link(ts(G[32:36, 2, :], zf, -1.0, None, ALU.mult))
                tt(G[32:36, 1, :], zf, G[32:36, 2, :], ALU.min).then_inc(gates_dve, 1)
                dve.wait_ge(gates_act, 1)
                link(stt(G[0:4, 1, :], zf, 0.0, G[32:36, 3, :], ALU.min, ALU.subtract))
                link(dve.tensor_tensor_scan(G[0:4, 2, 0:TP], ones4(), G[0:4, 1, 0:TP], 0.0, ALU.mult, ALU.add))
                sb_ = G[0:4, 2, TP:T].rearrange("p (b t) -> p b t", t=NS)
                lf_ = G[0:4, 1, TP:T].rearrange("p (b t) -> p b t", t=NS)
                link(dve.tensor_copy(sb_[:, :, 0], lf_[:, :, 0]))
                for t in range(1, NS):
                    link(tt(sb_[:, :, t], sb_[:, :, t - 1], lf_[:, :, t], ALU.add))
                link(tt(rows[0:4, :], zi, G[0:4, 2, :], ALU.subtract))
                link(dve.tensor_tensor_scan(mrow[:, 0:TP], ones4(), rows[0:4, 0:TP], 0.0, ALU.mult, ALU.max))
                sm_ = mrow[:, TP:T].rearrange("p (b t) -> p b t", t=NS)
                a_ = rows[0:4, TP:T].rearrange("p (b t) -> p b t", t=NS)
                m0 = stat[0:4, 22:30]
                link(tt(sm_[:, :, 0], m0, a_[:, :, 0], ALU.max))
                for t in range(1, NS):
                    link(tt(sm_[:, :, t], sm_[:, :, t - 1], a_[:, :, t], ALU.max))
                tt(rows[32:36, :], G[0:4, 2, :], mrow[:, 0:T], ALU.add).then_inc(m_out, 1)
                link(ts(G[0:4, 4, 0:TP], rows[0:4, 0:TP], mrow[:, TP - 1:TP], None, ALU.subtract))
                last = sm_[:, :, NS - 1:NS]
                link(tt(G[0:4, 4, TP:T].rearrange("p (b t) -> p b t", t=NS), a_, last.broadcast_to([NH, NB, NS]), ALU.subtract))
                m0b = m0.rearrange("p (b t) -> p b t", t=1)
                link(tt(G[0:4, 5, 0:TS].rearrange("p (b t) -> p b t", t=NS), m0b.broadcast_to([NH, NB, NS]), sm_, ALU.subtract))
                dve.wait_ge(m_out, 1)
                tt(G[0:4, 5, TS:TS + NB], m0, sm_[:, :, NS - 1], ALU.subtract).then_inc(gates_dve, 1)

            def ones4():
                return gates[0:4, 3, 0:TP]

            conv_at, conv_input, now = [0], [0], [0]

            def conv_part(j, part):
                u = upad[:, j, :]
                taps = cw[:, j, :].rearrange("p (b t k) -> p b t k", b=1, t=1).broadcast_to([P, NB, 2, CK])
                if part == 0:
                    link(ts(cacc[:, 0:TP], u[:, 0:TP], cw[:, j, 0:1], vec[:, CB + j:CB + j + 1], ALU.mult, ALU.add))
                elif part in (1, 3):
                    q = part // 2
                    w = u[:, CH + TP:UPW].rearrange("p (b s) -> p b s", s=SEG)[:, :, 2 * q:2 * q + 2]
                    ap = [list(x) for x in w.ap]
                    link(tt(prod[:, :, :, :], bass.AP(w.tensor, w.offset, [ap[0], ap[1], [1, 2], [1, CK]]), taps, ALU.mult))
                elif part in (2, 4):
                    q = part // 2 - 1
                    link(dve.tensor_reduce(cacc[:, TP:T].rearrange("p (b t) -> p b t", t=NS)[:, :, 2 * q:2 * q + 2],
                                           prod[:, :, :, :], mybir.AxisListType.X, ALU.add))
                elif part < CONV_PARTS - 1:
                    k = part - 4
                    link(stt(cacc[:, 0:TP], u[:, k:k + TP], cw[:, j, k:k + 1], cacc[:, 0:TP], ALU.mult, ALU.add))
                else:
                    dve.wait_ge(small_done, ring_of[("ut", j)] + 1)
                    link(stt(u[:, CH:CH + TP], u[:, CH:CH + TP], cw[:, j, CH:CH + 1], cacc[:, 0:TP], ALU.mult, ALU.add))
                    ts(u[:, CH + TP:CH + T], cacc[:, TP:T], vec[:, CB + j:CB + j + 1], None, ALU.add).then_inc(uc_ready, 1)
                    dve.wait_ge(uc_ready, j + 1)
                    conv_done_in[j] = now[0]

            def conv(n):
                until = min(conv_at[0] + n, CONV_PARTS * conv_input[0])
                for at_part in range(conv_at[0], until):
                    conv_part(at_part // CONV_PARTS, at_part % CONV_PARTS)
                conv_at[0] = until

            def kv(h):
                dve.wait_ge(rt_ready, 1)
                wait_taken(dve, "rt")
                for q in range(3):
                    o = take(dve, ("kt", h, q))
                    if q < 2:
                        chain.raised_by(ts(gk[:, 2 * q, :], o[:, 0:DH], rt[:, 2 * q, 2 * NH + h:2 * NH + h + 1], None, ALU.mult))
                        ts(gk[:, 2 * q + 1, :], o[:, DH:2 * DH], rt[:, 2 * q + 1, 2 * NH + h:2 * NH + h + 1], None, ALU.mult).then_inc(out_sem(("kt", h, q)), 1)
                    else:
                        g = rt[0:TS, NI, 2 * NH + h:2 * NH + h + 1]
                        chain.raised_by(ts(gks3[2 * TS:3 * TS, h % 2, :], o[0:TS, 0:DH], g, None, ALU.mult))
                        link(ts(gks3[0:TS, h % 2, :], o[0:TS, 0:DH], g, None, ALU.mult))
                        stt(gks3[TS:2 * TS, h % 2, :], o[0:TS, 0:DH], g, gks3[0:TS, h % 2, :].bitcast(F32),
                            ALU.mult, ALU.subtract).then_inc(out_sem(("kt", h, q)), 1)
                wait_taken(dve, ("vt", h, 2))
                tt(vks3[2 * TS:3 * TS, h % 2, :], vks[:, h % 2, 0:DH], vks3[0:TS, h % 2, :].bitcast(F32), ALU.subtract).then_inc(vks3_ready, 1)

            def scores(h):
                for j in range(NI + 1):
                    dve.wait_ge(exp_ready, (NI + 1) * h + j + 1)
                    name = ("s", h, j) if j < NI else ("ss", h)
                    o = take(dve, name)
                    if j < NI:
                        tt(sT[:, j, P * j:TP], sT[:, j, P * j:TP], o[:, P * j:TP], ALU.mult).then_inc(out_sem(name), 1)
                    else:
                        tt(sTs[:, :], sTs[:, :], o[0:TS, 0:TS], ALU.mult).then_inc(out_sem(name), 1)
                wait_taken(dve, ("mbs", h))
                if h:
                    dve.wait_ge(held_done, h)
                else:
                    dve.wait_ge(consts_set, 3)
                for c in range(2):
                    dst = qm[:, c, :].rearrange("p (b s) -> p b s", s=36)[:, :, 0:NS]
                    t = tt(dst, vqT[:, c, TP:T].rearrange("p (b t) -> p b t", t=NS), mb[:, T:T + TS].rearrange("p (b t) -> p b t", t=NS), ALU.mult)
                    if c == 0:
                        chain.raised_by(t)
                t.then_inc(qm_ready, 1)

            def av(h):
                mask(h, 0)
                conv(4)
                o = take(dve, ("n", h))
                if h:
                    dve.wait_ge(nout_out, 32 * h)
                wait_taken(dve, "rts")
                dve.wait_ge(consts_in["n_head"], 16 * (h + 1))
                chain.raised_by(dve.tensor_copy(nout[0:1, 0, :], o[0:1, 0:DH]))
                stt(nout[:, 1, :], nh[:, :], gib[:, h:h + 1], o[0:NB, DH:2 * DH], ALU.mult, ALU.add).then_inc(out_sem(("n", h)), 1)

                update(h, 0)
                update(h, 1)
                mask(h, 1)

            def mask(h, pair):
                p = NB // 2 * h + pair
                if p:
                    v = p - 1
                    dve.wait_ge(small_done, ring_of[("u", v // (NB // 2), v % (NB // 2), 1)] + 1)
                wait_taken(dve, ("kt", h, 2))
                keys = gks3[:, h % 2, :].bitcast(F32).rearrange("p (b k) -> p b k", b=1).broadcast_to([3 * TS, 2, DH])
                own = bm3[:, 2 * pair:2 * pair + 2].bitcast(F32).rearrange("p (b k) -> p b k", k=1).broadcast_to([3 * TS, 2, DH])
                tt(km[:, :, :], keys, own, ALU.mult).then_inc(km_ready, 1)

            def update(h, b):
                u, pair = NB * h + b, b // 2
                if u >= 2:
                    dve.wait_ge(cnew_out[u % 2], 16 * (u // 2))
                dve.wait_ge(cin_in[u % 2], 16 * (u // 2 + 1))
                for c in range(2):
                    name = ("u", h, pair, c)
                    o = take(dve, name)
                    t = stt(cnew[:, u % 2, c, :], cin[:, u % 2, c, :], gic[:, h % 2, b:b + 1], o[:, DH * (b % 2):DH * (b % 2) + DH],
                            ALU.mult, ALU.add)
                    if b % 2:
                        t.then_inc(out_sem(name), 1)
                    elif c:
                        t.then_inc(even_new, 1)
                    else:
                        chain.raised_by(t)

            def state(h, b):
                if b % 2 and b + 1 < NB:
                    update(h, b + 1)
                    update(h, b + 2)
                    if b + 3 < NB:
                        mask(h, (b + 3) // 2)
                if b != 2:
                    conv(2)

            def weights(h):
                conv(4)

            def headnorm(h):
                dve.wait_ge(em_ready, 1)
                for i in range(NI):
                    wait_taken(dve, ("h", h, i))
                dve.wait_ge(held_out, h + 1)
                for i in range(NI + 1):
                    n = P if i < NI else TS
                    chain.raised_by(stt(stat[0:n, i:i + 1], ht[0:n, i, DH:DH + 1], -1.0, ht[0:n, i, DH:DH + 1], ALU.mult, ALU.max))
                    chain.raised_by(dve.bn_stats(bst[0:n, i, :], ht[0:n, i, 0:DH]))
                dve.wait_ge(dve_chain, chain.n)
                for i in range(NI + 1):
                    n = P if i < NI else TS
                    chain.raised_by(dve.bn_aggr(stat[0:n, 12 + 2 * i:14 + 2 * i], bst[0:n, i, :]))
                link(tt(stat[:, 0:5], stat[:, 0:5], em[:, :, h], ALU.max))
                link(dve.reciprocal(stat[:, 0:5], stat[:, 0:5]))
                var = stat[:, 12:22].rearrange("p (i q) -> p i q", q=2)[:, :, 1]
                link(tt(stat[:, 5:10], stat[:, 0:5], stat[:, 0:5], ALU.mult))
                link(tt(stat[:, 5:10], stat[:, 5:10], var, ALU.mult))
                ts(stat[:, 5:10], stat[:, 5:10], EPS, None, ALU.add).then_inc(hv_ready, 1)
                conv(4)
                dve.wait_ge(hr_ready, h + 1)
                link(tt(stat[:, 0:5], stat[:, 0:5], stat[:, 5:10], ALU.mult))
                for i in range(NI + 1):
                    n = P if i < NI else TS
                    t = ts(ht[0:n, i, 0:DH], ht[0:n, i, 0:DH], stat[0:n, 12 + 2 * i:13 + 2 * i], stat[0:n, i:i + 1], ALU.subtract, ALU.mult)
                    if i < NI:
                        chain.raised_by(t)
                dve.wait_ge(dve_chain, chain.n)
                t.then_inc(hn_ready, 1)

            def headout(h):
                last_head = h == NH - 1
                if last_head:
                    wait_acc_out(dve, index_of[("o", h)], 0)
                    wait_acc_out(dve, index_of[("o", h)], 1)

                def gained(dst, src, k):
                    gain = vec[:, HEADG + k:HEADG + k + 1]
                    if last_head:
                        return stt(dst, src, gain, dst, ALU.mult, ALU.mult)
                    return ts(dst, src, gain, None, ALU.mult)

                for c in range(2):
                    k = 2 * h + c
                    o = take(dve, ("hT", h, c))
                    gained(hab[:, k, 0:TP], o, k).then_inc(out_sem(("hT", h, c)), 1)
                o = take(dve, ("hTs", h))
                for c in range(2):
                    k = 2 * h + c
                    t = gained(hab[:, k, TP:T], o[:, TS * c:TS * c + TS], k)
                    if c == 0:
                        chain.raised_by(t)
                t.then_inc(out_sem(("hTs", h)), 1)
                conv(4)

            def convmean(_):
                conv(CONV_PARTS * KT)
                dve.wait_ge(dve_chain, chain.n)
                for name, (a, b) in (("mua", HALVES[0]), ("mub", HALVES[1])):
                    o = take(dve, name)
                    if name == "mua":
                        wait_taken(dve, ("n", NH - 1))
                        dve.wait_ge(small_done, ring_of[("n", NH - 1)] + 1)
                    ts(lnt[:, 0, a:b], o[:, 0:b - a], 1.0 / D, None, ALU.mult).then_inc(out_sem(name), 1)
                wait_taken(dve, "mua")
                wait_taken(dve, "mub")
                for j in range(KT):
                    tt(upad[:, j, CH:CH + T], upad[:, j, CH:CH + T], lnt[:, 0, :], ALU.subtract).then_inc(xc_ready, 1)

            def convapply(part):
                if part == 0:
                    wait_taken(dve, "vara")
                    wait_taken(dve, "varb")
                    dve.reciprocal(lnt[:, 1, :], lnt[:, 1, :]).then_inc(lnstd, 1)
                    dve.wait_ge(lnstd, 1)
                    dve.wait_ge(xc_ready, KT)
                    dve.wait_ge(usq_added, KT - 1)

                for j in APPLY[part]:
                    if j >= 4:
                        dve.wait_ge(zs, j - 3)
                    tt(lnt[:, 2 + j % 4, :], upad[:, j, CH:CH + T], lnt[:, 1, :], ALU.mult).then_inc(yln, 1)

            def split(_):
                for k in range(KT):
                    dve.wait_ge(hhi_ready, k + 1)
                    tt(hlo[:, k, :], hab[:, k, :], hhi[:, k, :].bitcast(F32), ALU.subtract).then_inc(hlo_ready, 1)
                for j in range(KT):
                    dve.wait_ge(uhi_ready, j + 1)
                    tt(ulo[:, j, CH:CH + T], upad[:, j, CH:CH + T], uhi[:, j, :].bitcast(F32), ALU.subtract).then_inc(ulo_ready, 1)

            def residual(part):
                if part == 0:
                    o = take(dve, "xrs")
                    ts(xrs[:, :], o[:, 0:KT * TS], 1.0, None, ALU.mult).then_inc(out_sem("xrs"), 1)
                    wait_taken(dve, "xrs")
                for k in RESIDUAL[part]:
                    o = take(dve, ("xr", k))
                    wait_acc_out(dve, index_of[("out", k // 2)], k % 2)
                    link(tt(x1[:, k, TP:T], x1[:, k, TP:T], xrs[:, TS * k:TS * k + TS], ALU.add))
                    tt(x1[:, k, 0:TP], x1[:, k, 0:TP], o, ALU.add).then_inc(out_sem(("xr", k)), 1)
                    if k:
                        low_part(k - 1)
                if part == 2:
                    low_part(KT - 1)
                    split_lo(index_of[("out", 3)] + 2)

            def low_part(k):
                dve.wait_ge(hfhi, k + 1)
                wait_taken(dve, ("xr", k))
                stt(flo[:, k, :], x1[:, k, :], vec[:, FG + k:FG + k + 1], fhi[:, k, :].bitcast(F32),
                    ALU.mult, ALU.subtract).then_inc(hflo, 1)

            def norm2(_):
                wait_taken(dve, "qa")
                wait_taken(dve, "qb")
                dve.reciprocal(mb[:, 0:T], mb[:, 0:T]).then_inc(std2, 1)
                dve.wait_ge(std2, 1)

            def panel(kind, i):
                n = index_of[(kind, i)]
                if (kind, i) == ("glu", 1):
                    wait_taken(dve, ("cst", 1, 1))
                    wait_taken(dve, ("cst", 1, 0))
                    wait_taken(dve, "cw")
                conv(BEFORE.get(kind, 0))
                if kind == "if":
                    logits()
                if kind == "glu":
                    if i == 0:
                        dve.wait_ge(consts_set, 2)
                    p, s, done = acc_ready(dve, n, 1)
                    wait_acc_out(dve, n, 0)
                    new = upad[:, i, CH + TP:UPW].rearrange("p (b s) -> p b s", s=SEG)[:, :, CH:SEG]
                    chain.raised_by(tt(new, s.rearrange("p (b t) -> p b t", t=NS), sigmoids(i)[:, TP:T].rearrange("p (b t) -> p b t", t=NS), ALU.mult))
                    tt(upad[:, i, CH:CH + TP].rearrange("p (a t) -> p a t", a=2), p, sigmoids(i)[:, 0:TP].rearrange("p (a t) -> p a t", a=2), ALU.mult).then_inc(done, 1)
                    wait_acc_out(dve, n, 1)
                    dve.wait_ge(dve_chain, chain.n)
                    if i >= 2:
                        dve.wait_ge(small_done, ring_of[("ut", i - 2)] + 1)
                    dve.tensor_copy(unew[:, i % 2, :].rearrange("p (b t) -> p b t", t=NS), new).then_inc(unew_ready, 1)
                    conv_input[0] = i + 1
                elif kind == "branch":
                    if i == 0:
                        dve.wait_ge(ysig, KT)
                        dve.wait_ge(zs, KT)
                    for c in range(2):
                        p, s, done = acc_ready(dve, n, c)
                        wait_acc_out(dve, index_of[("gate", i)], c)
                        g = sga[:, i % 2, c, :]
                        chain.raised_by(tt(g[:, TP:T], s, g[:, TP:T], ALU.mult))
                        tt(g[:, 0:TP].rearrange("p (a t) -> p a t", a=2), p, g[:, 0:TP].rearrange("p (a t) -> p a t", a=2), ALU.mult).then_inc(done, 1)
                    wait_acc_out(dve, n, 0)
                    wait_acc_out(dve, n, 1)
                    dve.wait_ge(dve_chain, chain.n)
                    tt(mix[:, i, :], sga[:, i % 2, 0, :], sga[:, i % 2, 1, :], ALU.add).then_inc(mix_ready, 1)
                    if i >= KT - 2:
                        wait_panel_used(dve, index_of[("gate", KT - 1)])
                        for k in range(KT - 2) if i == KT - 2 else range(KT - 2, KT):
                            dve.wait_ge(mix_ready, k + 1)
                            dve.wait_ge(mhi_ready, k + 1)
                            tt(alo[:, k, :], mix[:, k, :], ahi[:, k, :].bitcast(F32), ALU.subtract).then_inc(mlo_ready, 1)
                elif kind == "o" and i < NH - 1:
                    if i == 0:
                        wait_taken(dve, ("hTs", NH - 2))
                    for c in range(2):
                        wait_acc_out(dve, n, c)
                        wait_acc_out(dve, n, 0)
                        k = 2 * i + c
                        t = tt(hab[:, k, :], hab[:, k, :], sga[:, i % 2, c, :], ALU.mult)
                        if c == 0:
                            chain.raised_by(t)
                    t.then_inc(hab_gated, 1)
                elif kind == "down":
                    def add(c):
                        k = 2 * i[0] + c
                        p, s, done = acc_ready(dve, n, c)
                        chain.raised_by(tt(x1[:, k, TP:T], s, x1[:, k, TP:T], ALU.add))
                        tt(x1[:, k, 0:TP].rearrange("p (a t) -> p a t", a=2), p, x1[:, k, 0:TP].rearrange("p (a t) -> p a t", a=2), ALU.add).then_inc(done, 1)

                    if i[1] == 2:
                        add(0)
                    if n + 1 < len(panels):
                        split_acts(n + 1)
                    if i[1] == 2:
                        add(1)
                elif kind == "up":
                    wait_taken(dve, ("fs", i))
                    if i:
                        dve.wait_ge(flast_ready, i)
                    else:
                        dve.wait_ge(consts_set, 4)
                        wait_taken(dve, ("vec", 1))
                        wait_taken(dve, ("vec", 2))
                    for c in range(2):
                        k = KF * c + i
                        if c == 1 and i == KF - 1:
                            split_acts(n + 1, range(PRE))
                        p, s, done = acc_ready(dve, n, c)
                        dst = up[:, c, FK - 1 + TP:FK - 1 + TP + NB * FSEG].rearrange("p (b s) -> p b s", s=FSEG)[:, :, 2:FSEG]
                        chain.raised_by(tt(dst, s.rearrange("p (b s) -> p b s", s=NS), mb[:, TP:T].rearrange("p (b s) -> p b s", s=NS), ALU.mult))
                        tt(up[:, c, FK - 1:FK - 1 + TP].rearrange("p (a t) -> p a t", a=2), p, mb[:, 0:TP].rearrange("p (a t) -> p a t", a=2), ALU.mult).then_inc(done, 1)
                        wait_acc_out(dve, n, c)
                        if c == 1 and i == KF - 1:
                            split_acts(n + 1, range(PRE, KT))
                        link(ts(upc[:, c, :], up[:, c, 0:FOUT], fcw[:, 0, k:k + 1], vec[:, FB + k:FB + k + 1], ALU.mult, ALU.add))
                        link(stt(upc[:, c, :], up[:, c, 1:1 + FOUT], fcw[:, 1, k:k + 1], upc[:, c, :], ALU.mult, ALU.add))
                        t = stt(upc[:, c, :], up[:, c, 2:2 + FOUT], fcw[:, 2, k:k + 1], upc[:, c, :], ALU.mult, ALU.add)
                        if c == 0:
                            t.then_inc(sig_ready, 1)
                        else:
                            link(t)
                    dve.wait_ge(sig_ready, 2 * i + 2)
                    link(tt(usig[:, :], usig[:, :], upc[:, 0, :], ALU.mult))
                    dst = act_tile(i)
                    tt(dst[:, 0:TP], usig[:, 0:TP], upc[:, 1, 0:TP], ALU.mult).then_inc(act_ready, 1)

                    def cut(x):
                        return x[:, TP:TP + NB * FSEG].rearrange("p (b s) -> p b s", s=FSEG)[:, :, 2:FSEG]
                    tt(dst[:, TP:T].rearrange("p (b t) -> p b t", t=NS), cut(usig), cut(upc[:, 1, :]), ALU.mult).then_inc(act_ready, 1)
                    dve.wait_ge(act_ready, 2 * i + 2)
                if n + 2 < len(panels) and not on_pool(n + 2) and (kind, i) != ("out", 3):
                    split_lo(n + 2)
                if (kind, i) != ("glu", 0):
                    conv(BEHIND.get(kind, 0))

            def split_acts(n, ks=None):
                g, q = panels[n][1]
                for k in ks or range(ktiles(n)):
                    kt = KT * q + k
                    u = KF * g + kt
                    wait_split_free(dve, u)
                    dve.wait_ge(dhi_ready, u + 1)
                    hi, lo = split_act(u)
                    tt(lo, act_tile(kt), hi.bitcast(F32), ALU.subtract).then_inc(dlo_ready, 1)

            def final(_):
                dve.wait_ge(fg_in, 16)
                total(0)
                for i in range(NI + 1):
                    n = P if i < NI else TS
                    if i < NI:
                        total(i + 1)
                    dve.wait_ge(yroot, i + 1)
                    dve.reciprocal(stat[0:n, 8 + i:9 + i], stat[0:n, 8 + i:9 + i]).then_inc(yrs, 1)
                    dve.wait_ge(yrs, i + 1)
                    o = small_at(("y", i, 1))
                    stt(yt[0:n, i, 512:1024], o[0:n, :], stat[0:n, 8 + i:9 + i], fgb[0:n, 512:1024], ALU.mult, ALU.mult).then_inc(out_sem(("y", i, 1)), 1)

            def total(i):
                n = P if i < NI else TS
                dve.wait_ge(yssq1, i + 1)
                wait_taken(dve, ("y", i, 0))
                tt(stat[0:n, 8 + i:9 + i], stat[0:n, 16 + 2 * i:17 + 2 * i], stat[0:n, 17 + 2 * i:18 + 2 * i], ALU.add).then_inc(ysum, 1)

            for now[0], s in enumerate(steps):
                {"setup": setup,
                 "gates": gates_step,
                 "gateturn": skip,
                 "tail": skip,
                 "kv": kv,
                 "weights": weights,
                 "scores": scores,
                 "av": av,
                 "state": state,
                 "headnorm": headnorm,
                 "headout": headout,
                 "convmean": convmean,
                 "convvar": skip,
                 "convapply": convapply,
                 "split": split,
                 "residual": residual,
                 "norm2": norm2,
                 "fstate": skip,
                 "ftail": skip,
                 "turnout": skip,
                 "constants": skip,
                 "final": final,
                 "panel": panel}[s[0]](*s[1:])

        @block.gpsimd
        def _(pool):
            chain = Count(pool_chain)

            def link(ins):
                chain.raised_by(ins)
                pool.wait_ge(pool_chain, chain.n)

            def setup(_):
                pool.memset(raw[:, 0, 0:KT * P], 0.0).then_inc(raw_zeroed, 1)
                link(pool.memset(ident[:, :], 0.0))
                link(pool.affine_select(out=ident[:, :], in_=ident[:, :], compare_op=ALU.not_equal, fill=1.0,
                                        base=0, pattern=[[-1, P]], channel_multiplier=1))
                link(pool.memset(epsc[:, 0:1], EPS))
                link(pool.memset(epsc[:, 1:2], -0.5))
                link(pool.memset(stat[:, :], 1.0))
                pool.memset(ones[:, :], 1.0).then_inc(consts_set, 1)
                pool.wait_ge(consts_set, 1)
                pool.dma_start(stat[0:4, 38:39], b_if[0, 0:NH].rearrange("(a b) -> a b", b=1)).then_inc(consts_in["bias_i"], 16)
                pool.dma_start(stat[32:36, 38:39], b_if[0, NH:2 * NH].rearrange("(a b) -> a b", b=1)).then_inc(consts_in["bias_f"], 16)
                pool.wait_ge(ssq_ready, 1)
                pool.wait_ge(ssq_dve, 1)
                link(pool.tensor_scalar(stat[:, 8:13], stat[:, 0:5], 1.0 / D, EPS, ALU.mult, ALU.add))
                pool.tensor_tensor(stat[:, 8:13], stat[:, 8:13], epsc[:, 1:2].broadcast_to([P, 5]), ALU.pow).then_inc(rs_ready, 1)
                pool.dma_start(stat[0:4, 22:30], state_m[0].rearrange("b h -> h b"), allow_slow_non_contiguous=True).then_inc(consts_in["m"], 16)
                link(pool.memset(sel[:, :, :], 0.0))
                link(pool.affine_select(out=sel[:, :, :], in_=sel[:, :, :], compare_op=ALU.not_equal, fill=1.0,
                                        base=0, pattern=[[-1, NH], [0, P]], channel_multiplier=1))
                link(pool.memset(bmask[:, :], 1.0))
                link(pool.affine_select(out=bmask[:, :], in_=bmask[:, :], compare_op=ALU.is_ge, fill=0.0,
                                        base=0, pattern=[[-NS, NB]], channel_multiplier=1))
                link(pool.affine_select(out=bmask[:, :], in_=bmask[:, :], compare_op=ALU.is_ge, fill=0.0,
                                        base=NS - 1, pattern=[[NS, NB]], channel_multiplier=-1))
                link(pool.memset(rows[:, :], 0.0))
                link(pool.memset(rt[:, NI, :], 0.0))
                link(pool.memset(gates[0:4, 3, :], 1.0))
                pool.memset(upad[:, :, 0:CH], 0.0).then_inc(consts_set, 1)
                pool.wait_ge(consts_set, 2)

            def kv(h):
                if h == 0:
                    wait_taken(pool, "xTs")
                    wait_taken(pool, ("cst", 1, 1))
                    wait_taken(pool, ("cst", 1, 0))
                    pool.wait_ge(gates_dve, 2)
                    pool.wait_ge(rows_ready, 1)
                    wait_taken(pool, "rts")
                    link(pool.memset(vk[:, :, DH:DH + 1], 1.0))
                    link(pool.memset(vks[:, :, DH:DH + 1], 1.0))
                    pool.memset(qm[:, :, :], 0.0).then_inc(consts_set, 1)
                for q in range(2):
                    wait_taken(pool, ("kt", h, q))
                link(pool.tensor_tensor(gsum[:, :], gk[:, 0, :], gk[:, 1, :], ALU.add))
                link(pool.tensor_tensor(gsum[:, :], gsum[:, :], gk[:, 2, :], ALU.add))
                pool.tensor_tensor(gsum[:, :], gsum[:, :], gk[:, 3, :], ALU.add).then_inc(gsum_ready, 1)

            def scores(h):
                for j in range(NI):
                    wait_taken(pool, ("s", h, j))
                    blk = sT[:, j, P * j:P * j + P]
                    pool.affine_select(out=blk, in_=blk, compare_op=ALU.is_ge, fill=0.0, base=0,
                                       pattern=[[1, P]], channel_multiplier=-1).then_inc(st_masked, 1)
                wait_taken(pool, ("ss", h))
                v = sTs[:, :].rearrange("p (b t) -> p b t", t=NS)
                pool.affine_select(out=v, in_=v, compare_op=ALU.is_ge, fill=0.0, base=0,
                                   pattern=[[NS, NB], [1, NS]], channel_multiplier=-1).then_inc(st_masked, 1)
                pool.wait_ge(st_masked, (NI + 2) * h + NI + 1)
                pool.affine_select(out=v, in_=v, compare_op=ALU.is_ge, fill=0.0, base=0,
                                   pattern=[[-NS, NB], [0, NS]], channel_multiplier=1).then_inc(st_masked, 1)

            def add_conv(j):
                if j == 0:
                    return
                pool.wait_ge(uc_ready, j + 1)
                if j > 1:
                    pool.wait_ge(u_added, j - 1)
                other = upad[:, 0, CH:CH + T] if j == 1 else usum[:, :]
                pool.tensor_tensor(usum[:, :], other, upad[:, j, CH:CH + T], ALU.add).then_inc(u_added, 1)

            def convmean(_):
                pool.wait_ge(small_done, ring_of["mub"] + 1)
                for j in range(1, KT):
                    pool.wait_ge(sqc_ready, j + 1)
                    if j > 1:
                        pool.wait_ge(usq_added, j - 1)
                    other = lnt[:, 2, :] if j == 1 else usum[:, :]
                    pool.tensor_tensor(usum[:, :], other, lnt[:, 2 + j % 4, :], ALU.add).then_inc(usq_added, 1)

            def headnorm(h):
                pool.wait_ge(hv_ready, h + 1)
                pool.tensor_tensor(stat[:, 5:10], stat[:, 5:10], epsc[:, 1:2].broadcast_to([P, 5]), ALU.pow).then_inc(hr_ready, 1)
                if h == NH - 1:
                    silu(1)

            def panel(kind, i):
                n = index_of[(kind, i)] + 2
                if n < len(panels) and on_pool(n):
                    pool.wait_ge(w_hi, n + 1)
                    pool.tensor_tensor(panel_view(wlo, n % 2, n), panel_view(raw, n % NRAW, n),
                                       panel_view(whi, n % 2, n).bitcast(F32), ALU.subtract).then_inc(w_lo_pool, 1)

            def norm2(_):
                pool.wait_ge(mlo_ready, KT)
                link(pool.memset(up[:, :, 0:FK - 1], 0.0))
                pool.memset(up[:, :, FPW - 4:FPW], 0.0).then_inc(consts_set, 1)

            def convapply(part):
                if part == 0:
                    silu(0)

            def silu(part):
                for j in APPLY[part]:
                    pool.wait_ge(ysig, j + 1)
                    pool.tensor_tensor(upad[:, j, CH:CH + T], upad[:, j, CH:CH + T], lnt[:, 2 + j % 4, :], ALU.mult).then_inc(zs, 1)

            def residual(part):
                for j in RESIDUAL[part]:
                    if j == 0:
                        continue
                    pool.wait_ge(sq_ready, j + 1)
                    if j > 1:
                        pool.wait_ge(sqsum_ready, j - 1)
                    other = sq2[:, 0, :] if j == 1 else sqsum[:, :]
                    pool.tensor_tensor(sqsum[:, :], other, sq2[:, j % 4, :], ALU.add).then_inc(sqsum_ready, 1)

            def turnout(q):
                pool.wait_ge(fg_in, 16)
                for i in TURNOUT[q]:
                    n = P if i < NI else TS
                    pool.wait_ge(y0_copied, i + 1)
                    pool.tensor_tensor(yt[0:n, i, 0:512], yt[0:n, i, 0:512], fgb[0:n, 0:512], ALU.mult).then_inc(y0_gained, 1)

            for at_step, s in enumerate(steps):
                {"setup": setup,
                 "gates": skip,
                 "gateturn": skip,
                 "tail": skip,
                 "kv": kv,
                 "weights": skip,
                 "scores": scores,
                 "av": skip,
                 "state": skip,
                 "headnorm": headnorm,
                 "headout": skip,
                 "convmean": convmean,
                 "convvar": skip,
                 "convapply": convapply,
                 "split": skip,
                 "residual": residual,
                 "norm2": norm2,
                 "fstate": skip,
                 "ftail": skip,
                 "turnout": turnout,
                 "constants": skip,
                 "final": skip,
                 "panel": panel}[s[0]](*s[1:])
                for j in range(KT):
                    if conv_done_in[j] == at_step:
                        add_conv(j)


_INS = ['x_prompt', 'x_sample', 'state_C', 'state_n', 'state_m', 'state_conv', 'state_ffn', 'mix_norm_g',
        'w_in', 'b_if', 'head_norm_g', 'w_mlstm_out', 'conv_w', 'conv_b', 'conv_ln_g', 'conv_ln_b',
        'w_conv_out', 'w_out', 'ffn_norm_g', 'w_up', 'ffn_conv_w', 'ffn_conv_b', 'w_down', 'final_norm_g']
_OUTS = [(1, TP, D), (NB, NS, D), (1, 1, NH, DH, DH), (1, 1, NH, DH), (1, 1, NH), (1, 1, CH, D),
         (1, 1, FK - 1, 2 * DFF), (1, NB, NH, DH, DH), (1, NB, NH, DH), (1, NB, NH), (1, NB, CH, D),
         (1, NB, FK - 1, 2 * DFF)]


def kernel(**inputs):
    import numpy as _np
    import concourse.bacc as _bacc
    from concourse import mybir as _mybir
    from concourse.bass_utils import run_bass_kernel_spmd as _run

    nc = _bacc.Bacc("TRN2", target_bir_lowering=False, num_devices=1)
    arrays, args = {}, []
    for name in _INS:
        a = _np.ascontiguousarray(inputs[name])
        arrays[f"in_{name}"] = a
        args.append(nc.dram_tensor(f"in_{name}", a.shape, _mybir.dt.from_np(a.dtype), kind="ExternalInput").ap())
    for i, shape in enumerate(_OUTS):
        args.append(nc.dram_tensor(f"out_{i}", shape, _mybir.dt.float32, kind="ExternalOutput").ap())
    build(nc, *args)
    r = _run(nc, [arrays], core_ids=[0])
    return tuple(r.results[0][f"out_{i}"] for i in range(len(_OUTS)))
```
